# Optimizing a Trainium2 kernel written in Bass

```python
import math
import jax, jax.numpy as jnp
from jax import lax
import numpy as np

D_MODEL = 1024
BATCH = 1
SEQ = 1024
DEPTH = 2

CTX_LEN = 256
GRID_W = 64
N_MIXERS = 2
N_ATTN_LAYERS = (DEPTH + N_MIXERS - 1) // N_MIXERS
N_CMLP_LAYERS = DEPTH // N_MIXERS
DA_HEADS = 8
DA_QK_DIM = 64
DA_V_DIM = 2 * DA_QK_DIM
Q_BLOCK = 128
ROPE_BASE = 10000.0
ROPE_AXIS_DIM = DA_QK_DIM // 2
QKV_WIDTH = 2 * DA_HEADS * DA_QK_DIM * 2 + DA_HEADS * DA_V_DIM
CHUNK = 128
CM_WIDTH = D_MODEL
CM_GROUPS = 8
CM_GROUP_DIM = CM_WIDTH // CM_GROUPS
FFN_HIDDEN = ((math.ceil(8 * D_MODEL / 3) + 255) // 256) * 256
N_MOD = 6
EPS = 1e-6

kernel_name = 'hybrid_diffattn_chunkmlp_dit'

def rms_norm(x, g):
    xf = x.astype(jnp.float32)
    y = xf * lax.rsqrt(jnp.mean(xf * xf, axis=-1, keepdims=True) + EPS)
    return (y * g.astype(jnp.float32)).astype(x.dtype)

def layer_norm(x, g, b):
    xf = x.astype(jnp.float32)
    mu = jnp.mean(xf, axis=-1, keepdims=True)
    var = jnp.mean(jnp.square(xf - mu), axis=-1, keepdims=True)
    y = (xf - mu) * lax.rsqrt(var + EPS) * g.astype(jnp.float32) + b.astype(jnp.float32)
    return y.astype(x.dtype)

def modulate(h, shift, scale):
    return h * (1 + scale) + shift

def axial_angles(n_tokens):
    rows = n_tokens // GRID_W
    row = jnp.broadcast_to(jnp.arange(rows, dtype=jnp.float32)[:, None], (rows, GRID_W)).reshape(-1)
    col = jnp.broadcast_to(jnp.arange(GRID_W, dtype=jnp.float32)[None, :], (rows, GRID_W)).reshape(-1)
    inv_freq = ROPE_BASE ** (-jnp.arange(0, ROPE_AXIS_DIM, 2, dtype=jnp.float32) / ROPE_AXIS_DIM)
    return row[:, None] * inv_freq, col[:, None] * inv_freq

def rotate(x, ang):
    cos = jnp.cos(ang)[None, :, None, :].astype(x.dtype)
    sin = jnp.sin(ang)[None, :, None, :].astype(x.dtype)
    x1, x2 = jnp.split(x, 2, axis=-1)
    return jnp.concatenate([x1 * cos - x2 * sin, x2 * cos + x1 * sin], axis=-1)

def rope_2d(x, ang_row, ang_col):
    x_row, x_col = jnp.split(x, 2, axis=-1)
    return jnp.concatenate([rotate(x_row, ang_row), rotate(x_col, ang_col)], axis=-1)

def diff_attend(q, k, v, lam):
    b, sq, h2, dk = q.shape
    n_blk = sq // Q_BLOCK
    q_blocks = jnp.moveaxis(q.reshape(b, n_blk, Q_BLOCK, h2, dk), 1, 0)
    scale = dk ** -0.5

    def one_block(qb):
        s = jnp.einsum('bqhd,bkhd->bhqk', qb, k, preferred_element_type=jnp.float32) * scale
        p = jax.nn.softmax(s, axis=-1).reshape(b, h2 // 2, 2, Q_BLOCK, -1)
        w = (p[:, :, 0] - lam * p[:, :, 1]).astype(v.dtype)
        return jnp.einsum('bhqk,bkhe->bqhe', w, v)

    out = lax.map(one_block, q_blocks)
    return jnp.moveaxis(out, 0, 1).reshape(b, sq, h2 // 2, -1)

def diff_attention(hx, hc, j, layer_idx, ang_row, ang_col, ctx_live,
                   w_qkv, w_attn_out, lam_q1, lam_k1, lam_q2, lam_k2, g_subln):
    lam_init = 0.8 - 0.6 * math.exp(-0.3 * layer_idx)
    f32 = jnp.float32
    lam = (jnp.exp(jnp.sum(lam_q1[j].astype(f32) * lam_k1[j].astype(f32)))
           - jnp.exp(jnp.sum(lam_q2[j].astype(f32) * lam_k2[j].astype(f32))) + lam_init)
    qk_w = 2 * DA_HEADS * DA_QK_DIM

    def project(h):
        b, s, _ = h.shape
        q, k, v = jnp.split(h @ w_qkv[j], [qk_w, 2 * qk_w], axis=-1)
        return (q.reshape(b, s, 2 * DA_HEADS, DA_QK_DIM),
                k.reshape(b, s, 2 * DA_HEADS, DA_QK_DIM),
                v.reshape(b, s, DA_HEADS, DA_V_DIM))

    def finish(o):
        b, s = o.shape[:2]
        o = rms_norm(o, g_subln[j]) * (1 - lam_init)
        return o.reshape(b, s, DA_HEADS * DA_V_DIM) @ w_attn_out[j]

    qx, kx, vx = project(hx)
    qx = rope_2d(qx, ang_row, ang_col)
    kx = rope_2d(kx, ang_row, ang_col)
    qc, kc, vc = project(hc)
    k_all = jnp.concatenate([kc, kx], axis=1)
    v_all = jnp.concatenate([vc, vx], axis=1)
    yx = finish(diff_attend(qx, k_all, v_all, lam))
    yc = finish(diff_attend(qc, kc, vc, lam)) if ctx_live else None
    return yx, yc

def chunk_mlp(h, j, w_uv, b_uv, g_sgu, b_sgu, w_spatial, b_spatial, w_cmlp_out):
    b, s, _ = h.shape
    z = jax.nn.gelu(h @ w_uv[j] + b_uv[j], approximate=False)
    u, v = jnp.split(z, 2, axis=-1)
    v = layer_norm(v, g_sgu[j], b_sgu[j])
    v = v.reshape(b, s // CHUNK, CHUNK, CM_GROUPS, CM_GROUP_DIM)
    sv = (jnp.einsum('gpq,bnqge->bnpge', w_spatial[j], v)
          + b_spatial[j].T[None, None, :, :, None])
    return (u * sv.reshape(b, s, CM_WIDTH)) @ w_cmlp_out[j]

def swiglu(h, j, w_ffn_in, w_ffn_out):
    gate, up = jnp.split(h @ w_ffn_in[j], 2, axis=-1)
    return (jax.nn.silu(gate) * up) @ w_ffn_out[j]

def setup_inputs(seed: int = 0) -> dict:
    key = jax.random.key(seed)
    ks = jax.random.split(key, 26)
    nrm = jax.random.normal
    f32 = jnp.float32
    D, NA, NB, F = D_MODEL, N_ATTN_LAYERS, N_CMLP_LAYERS, FFN_HIDDEN
    return {
        'x': nrm(ks[0], (BATCH, SEQ, D), f32),
        'c': nrm(ks[1], (BATCH, D), f32),
        'ctx': nrm(ks[2], (BATCH, CTX_LEN, D), f32),
        'c_ctx': nrm(ks[3], (D,), f32),
        'w_ada': nrm(ks[4], (DEPTH, D, N_MOD * D), f32) * (0.5 * D ** -0.5),
        'b_ada': nrm(ks[5], (DEPTH, N_MOD * D), f32) * 0.01,
        'g_mix_pre': 1.0 + 0.05 * nrm(ks[6], (DEPTH, D), f32),
        'g_mix_post': 1.0 + 0.05 * nrm(ks[7], (DEPTH, D), f32),
        'g_ffn_pre': 1.0 + 0.05 * nrm(ks[8], (DEPTH, D), f32),
        'g_ffn_post': 1.0 + 0.05 * nrm(ks[9], (DEPTH, D), f32),
        'w_qkv': nrm(ks[10], (NA, D, QKV_WIDTH), f32) * D ** -0.5,
        'w_attn_out': nrm(ks[11], (NA, DA_HEADS * DA_V_DIM, D), f32) * (DA_HEADS * DA_V_DIM) ** -0.5,
        'lam_q1': 0.1 * nrm(ks[12], (NA, DA_QK_DIM), f32),
        'lam_k1': 0.1 * nrm(ks[13], (NA, DA_QK_DIM), f32),
        'lam_q2': 0.1 * nrm(ks[14], (NA, DA_QK_DIM), f32),
        'lam_k2': 0.1 * nrm(ks[15], (NA, DA_QK_DIM), f32),
        'g_subln': 1.0 + 0.05 * nrm(ks[16], (NA, DA_V_DIM), f32),
        'w_uv': nrm(ks[17], (NB, D, 2 * CM_WIDTH), f32) * D ** -0.5,
        'b_uv': 0.02 * nrm(ks[18], (NB, 2 * CM_WIDTH), f32),
        'g_sgu': 1.0 + 0.05 * nrm(ks[19], (NB, CM_WIDTH), f32),
        'b_sgu': 0.02 * nrm(ks[20], (NB, CM_WIDTH), f32),
        'w_spatial': nrm(ks[21], (NB, CM_GROUPS, CHUNK, CHUNK), f32) * (0.5 * CHUNK ** -0.5),
        'b_spatial': 1.0 + 0.1 * nrm(ks[22], (NB, CM_GROUPS, CHUNK), f32),
        'w_cmlp_out': nrm(ks[23], (NB, CM_WIDTH, D), f32) * CM_WIDTH ** -0.5,
        'w_ffn_in': nrm(ks[24], (DEPTH, D, 2 * F), f32) * D ** -0.5,
        'w_ffn_out': nrm(ks[25], (DEPTH, F, D), f32) * F ** -0.5,
    }

def reference(x, c, ctx, c_ctx, w_ada, b_ada, g_mix_pre, g_mix_post, g_ffn_pre, g_ffn_post,
              w_qkv, w_attn_out, lam_q1, lam_k1, lam_q2, lam_k2, g_subln,
              w_uv, b_uv, g_sgu, b_sgu, w_spatial, b_spatial, w_cmlp_out,
              w_ffn_in, w_ffn_out):
    ang_row, ang_col = axial_angles(x.shape[1])
    silu_c = jax.nn.silu(c)
    silu_cc = jax.nn.silu(c_ctx)
    last_attn = max(i for i in range(DEPTH) if i % N_MIXERS == 0)
    for i in range(DEPTH):
        is_attn = (i % N_MIXERS == 0)
        j = i // N_MIXERS
        ctx_live = i < last_attn
        mod_x = (silu_c @ w_ada[i] + b_ada[i])[:, None, :]
        mod_c = silu_cc @ w_ada[i] + b_ada[i]
        sh_m, sc_m, g_m, sh_f, sc_f, g_f = jnp.split(mod_x, N_MOD, axis=-1)
        csh_m, csc_m, cg_m, csh_f, csc_f, cg_f = jnp.split(mod_c, N_MOD, axis=-1)

        hx = modulate(rms_norm(x, g_mix_pre[i]), sh_m, sc_m)
        if is_attn:
            hc = modulate(rms_norm(ctx, g_mix_pre[i]), csh_m, csc_m)
            yx, yc = diff_attention(hx, hc, j, i, ang_row, ang_col, ctx_live,
                                    w_qkv, w_attn_out, lam_q1, lam_k1, lam_q2, lam_k2, g_subln)
        else:
            yx = chunk_mlp(hx, j, w_uv, b_uv, g_sgu, b_sgu, w_spatial, b_spatial, w_cmlp_out)
            if ctx_live:
                hc = modulate(rms_norm(ctx, g_mix_pre[i]), csh_m, csc_m)
                yc = chunk_mlp(hc, j, w_uv, b_uv, g_sgu, b_sgu, w_spatial, b_spatial, w_cmlp_out)
        x = x + g_m * rms_norm(yx, g_mix_post[i])
        fx = swiglu(modulate(rms_norm(x, g_ffn_pre[i]), sh_f, sc_f), i, w_ffn_in, w_ffn_out)
        x = x + g_f * rms_norm(fx, g_ffn_post[i])

        if ctx_live:
            ctx = ctx + cg_m * rms_norm(yc, g_mix_post[i])
            fc = swiglu(modulate(rms_norm(ctx, g_ffn_pre[i]), csh_f, csc_f), i, w_ffn_in, w_ffn_out)
            ctx = ctx + cg_f * rms_norm(fc, g_ffn_post[i])
    return x


_drawn_inputs = setup_inputs


def setup_inputs(seed=0):
    import zlib

    import numpy as np

    out = dict(_drawn_inputs(seed))
    spreads = {}
    factors = {'g_mix_pre': 3.172,
     'g_mix_post': 2.764,
     'g_ffn_post': 2.798,
     'lam_q1': 5.112,
     'lam_q2': 64.0,
     'lam_k2': 4.638,
     'g_subln': 3.326,
     'b_uv': 8.0,
     'g_sgu': 8.0,
     'b_sgu': 46.956,
     'b_spatial': 4.602}
    for name, (base, spread) in spreads.items():
        noise = np.random.default_rng([zlib.crc32(name.encode()), seed]).standard_normal(out[name].shape)
        drawn = base * np.exp(spread * noise) if base else spread * noise
        out[name] = __import__('jax').numpy.asarray(drawn.astype(out[name].dtype))
    for name, factor in factors.items():
        out[name] = (out[name] * factor).astype(out[name].dtype)
    return out
```

```python
import math
from contextlib import ExitStack

import numpy as np
import concourse.bass as bass
from concourse import mybir
from concourse.alu_op_type import AluOpType as ALU

ACT = mybir.ActivationFunctionType
AX = mybir.AxisListType
F32 = mybir.dt.float32
F32R = mybir.dt.float32r

P = 128
D = 1024
KT = D // P
T = 1024
C = 256
TA = T + C
HALF = T // 2
FH = 2816
HT = FH // P
DH = 64
NPAIR = 8
NADA = 2 * 6 * KT
EPS = 1e-6
LAM_INIT = 0.8 - 0.6 * math.exp(-0.3 * 0)
NRING = 4
GROUPS_KT = [(0, 8), (8, 16), (16, HT)]

V_BADA = 0
V_MIXPRE = V_BADA + NADA
V_MIXPOST = V_MIXPRE + 2 * KT
V_FFNPRE = V_MIXPOST + 2 * KT
V_FFNPOST = V_FFNPRE + 2 * KT
V_C = V_FFNPOST + 2 * KT
V_CCTX = V_C + KT
V_BU = V_CCTX + KT
V_SUBLN = V_BU + KT
NV = V_SUBLN + 1
SH_M, SC_M, G_M, SH_F, SC_F, G_F = range(6)


def wait(eng, sem, value):
    if isinstance(value, int) and value <= 0:
        return
    eng.wait_ge(sem, value)


def loop(eng, n, body):
    body(0)
    if n > 1:
        with eng.Fori(1, n) as i:
            body(i)


class Steps:

    def __init__(self, eng, sem):
        self.eng, self.sem, self.n, self.base = eng, sem, 0, 0

    def did(self, ins):
        ins.then_inc(self.sem, 1)
        self.n += 1

    def sync(self):
        self.eng.wait_ge(self.sem, self.base + self.n)

    def loop(self, n, per, body):
        start = self.n
        body(0)
        assert self.n - start == per, (self.n - start, per)
        if n > 1:
            with self.eng.Fori(1, n) as i:
                self.n, self.base = start, i * per
                body(i)
            self.base = 0
        self.n = start + n * per


def product(pe, out, n_kt, weight, x):
    for kt in range(n_kt):
        for a, b in ((0, 0), (0, 1), (1, 0)):
            last = pe.matmul(out, weight(a, kt), x(b, kt), start=weight.first and kt == 0 and a == b == 0,
                             stop=weight.last and kt == n_kt - 1 and a == 1)
    return last


class W:

    def __init__(self, at, first=True, last=True):
        self.at, self.first, self.last = at, first, last

    def __call__(self, a, kt):
        return self.at(a, kt)


def split_weights(pool, turn, steps, raw, ws, slot, n_kt, split_ready):
    pool.sem_inc(turn, 1)
    steps.did(pool.tensor_scalar(ws[:, slot, 0, 0:n_kt, :], raw[:, slot, 0:n_kt, :], 1.0, 1.0, ALU.mult, ALU.mult))
    steps.sync()
    pool.tensor_tensor(ws[:, slot, 1, 0:n_kt, :], raw[:, slot, 0:n_kt, :],
                       ws[:, slot, 0, 0:n_kt, :].bitcast(F32), ALU.subtract).then_inc(split_ready, 1)


def build(nc, a, out):
    with ExitStack() as keep:
        def sb(name, shape, dt=F32):
            return keep.enter_context(nc.sbuf_tensor(name, shape, dt))

        qT = nc.dram_tensor("q_scratch", [KT, P, 2, T], F32, kind="Internal").ap()
        kT = nc.dram_tensor("k_scratch", [KT, P, 2, TA], F32, kind="Internal").ap()
        vS = nc.dram_tensor("v_scratch", [TA // P, P, D], F32, kind="Internal").ap()
        oT = nc.dram_tensor("o_scratch", [NPAIR, P, 2, T], F32, kind="Internal").ap()
        xS = nc.dram_tensor("x_scratch", [KT, P, T], F32, kind="Internal").ap()
        c = {
            "vecs": sb("vecs", [P, NV]),
            "mod": sb("mod", [P, NADA]),
            "modc": sb("modc", [P, 2 * KT]),
            "A": sb("A", [P, 5, KT]),
            "G": sb("G", [P, 4, KT]),
            "neglam": sb("neglam", [P, 1]),
            "gsub": sb("gsub", [P, 1]),
            "ones": sb("ones", [P, P]),
            "eps": sb("eps", [P, 1]),
        }
        block1(nc, a, c, qT, kT, vS)
        block2(nc, a, c, qT, kT, vS, oT)
        block3(nc, a, c, oT, xS, out)


def block1(nc, a, c, qT, kT, vS):
    with ExitStack() as ctx:
        def sb(name, shape, dt=F32):
            return ctx.enter_context(nc.sbuf_tensor(name, shape, dt))

        def sem(name):
            return ctx.enter_context(nc.semaphore(name))

        h = sb("h_all", [P, 2, KT, TA], F32R)
        ws = sb("wsplit1", [P, NRING, 2, KT, P], F32R)
        raw = sb("wraw1", [P, NRING, KT, P])
        ada = sb("ada_raw", [P, NRING, KT, P])
        y = sb("x_in", [P, 2, KT, HALF])
        trig = sb("trig", [P, 2, T])
        sq = sb("sq1", [P, 2, HALF])
        t = sb("t1", [P, 2, HALF])
        acc = sb("acc1", [P, HALF])
        rstd = sb("rstd1", [P, HALF])
        st = sb("qk_out", [P, 2, 2, HALF], F32R)
        lamv = sb("lamv", [P, 4, DH])
        lams = sb("lams", [P, 4])
        sx = sb("silu_c", [P, KT, 2])
        bank = [ctx.enter_context(nc.psum_tensor(f"acc1_{b}", [P, HALF], F32)) for b in range(4)]
        pstat = ctx.enter_context(nc.psum_tensor("stat1", [P, HALF], F32))
        pada = [ctx.enter_context(nc.psum_tensor(f"ada_ps{b}", [P, HALF], F32)) for b in range(2)]

        vecs_in, lam_in, trig_in = sem("vecs_in"), sem("lam_in"), sem("trig_in")
        x_in = [sem(f"x_in{s}") for s in range(3)]
        raw_full = [sem(f"b1_raw_full{s}") for s in range(NRING)]
        ada_full = [sem(f"ada_full{s}") for s in range(NRING)]
        split_ready = sem("b1_split_ready")
        ada_used, mod_out = sem("ada_used"), sem("mod_out")
        silu_ready, const_ready, mods_ready = sem("silu_ready"), sem("const_ready"), sem("mods_ready")
        sq_ready, sq_used = sem("b1_sq_ready"), sem("b1_sq_used")
        stat_ready, std_ready, t_ready = sem("b1_stat_ready"), sem("b1_std_ready"), sem("b1_t_ready")
        hf_ready, h_ready = sem("b1_hf_ready"), sem("b1_h_ready")
        group_ready = sem("b1_group_ready")
        bank_free = [sem(f"b1_bank_free{b}") for b in range(4)]
        qk_done = sem("qk_done")
        st_out = [sem(f"st_out{s}") for s in range(2)]
        v_out = [sem(f"v_out{s}") for s in range(2)]
        dve_step, pool_step, turn = sem("b1_dve_step"), sem("b1_pool_step"), sem("b1_turn")
        lam_exp = sem("lam_exp")

        SEG = [(0, C, HALF), (1, C + HALF, HALF), (0, 0, C)]
        FIRST_ADA = 2 * KT
        ADA_PER = 5
        QKG = [[1, 2], [0, 1, 2]]
        G_K, G_V = 2 * KT, 2 * KT + 3 * KT
        VT = TA // P

        def cols(g):
            return (0, C) if g == 0 else (C + (g - 1) * HALF, C + g * HALF)

        block = ctx.enter_context(nc.Block())

        @block.sync
        def _(sp):
            def load_ada(n, s):
                wait(sp, ada_used, n - NRING + 1)
                sp.dma_start(ada[:, s], a["w_ada"][n].rearrange("p (k c) -> p k c", k=KT)).then_inc(ada_full[s], 16)

            def load_w(u, s):
                wait(sp, split_ready, u - NRING + 1)
                sp.dma_start(raw[:, s], a["w_qkv"][u].rearrange("p (k c) -> p k c", k=KT)).then_inc(raw_full[s], 16)

            sp.dma_start(c["vecs"][:], a["vecs"]).then_inc(vecs_in, 16)
            for n in range(2):
                load_ada(n, n)
            sp.dma_start(y[:, 0], a["xT"][:, :, 0:HALF].rearrange("k p t -> p k t")).then_inc(x_in[0], 16)
            for n in range(2, FIRST_ADA):
                load_ada(n, n % NRING)
            sp.dma_start(y[:, 1], a["xT"][:, :, HALF:T].rearrange("k p t -> p k t")).then_inc(x_in[1], 16)
            for u in range(NRING):
                load_w(u, u)
            sp.dma_start(trig[:], a["trig"]).then_inc(trig_in, 16)
            sp.dma_start(lamv[:], a["lamv"]).then_inc(lam_in, 16)
            sp.wait_ge(t_ready, KT)
            sp.dma_start(y[:, 0, :, 0:C], a["ctxT"].rearrange("k p t -> p k t")).then_inc(x_in[2], 16)
            with sp.Fori(0, 4) as i:
                for k in range(4):
                    for m in range(ADA_PER):
                        n = ADA_PER * k + m
                        load_ada(FIRST_ADA + 4 * ADA_PER * i + n, n % NRING)
                    load_w(4 * i + k + NRING, k)
            for u in range(16 + NRING, 24):
                load_w(u, u % NRING)

        @block.gpsimd
        def _(pool):
            steps = Steps(pool, pool_step)

            def groups_until(i, k):
                u = 4 * i + k
                if u < KT:
                    return len(QKG[0]) * (u + 1)
                if u < 2 * KT:
                    return G_K + len(QKG[1]) * (u + 1 - KT)
                return G_V + VT * (i - 3)

            for i in range(6):
                for k in range(4):
                    pool.wait_ge(raw_full[k], 16 * (i + 1))
                    if i:
                        pool.wait_ge(group_ready, groups_until(i - 1, k))
                    split_weights(pool, turn, steps, raw, ws, k, KT, split_ready)

        @block.tensor
        def _(pe):
            pe.wait_ge(silu_ready, 2)
            for n in range(FIRST_ADA):
                pe.wait_ge(ada_full[n % NRING], 16 * (n // NRING + 1))
                for kt in range(KT):
                    last = pe.matmul(pada[0][:, 2 * n:2 * n + 2], ada[:, n % NRING, kt], sx[:, kt],
                                     start=kt == 0, stop=kt == KT - 1)
                last.then_inc(ada_used, 1)
            pe.wait_ge(const_ready, 1)
            for s, (_, _, w) in enumerate(SEG):
                pe.wait_ge(sq_used, KT * (s + 1))
                wait(pe, std_ready, s)
                pe.matmul(pstat[:, 0:w], c["ones"][:], acc[:, 0:w], start=True, stop=True).then_inc(stat_ready, 1)

            def unit(i, k, kind, unit0, group0):
                u = unit0 + 4 * i + k
                groups = QKG[kind]
                ng = len(groups)
                wait(pe, split_ready, u + 1)
                for n, g in enumerate(groups):
                    at = ng * k + n
                    if kind == 0 and k == 0:
                        pe.wait_ge(h_ready, KT * g)
                    if kind == 1:
                        pe.wait_ge(h_ready, 3 * KT)
                    b = at % 4
                    wait(pe, bank_free[b], group0 // 4 + ng * i + at // 4)
                    lo, hi = cols(g)
                    last = product(pe, bank[b][:, 0:hi - lo], KT, W(lambda p, kt: ws[:, k, p, kt]),
                                   lambda p, kt: h[:, p, kt, lo:hi])
                    last.then_inc(group_ready, 1)
                for m in range(ADA_PER):
                    n = ADA_PER * k + m
                    wait(pe, ada_full[n % NRING], 16 * (FIRST_ADA // NRING + ADA_PER * (unit0 // 4 + i) + n // NRING + 1))
                    if m == 0:
                        wait(pe, mod_out, 4 if isinstance(u, int) and u == 0 else u + 3)
                    for kt in range(KT):
                        last = pe.matmul(pada[k % 2][:, n:n + 1], ada[:, n % NRING, kt], sx[:, kt, 0:1],
                                         start=kt == 0, stop=kt == KT - 1)
                    last.then_inc(ada_used, 1)

            for kind, unit0, group0 in ((0, 0, 0), (1, KT, G_K)):
                loop(pe, 2, lambda i: [unit(i, k, kind, unit0, group0) for k in range(4)])
            for half in range(2):
                pe.wait_ge(split_ready, 2 * KT + 4 * half + 4)
                for n in range(VT):
                    g = G_V + VT * half + n
                    pe.wait_ge(bank_free[g % 4], g // 4)
                    last = product(pe, bank[g % 4][:], KT, W(lambda p, kt: h[:, p, kt, n * P:(n + 1) * P]),
                                   lambda p, kt: ws[:, 0:4, p, kt])
                    last.then_inc(group_ready, 1)

        @block.scalar
        def _(act):
            act.wait_ge(vecs_in, 16)
            act.activation(sx[:, :, 0], c["vecs"][:, V_C:V_C + KT], ACT.Silu).then_inc(silu_ready, 1)
            act.activation(sx[:, :, 1], c["vecs"][:, V_CCTX:V_CCTX + KT], ACT.Silu).then_inc(silu_ready, 1)
            act.wait_ge(lam_in, 16)
            act.wait_ge(dve_step, 4)
            act.activation(lams[:, 2:4], lams[:, 0:2], ACT.Exp).then_inc(lam_exp, 1)
            act.wait_ge(ada_used, FIRST_ADA)
            both = pada[0][:, 0:2 * FIRST_ADA].rearrange("p (n s) -> p s n", s=2)
            for j in range(2):
                act.activation(c["mod"][:, j * KT:(j + 1) * KT], both[:, 0, j * KT:(j + 1) * KT],
                               ACT.Copy).then_inc(mod_out, 1)
                act.activation(c["modc"][:, j * KT:(j + 1) * KT], both[:, 1, j * KT:(j + 1) * KT],
                               ACT.Copy).then_inc(mod_out, 1)
            act.wait_ge(const_ready, 2)
            act.wait_ge(mods_ready, 1)
            for s, (slot, _, w) in enumerate(SEG):
                act.wait_ge(x_in[s], 16)
                for kt in range(KT):
                    wait(act, sq_used, KT * s + kt - 1)
                    act.activation(sq[:, kt % 2, 0:w], y[:, slot, kt, 0:w], ACT.Square).then_inc(sq_ready, 1)
                act.wait_ge(stat_ready, s + 1)
                wait(act, t_ready, KT * s)
                act.activation(rstd[:, 0:w], pstat[:, 0:w], ACT.Sqrt, bias=c["eps"][:]).then_inc(std_ready, 1)
                scale = c["A"][:, 4 if s == 2 else 0]
                shift = (c["modc"] if s == 2 else c["mod"])
                for kt in range(KT):
                    act.wait_ge(t_ready, KT * s + kt + 1)
                    act.activation(t[:, kt % 2, 0:w], t[:, kt % 2, 0:w], ACT.Identity,
                                   bias=shift[:, kt:kt + 1], scale=scale[:, kt:kt + 1]).then_inc(hf_ready, 1)

            act.wait_ge(h_ready, 3 * KT)

            def unit(i, k, kind, unit0, group0):
                groups = QKG[kind]
                ng = len(groups)
                for n, g in enumerate(groups):
                    at = ng * k + n
                    G = group0 + 4 * ng * i + at
                    lo, hi = cols(g)
                    wait(act, group_ready, G + 1)
                    wait(act, qk_done, G)
                    act.activation(t[:, 0, 0:hi - lo], bank[at % 4][:, 0:hi - lo], ACT.Copy,
                                   scale=DH ** -0.5 if kind == 0 else 1.0).then_inc(bank_free[at % 4], 1)
                    wait(act, qk_done, G + 1)
                    if kind == 0:
                        dst = qT[4 * i + k][:, :, lo - C:hi - C]
                    else:
                        dst = kT[4 * i + k][:, :, lo:hi]
                    act.dma_start(dst, st[:, at % 2, :, 0:hi - lo].bitcast(F32)).then_inc(st_out[at % 2], 16)
                wait(act, ada_used, FIRST_ADA + ADA_PER * (unit0 + 4 * i + k + 1))
                at = FIRST_ADA + ADA_PER * (unit0 + 4 * i + k)
                act.activation(c["mod"][:, bass.ds(at, ADA_PER)], pada[k % 2][:, ADA_PER * k:ADA_PER * (k + 1)],
                               ACT.Copy).then_inc(mod_out, 1)

            for kind, unit0, group0 in ((0, 0, 0), (1, KT, G_K)):
                loop(act, 2, lambda i: [unit(i, k, kind, unit0, group0) for k in range(4)])
            act.wait_ge(qk_done, G_V)
            for half in range(2):
                for n in range(VT):
                    m = VT * half + n
                    g = G_V + m
                    act.wait_ge(group_ready, g + 1)
                    wait(act, v_out[m % 2], 16 * (m // 2))
                    act.activation(t[:, m % 2], bank[g % 4][:], ACT.Copy).then_inc(bank_free[g % 4], 1)
                    act.wait_ge(bank_free[g % 4], g // 4 + 1)
                    act.dma_start(vS[n][:, half * HALF:(half + 1) * HALF], t[:, m % 2]).then_inc(v_out[m % 2], 16)
            for s in range(2):
                act.wait_ge(st_out[s], 16 * (2 * KT + 3 * KT) // 2)
                act.wait_ge(v_out[s], 16 * VT)

        @block.vector
        def _(dve):
            steps = Steps(dve, dve_step)
            vec = c["vecs"]
            swap = [(p + 16) % 32 for p in range(32)]
            dve.wait_ge(lam_in, 16)
            for j in range(2):
                steps.did(dve.tensor_tensor(lamv[:, 2 * j], lamv[:, 2 * j], lamv[:, 2 * j + 1], ALU.mult))
                steps.sync()
                steps.did(dve.tensor_reduce(lams[:, j:j + 1], lamv[:, 2 * j], AX.X, ALU.add))
            dve.memset(c["ones"][:], 1.0 / D).then_inc(const_ready, 1)
            dve.memset(c["eps"][:], EPS).then_inc(const_ready, 1)
            dve.wait_ge(lam_exp, 1)
            steps.did(dve.tensor_tensor(lams[:, 0:1], lams[:, 3:4], lams[:, 2:3], ALU.subtract))
            steps.sync()
            steps.did(dve.tensor_scalar(c["neglam"][:], lams[:, 0:1], -LAM_INIT, None, ALU.add))
            steps.did(dve.tensor_scalar(c["gsub"][:], vec[:, V_SUBLN:V_SUBLN + 1], 1.0 - LAM_INIT, None, ALU.mult))

            dve.wait_ge(mod_out, 4)
            steps.did(dve.tensor_tensor(c["mod"][:, 0:FIRST_ADA], c["mod"][:, 0:FIRST_ADA],
                                        vec[:, V_BADA:V_BADA + FIRST_ADA], ALU.add))
            steps.did(dve.tensor_tensor(c["modc"][:], c["modc"][:], vec[:, V_BADA:V_BADA + FIRST_ADA], ALU.add))
            steps.sync()
            steps.did(dve.scalar_tensor_tensor(out=c["A"][:, 0], in0=c["mod"][:, KT:2 * KT], scalar=1.0,
                                               in1=vec[:, V_MIXPRE:V_MIXPRE + KT], op0=ALU.add, op1=ALU.mult))
            dve.scalar_tensor_tensor(out=c["A"][:, 4], in0=c["modc"][:, KT:2 * KT], scalar=1.0,
                                     in1=vec[:, V_MIXPRE:V_MIXPRE + KT], op0=ALU.add,
                                     op1=ALU.mult).then_inc(mods_ready, 1)

            for s, (slot, col0, w) in enumerate(SEG):
                steps.did(dve.memset(acc[:, 0:w], 0.0))
                for kt in range(KT):
                    dve.wait_ge(sq_ready, KT * s + kt + 1)
                    wait(dve, sq_used, KT * s + kt)
                    if kt == 0:
                        steps.sync()
                    dve.tensor_tensor(acc[:, 0:w], acc[:, 0:w], sq[:, kt % 2, 0:w], ALU.add).then_inc(sq_used, 1)
                dve.wait_ge(std_ready, s + 1)
                steps.did(dve.reciprocal(rstd[:, 0:w], rstd[:, 0:w]))
                steps.sync()

                def scaled(kt):
                    wait(dve, h_ready, KT * s + kt - 1)
                    dve.tensor_tensor(t[:, kt % 2, 0:w], y[:, slot, kt, 0:w], rstd[:, 0:w],
                                      ALU.mult).then_inc(t_ready, 1)
                scaled(0)
                for kt in range(KT):
                    if kt + 1 < KT:
                        scaled(kt + 1)
                    dve.wait_ge(hf_ready, KT * s + kt + 1)
                    hi = h[:, 0, kt, col0:col0 + w]
                    steps.did(dve.tensor_copy(hi, t[:, kt % 2, 0:w]))
                    steps.sync()
                    dve.tensor_tensor(h[:, 1, kt, col0:col0 + w], t[:, kt % 2, 0:w], hi.bitcast(F32),
                                      ALU.subtract).then_inc(h_ready, 1)
            dve.wait_ge(h_ready, 3 * KT)
            dve.wait_ge(trig_in, 16)

            def unit(i, k, kind, unit0, group0):
                groups = QKG[kind]
                ng = len(groups)
                per_slot = ng * 4 // 2
                for n, g in enumerate(groups):
                    at = ng * k + n
                    lo, hi = cols(g)
                    w = hi - lo
                    s = st[:, at % 2]
                    used = group0 // 2 + per_slot * i + at // 2
                    wait(dve, bank_free[at % 4], group0 // 4 + ng * i + at // 4 + 1)
                    src = t[:, 0, 0:w]
                    if g > 0:
                        cos, sin = (trig[:, m, lo - C:hi - C] for m in range(2))
                        wait(dve, qk_done, group0 + 4 * ng * i + at)
                        steps.did(dve.stream_shuffle(t[:, 1, 0:w], src, swap))
                        steps.did(dve.tensor_tensor(acc[:, 0:w], src, cos, ALU.mult))
                        steps.sync()
                        steps.did(dve.tensor_tensor(t[:, 1, 0:w], t[:, 1, 0:w], sin, ALU.mult))
                        steps.sync()
                        steps.did(dve.tensor_tensor(acc[:, 0:w], acc[:, 0:w], t[:, 1, 0:w], ALU.add))
                        steps.sync()
                        src = acc[:, 0:w]
                    wait(dve, st_out[at % 2], 16 * used)
                    steps.did(dve.tensor_copy(s[:, 0, 0:w], src))
                    steps.sync()
                    dve.tensor_tensor(s[:, 1, 0:w], src, s[:, 0, 0:w].bitcast(F32),
                                      ALU.subtract).then_inc(qk_done, 1)

            for kind, unit0, group0 in ((0, 0, 0), (1, KT, G_K)):
                per = 4 * (10 if kind == 0 else 11)
                steps.loop(2, per, lambda i: [unit(i, k, kind, unit0, group0) for k in range(4)])

            dve.wait_ge(mod_out, 4 + 2 * KT)
            steps.did(dve.tensor_tensor(c["mod"][:, FIRST_ADA:NADA], c["mod"][:, FIRST_ADA:NADA],
                                        vec[:, V_BADA + FIRST_ADA:V_BADA + NADA], ALU.add))
            steps.sync()
            for n in range(4):
                layer, ffn = divmod(n, 2)
                m0 = layer * 6 * KT
                sc, gate = (SC_F, G_F) if ffn else (SC_M, G_M)
                pre = (V_FFNPRE if ffn else V_MIXPRE) + layer * KT
                post = (V_FFNPOST if ffn else V_MIXPOST) + layer * KT
                if n:
                    steps.did(dve.scalar_tensor_tensor(
                        out=c["A"][:, n], in0=c["mod"][:, m0 + sc * KT:m0 + (sc + 1) * KT], scalar=1.0,
                        in1=vec[:, pre:pre + KT], op0=ALU.add, op1=ALU.mult))
                steps.did(dve.tensor_tensor(c["G"][:, n], c["mod"][:, m0 + gate * KT:m0 + (gate + 1) * KT],
                                            vec[:, post:post + KT], ALU.mult))


def block2(nc, a, c, qT, kT, vS, oT):
    with ExitStack() as ctx:
        def sb(name, shape, dt=F32):
            return ctx.enter_context(nc.sbuf_tensor(name, shape, dt))

        def sem(name):
            return ctx.enter_context(nc.semaphore(name))

        QT = T // P
        NT = NPAIR * QT
        BODY = 2 * QT
        KEYS = TA // P
        LAST = NT // BODY - 1

        q = sb("q_stack", [P, 2, 2, T], F32R)
        kd = sb("k_double", [P, 2, 2, 2, TA], F32R)
        v = sb("v_pair", [P, 2, KEYS, P])
        prob = sb("prob", [P, 2, 2, TA])
        w = sb("w_diff", [P, 2, TA])
        wT = sb("w_diffT", [P, 2, KEYS, P])
        negmax = sb("negmax", [P, 2, 2])
        sums = sb("sums", [P, 2, 2])
        rsum = sb("rsum", [P, 2, 2])
        junk = sb("junk", [P, P])
        ss = sb("ss", [P, 2])
        ms = sb("ms", [P, 2])
        half = sb("minus_half", [P, 1])
        rstd = sb("rstd2", [P, 2])
        on = sb("o_norm", [P, 2, P])
        osb = sb("o_copy", [P, 4, P])
        of = sb("o_full", [P, 2, 2 * P])
        ost = sb("o_out", [P, 2, 2, 2 * P], F32R)
        ident = sb("ident", [P, P])

        s_ps = [ctx.enter_context(nc.psum_tensor(f"scores{e}", [P, 3 * 512], F32)) for e in range(2)]
        t_ps = ctx.enter_context(nc.psum_tensor("transposed", [P, 512], F32))
        o_ps = ctx.enter_context(nc.psum_tensor("o_ps", [P, 512], F32))

        ident_in, half_set = sem("ident_in"), sem("half_set")
        pair_in = [sem(f"pair_in{s}") for s in range(2)]
        s_ready, max_ready, exp_done = sem("s_ready"), sem("max_ready"), sem("exp_done")
        rsum_ready, p1_scaled, w_ready = sem("rsum_ready"), sem("p1_scaled"), sem("w_ready")
        t_ready, wT_ready, o_ready = sem("t_ready"), sem("wT_ready"), sem("o_ready")
        o_copied = sem("o_copied")
        ss_ready, rstd_ready, on_ready = sem("ss_ready"), sem("rstd_ready"), sem("on_ready")
        oT_ready, of_ready, ost_ready = sem("oT_ready"), sem("of_ready"), sem("ost_ready")
        o_out = [sem(f"o_out{s}") for s in range(2)]
        pool_step, dve_step, turn = sem("b2_pool_step"), sem("b2_dve_step"), sem("b2_turn")

        BANK = 512
        CUTS = [0, BANK, 2 * BANK, TA]
        CHUNKS = [(0, 4), (4, 8), (8, KEYS)]

        class Tile:

            def __init__(self, i, at, first=False, last=False):
                self.exists = not (first and at < 0) and not (last and at >= BODY)
                self.n = BODY * i + at
                self.s = at % 2
                self.q = at % QT
                self.pair = BODY // QT * i + at // QT
                self.buf = at // QT % 2
                self.fill = i + at // BODY
                self.duo = BODY // 2 * i + at // 2
                self.duo_slot = at // 2 % 2
                self.duo_fill = BODY // 4 * i + at // 4
                self.s4 = at % 4

        def steps_of(eng, step):
            for at in range(-2, BODY):
                step(lambda k: Tile(0, at + k, first=True))
            with eng.Fori(1, LAST) as i:
                for at in range(BODY):
                    step(lambda k: Tile(i, at + k))
            for at in range(BODY + 5):
                step(lambda k: Tile(LAST, at + k, last=True))

        block = ctx.enter_context(nc.Block())

        @block.sync
        def _(sp):
            def load_pair(p, s):
                for e in range(2):
                    rows = slice(e * DH, (e + 1) * DH)
                    for part in range(2):
                        sp.dma_start(q[part * DH:(part + 1) * DH, s, e].bitcast(F32), qT[p][rows, part]).then_inc(pair_in[s], 16)
                        for copy in range(2):
                            sp.dma_start(kd[copy * DH:(copy + 1) * DH, s, e, part].bitcast(F32),
                                         kT[p][rows, part]).then_inc(pair_in[s], 16)
                sp.dma_start(v[:, s], vS.rearrange("n p (h e) -> h p n e", h=NPAIR)[p]).then_inc(pair_in[s], 16)

            sp.dma_start(ident[:], a["ident"]).then_inc(ident_in, 16)
            load_pair(0, 0)
            load_pair(1, 1)

            def tile_done(o):
                if o.q == QT - 1 and not (isinstance(o.pair, int) and o.pair + 2 >= NPAIR) and not o.last:
                    sp.wait_ge(o_ready, o.n + 1)
                    load_pair(o.pair + 2, o.buf)
                if o.s == 1:
                    sp.wait_ge(ost_ready, o.duo + 1)
                    sp.dma_start(oT[o.pair][:, :, (o.q - 1) * P:(o.q + 1) * P],
                                 ost[:, o.duo_slot].bitcast(F32)).then_inc(o_out[o.duo_slot], 16)

            def body(i, last=False):
                for at in range(BODY):
                    o = Tile(i, at)
                    o.last = last
                    tile_done(o)
            body(0)
            with sp.Fori(1, LAST) as i:
                body(i)
            body(LAST, True)
            for s in range(2):
                sp.wait_ge(o_out[s], 16 * NT // 4)

        @block.tensor
        def _(pe):
            pe.wait_ge(ident_in, 16)

            def scores(new, e):
                if new.q == 0 and e == 0:
                    wait(pe, pair_in[new.buf], 16 * 13 * (new.fill + 1))
                wait(pe, exp_done, 2 * (new.n - 1) + e + 1)
                for lo, hi in zip(CUTS, CUTS[1:]):
                    for part in range(2):
                        last = pe.matmul(s_ps[e][:, lo:hi], q[:, new.buf, e, new.q * P:(new.q + 1) * P],
                                         kd[:, new.buf, e, part, lo:hi], start=part == 0, stop=part == 1)
                last.then_inc(s_ready, 1)

            def transposes(tr, ch):
                k0, k1 = CHUNKS[ch]
                wait(pe, wT_ready, 3 * tr.n + ch)
                for kt in range(k0, k1):
                    last = pe.transpose(t_ps[:, (kt - k0) * P:(kt - k0 + 1) * P],
                                        w[:, tr.s, kt * P:(kt + 1) * P], ident[:])
                last.then_inc(t_ready, 1)

            def step(tile):
                new, tr, pv, ot = tile(2), tile(0), tile(-1), tile(-4)
                if tr.exists:
                    wait(pe, w_ready, tr.n + 1)
                    wait(pe, of_ready, tr.n - 4)
                    transposes(tr, 0)
                if new.exists:
                    scores(new, 0)
                if tr.exists:
                    transposes(tr, 1)
                if new.exists:
                    scores(new, 1)
                if ot.exists:
                    wait(pe, on_ready, ot.n + 1)
                    wait(pe, wT_ready, 3 * tr.n + 2 if tr.exists else 3 * NT)
                    wait(pe, of_ready, ot.n)
                    pe.transpose(t_ps[:, 3 * P:4 * P], on[:, ot.s], ident[:]).then_inc(oT_ready, 1)
                if tr.exists:
                    transposes(tr, 2)
                if pv.exists:
                    wait(pe, wT_ready, 3 * pv.n + 3)
                    wait(pe, o_copied, pv.n)
                    for kt in range(KEYS):
                        last = pe.matmul(o_ps[:, 0:P], wT[:, pv.s, kt], v[:, pv.buf, kt],
                                         start=kt == 0, stop=kt == KEYS - 1)
                    last.then_inc(o_ready, 1)

            steps_of(pe, step)

        @block.scalar
        def _(act):
            def copy_wT(tr, ch):
                k0, k1 = CHUNKS[ch]
                wait(act, t_ready, 3 * tr.n + ch + 1)
                act.activation(wT[:, tr.s, k0:k1], t_ps[:, 0:(k1 - k0) * P], ACT.Copy).then_inc(wT_ready, 1)

            def exponentials(new, e):
                wait(act, max_ready, 2 * new.n + e + 1)
                wait(act, w_ready, new.n - 1)
                act.activation(prob[:, new.s, e], s_ps[e][:, 0:TA], ACT.Exp, bias=negmax[:, new.s, e:e + 1],
                               accum_out=sums[:, new.s, e:e + 1]).then_inc(exp_done, 1)

            def step(tile):
                new, tr, pv, ot = tile(2), tile(0), tile(-1), tile(-4)
                if tr.exists:
                    wait(act, o_ready, tr.n - 1)
                    copy_wT(tr, 0)
                if new.exists:
                    exponentials(new, 0)
                if tr.exists:
                    copy_wT(tr, 1)
                if new.exists:
                    exponentials(new, 1)
                if tr.exists:
                    copy_wT(tr, 2)
                if ot.exists:
                    wait(act, oT_ready, ot.n + 1)
                    wait(act, ost_ready, ot.duo - 1)
                    act.activation(of[:, ot.duo_slot, ot.s * P:(ot.s + 1) * P], t_ps[:, 3 * P:4 * P], ACT.Copy,
                                   scale=c["gsub"][:]).then_inc(of_ready, 1)
                if pv.exists:
                    wait(act, o_ready, pv.n + 1)
                    wait(act, on_ready, pv.n - 3)
                    act.activation(osb[:, pv.s4], o_ps[:, 0:P], ACT.Copy).then_inc(o_copied, 1)

            steps_of(act, step)

        @block.vector
        def _(dve):
            dve.memset(half[:], -0.5).then_inc(half_set, 1)

            def step(tile):
                new, nx, sq_t, on_t, ot = tile(2), tile(1), tile(-2), tile(-3), tile(-5)
                if nx.exists:
                    wait(dve, exp_done, 2 * nx.n + 2)
                    wait(dve, p1_scaled, nx.n - 1)
                    dve.reciprocal(rsum[:, nx.s], sums[:, nx.s]).then_inc(rsum_ready, 1)
                if new.exists:
                    for e in range(2):
                        wait(dve, s_ready, 2 * new.n + e + 1)
                        dve.tensor_reduce(negmax[:, new.s, e:e + 1], s_ps[e][:, 0:TA], AX.X,
                                          ALU.max, negate=True).then_inc(max_ready, 1)
                if sq_t.exists:
                    wait(dve, o_copied, sq_t.n + 1)
                    wait(dve, rstd_ready, sq_t.n - 1)
                    wait(dve, ss_ready, sq_t.n)
                    o = osb[:, sq_t.s4]
                    dve.tensor_tensor_reduce(junk[:], o, o, 1.0, 0.0, ALU.mult, ALU.add,
                                             ss[:, sq_t.s:sq_t.s + 1]).then_inc(ss_ready, 1)
                if nx.exists:
                    wait(dve, p1_scaled, nx.n + 1)
                    wait(dve, t_ready, 3 * (nx.n - 2) + 3)
                    wait(dve, rsum_ready, nx.n + 1)
                    dve.scalar_tensor_tensor(out=w[:, nx.s], in0=prob[:, nx.s, 0], scalar=rsum[:, nx.s, 0:1],
                                             in1=prob[:, nx.s, 1], op0=ALU.mult, op1=ALU.add).then_inc(w_ready, 1)
                if on_t.exists:
                    wait(dve, rstd_ready, on_t.n + 1)
                    wait(dve, oT_ready, on_t.n - 1)
                    dve.tensor_scalar(on[:, on_t.s], osb[:, on_t.s4], rstd[:, on_t.s:on_t.s + 1], None,
                                      ALU.mult).then_inc(on_ready, 1)
                if ot.exists and ot.s == 1:
                    full, part = of[:, ot.duo_slot], ost[:, ot.duo_slot]
                    wait(dve, of_ready, ot.n + 1)
                    wait(dve, o_out[ot.duo_slot], 16 * ot.duo_fill)
                    dve.tensor_copy(part[:, 0], full).then_inc(dve_step, 1)
                    wait(dve, dve_step, ot.duo + 1)
                    dve.tensor_tensor(part[:, 1], full, part[:, 0].bitcast(F32), ALU.subtract).then_inc(ost_ready, 1)

            steps_of(dve, step)

        @block.gpsimd
        def _(pool):
            pool.wait_ge(half_set, 1)

            def step(tile):
                nx, pv = tile(1), tile(-2)
                if nx.exists:
                    wait(pool, rsum_ready, nx.n + 1)
                    pool.sem_inc(turn, 1)
                    pool.tensor_scalar(prob[:, nx.s, 1], prob[:, nx.s, 1], rsum[:, nx.s, 1:2], c["neglam"][:],
                                       ALU.mult, ALU.mult).then_inc(p1_scaled, 1)
                if pv.exists:
                    wait(pool, ss_ready, pv.n + 1)
                    wait(pool, on_ready, pv.n - 1)
                    pool.sem_inc(turn, 1)
                    pool.tensor_scalar(ms[:, pv.s:pv.s + 1], ss[:, pv.s:pv.s + 1], 1.0 / P, EPS,
                                       ALU.mult, ALU.add).then_inc(pool_step, 1)
                    wait(pool, pool_step, pv.n + 1)
                    pool.tensor_tensor(rstd[:, pv.s:pv.s + 1], ms[:, pv.s:pv.s + 1], half[:],
                                       ALU.pow).then_inc(rstd_ready, 1)

            steps_of(pool, step)


def block3(nc, a, c, oT, xS, out):
    with ExitStack() as ctx:
        def sb(name, shape, dt=F32):
            return ctx.enter_context(nc.sbuf_tensor(name, shape, dt))

        def sem(name):
            return ctx.enter_context(nc.semaphore(name))

        CH = HALF // P

        base = -(-nc.sbuf_base // 32) * 32
        ctx.enter_context(nc.sbuf_tensor("hid_region", [P, HT * 2 * HALF + 8], F32))

        def at(name, shape, kb, dt=F32):
            return nc.alloc_sbuf_tensor_at(name, shape, dt, offset=base + kb * 1024)

        hid = at("hid", [P, HT, 2, HALF], 0, F32R)
        u = at("u", [P, KT, HALF], 32)
        v = at("v", [P, CH, D], 48)
        rows = at("rows", [P, 3, D], 64)
        bsp = at("bsp", [P, KT, P], 76)
        wsp = at("wsp", [P, KT, P], 80)

        h = sb("h", [P, 2, KT, HALF], F32R)
        ws = sb("wsplit3", [P, NRING, 2, KT, P], F32R)
        raw = sb("wraw3", [P, NRING, KT, P])
        y = sb("y", [P, KT, HALF])
        sq = sb("sq3", [P, 2, HALF])
        sil = sb("silu3", [P, 2, HALF])
        t = sb("t3", [P, 2, HALF])
        acc = sb("acc3", [P, HALF])
        rstd = sb("rstd3", [P, HALF])
        xr = sb("x_ring", [P, 2, HALF])
        st6 = sb("bn6", [P, CH, 2, 6])
        mv = sb("mv", [P, CH, 2])
        rln = sb("rln", [P, CH])
        bank = [ctx.enter_context(nc.psum_tensor(f"acc3_{b}", [P, HALF], F32)) for b in range(4)]
        pstat = ctx.enter_context(nc.psum_tensor("stat3", [P, HALF], F32))

        o_in, rows_in = [sem("o_in0"), sem("o_in1")], sem("rows_in")
        raw_full = [sem(f"b3_raw_full{s}") for s in range(NRING)]
        split_ready = sem("b3_split_ready")
        unit_done = sem("unit_done")
        mix_ready = sem("mix_ready")
        bank_free = [sem(f"b3_bank_free{b}") for b in range(4)]
        silu_ready, hid_ready = sem("silu_ready3"), sem("hid_ready")
        sq_ready, sq_used = sem("b3_sq_ready"), sem("b3_sq_used")
        stat_ready, std_ready = sem("b3_stat_ready"), sem("b3_std_ready")
        x_in = [sem(f"b3_x_in{s}") for s in range(2)]
        x_new, x_out = sem("x_new"), sem("x_out")
        t_ready, hf_ready, h_ready = sem("b3_t_ready"), sem("b3_hf_ready"), sem("b3_h_ready")
        u_ready, v_ready, var_std, ln_ready = sem("u_ready"), sem("v_ready"), sem("var_std"), sem("ln_ready")
        var_ready = sem("var_ready")
        dve_step, pool_step, turn = sem("b3_dve_step"), sem("b3_pool_step"), sem("b3_turn")

        stages = []
        U = G = H = S = 0
        for kind, layer in (("O", 0), ("F", 0), ("C", 1), ("F", 1)):
            for half in range(2):
                units = {"O": (0, KT), "F": (2 * HT, 3 * KT), "C": (2 * KT, KT)}[kind]
                groups = {"O": (0, KT), "F": (2 * HT, KT), "C": (3 * KT, KT)}[kind]
                s = dict(kind=kind, layer=layer, half=half, j=len(stages), U=U, G=G, H=H, S=S,
                         vec=2 * layer + (kind == "F"),
                         U_out=U + units[0], G_out=G + groups[0],
                         final=kind == "F" and layer == 1)
                U, G = U + sum(units), G + sum(groups)
                H += {"O": 0, "F": HT, "C": KT}[kind]
                S += HT if kind == "F" else 0
                s.update(U_end=U, H_end=H)
                stages.append(s)
        n_norm = {}
        for s in stages:
            n_norm["post", s["j"]] = len(n_norm)
            if not s["final"]:
                n_norm["pre", s["j"]] = len(n_norm)

        def prev(s):
            return stages[s["j"] - 1] if s["j"] else None

        def y_done(s, i4, f):
            per = 3 if s["kind"] == "F" else 1
            return s["U_out"] + per * (4 * i4 + f + 1)

        block = ctx.enter_context(nc.Block())

        @block.sync
        def _(sp):
            for half in range(2):
                for k in range(KT):
                    sp.dma_start(hid[:, half * KT + k].bitcast(F32), oT[k][:, :, half * HALF:(half + 1) * HALF]
                                 ).then_inc(o_in[half], 16)

            def load(u, slot, n_kt, src):
                wait(sp, split_ready, u - NRING + 1)
                sp.dma_start(raw[:, slot, 0:n_kt], src).then_inc(raw_full[slot], 16)

            def plain(name, u0, n):
                def body(i):
                    for k in range(4):
                        load(u0 + 4 * i + k, k, KT, a[name][4 * i + k].rearrange("p (k c) -> p k c", k=KT))
                loop(sp, n, body)

            for s in stages:
                if s["kind"] == "O":
                    plain("w_attn_out", s["U"], 2)
                elif s["kind"] == "C":
                    plain("w_uv", s["U"], 4)
                    plain("w_cmlp_out", s["U_out"], 2)
                else:
                    plain(f"w_ffn_in{s['layer']}", s["U"], HT // 2)

                    def body(i):
                        for f in range(4):
                            w = a[f"w_ffn_out{s['layer']}"][4 * i + f].rearrange("p (k c) -> p k c", k=HT)
                            for m, (k0, k1) in enumerate(GROUPS_KT):
                                n = 3 * f + m
                                load(s["U_out"] + 12 * i + n, n % NRING, k1 - k0, w[:, k0:k1])
                    loop(sp, 2, body)

        @block.gpsimd
        def _(pool):
            steps = Steps(pool, pool_step)

            def unit(u0, i4, k, n_kt, done=None):
                pool.wait_ge(raw_full[k % NRING], 16 * (u0 // NRING + i4 + k // NRING + 1))
                wait(pool, unit_done, u0 + 4 * i4 + k - NRING + 1 if done is None else done)
                split_weights(pool, turn, steps, raw, ws, k % NRING, n_kt, split_ready)

            for s in stages:
                if s["kind"] == "O":
                    steps.loop(2, 4, lambda i: [unit(s["U"], i, k, KT) for k in range(4)])
                elif s["kind"] == "C":
                    for i in range(3):
                        for k in range(4):
                            unit(s["U"], i, k, KT, s["U"] + 4 * i if i else None)
                    steps.loop(3, 4, lambda i: [unit(s["U"] + 12, i, k, KT) for k in range(4)])
                else:
                    steps.loop(HT // 2, 4, lambda i: [unit(s["U"], i, k, KT) for k in range(4)])
                    steps.loop(2, 12, lambda i: [unit(s["U_out"], 3 * i, 3 * f + m, k1 - k0)
                                                 for f in range(4) for m, (k0, k1) in enumerate(GROUPS_KT)])

        @block.tensor
        def _(pe):
            def bank_wait(g0, i4, at):
                wait(pe, bank_free[at % 4], g0 // 4 + i4 + at // 4)

            def stat(which, s):
                if s is None or (which, s["j"]) not in n_norm:
                    return
                n = n_norm[which, s["j"]]
                pe.wait_ge(sq_used, KT * (n + 1))
                wait(pe, std_ready, n)
                pe.matmul(pstat[:], c["ones"][:], acc[:], start=True, stop=True).then_inc(stat_ready, 1)

            def one(u0, g0, i, k, x):
                wait(pe, split_ready, u0 + 4 * i + k + 1)
                bank_wait(g0, i, k)
                product(pe, bank[k][:], KT, W(lambda p, kt: ws[:, k, p, kt]), x).then_inc(unit_done, 1)

            for s in stages:
                if s["kind"] == "O":
                    pe.wait_ge(o_in[s["half"]], 16 * KT)
                    for n in range(KT):
                        one(s["U"], s["G"], n // 4, n % 4, lambda p, kt: hid[:, s["half"] * KT + kt, p])
                        if n == 0:
                            stat("post", prev(s))
                        if n == 2:
                            stat("pre", prev(s))
                    continue

                pe.wait_ge(h_ready, KT * (s["j"] - 1))
                if s["kind"] == "F":
                    def hidden_tile(i, m):
                        for k in (2 * m, 2 * m + 1):
                            one(s["U"], s["G"], i, k, lambda p, kt: h[:, p, kt])
                    for i in range(3):
                        for m in range(2):
                            hidden_tile(i, m)
                            if (i, m) == (0, 0):
                                stat("post", prev(s))
                            if (i, m) == (2, 0):
                                stat("pre", prev(s))
                    with pe.Fori(3, HT // 2) as i:
                        for m in range(2):
                            hidden_tile(i, m)

                    def body(i):
                        for f in range(4):
                            bank_wait(s["G_out"], i, f)
                            for m, (k0, k1) in enumerate(GROUPS_KT):
                                n = 3 * f + m
                                wait(pe, split_ready, s["U_out"] + 12 * i + n + 1)
                                pe.wait_ge(hid_ready, s["H"] + k1)
                                product(pe, bank[f][:], k1 - k0,
                                        W(lambda p, kt: ws[:, n % NRING, p, kt], m == 0, m == 2),
                                        lambda p, kt: hid[:, k0 + kt, p]).then_inc(unit_done, 1)
                    loop(pe, 2, body)
                else:
                    for half in range(2):
                        pe.wait_ge(split_ready, s["U"] + 4 * half + 4)
                        for n in range(CH):
                            bank_wait(s["G"], half, n)
                            product(pe, bank[n][:], KT, W(lambda p, kt: h[:, p, kt, n * P:(n + 1) * P]),
                                    lambda p, kt: ws[:, 0:4, p, kt]).then_inc(unit_done, 1)
                            if (half, n) == (0, 1):
                                stat("post", prev(s))
                    stat("pre", prev(s))
                    loop(pe, 2, lambda i: [one(s["U"] + KT, s["G"] + KT, i, k, lambda p, kt: h[:, p, kt])
                                           for k in range(4)])
                    pe.wait_ge(ln_ready, CH * (s["half"] + 1))
                    for g in range(KT):
                        bank_wait(s["G"] + 2 * KT, 0, g)
                        for n in range(CH):
                            last = pe.matmul(bank[g % 4][:, n * P:(n + 1) * P], v[:, n, g * P:(g + 1) * P],
                                             wsp[:, g], start=True, stop=True)
                        last.then_inc(mix_ready, 1)
                    pe.wait_ge(hid_ready, s["H_end"])
                    loop(pe, 2, lambda i: [one(s["U_out"], s["G_out"], i, k, lambda p, kt: hid[:, kt, p])
                                           for k in range(4)])
            stat("post", stages[-1])

        @block.scalar
        def _(act):
            def square(n, ft):
                wait(act, sq_used, KT * n + ft - 1)
                act.activation(sq[:, ft % 2], y[:, ft], ACT.Square).then_inc(sq_ready, 1)

            def load_x(s, ft):
                j = s["j"]
                if j >= 2 and ft == 0:
                    act.wait_ge(x_out, 16 * (j - 1))
                wait(act, x_new, KT * j + ft - 1)
                src = a["xT"] if s["kind"] == "O" else xS
                act.dma_start(xr[:, ft % 2], src[ft][:, s["half"] * HALF:(s["half"] + 1) * HALF]
                              ).then_inc(x_in[ft % 2], 16)

            def std(which, s):
                n = n_norm[which, s["j"]]
                act.wait_ge(stat_ready, n + 1)
                if which == "post":
                    wait(act, t_ready, KT * min(s["j"], len(stages) - 2))
                else:
                    act.wait_ge(x_new, KT * (s["j"] + 1))
                act.activation(rstd[:], pstat[:], ACT.Sqrt, bias=c["eps"][:]).then_inc(std_ready, 1)

            def post(s):
                std("post", s)
                for ft in range(KT):
                    act.wait_ge(x_new, KT * s["j"] + ft + 1)
                    if ft + 2 < KT:
                        load_x(s, ft + 2)
                    if not s["final"]:
                        square(n_norm["pre", s["j"]], ft)
                cols = slice(s["half"] * HALF, (s["half"] + 1) * HALF)
                dst = out if s["final"] else xS
                act.dma_start(dst[:, :, cols].rearrange("k p t -> p k t"), y[:]).then_inc(x_out, 16)

            def make_h(s):
                m = s["vec"] + 1
                shift0 = (m // 2) * 6 * KT + (SH_F if m % 2 else SH_M) * KT
                for ft in range(KT):
                    act.wait_ge(t_ready, KT * s["j"] + ft + 1)
                    act.activation(t[:, ft % 2], t[:, ft % 2], ACT.Identity,
                                   bias=c["mod"][:, shift0 + ft:shift0 + ft + 1],
                                   scale=c["A"][:, m, ft:ft + 1]).then_inc(hf_ready, 1)

            for s in stages:
                p = prev(s)
                if p:
                    load_x(p, 0)
                    load_x(p, 1)
                if s["kind"] == "O":
                    if p:
                        post(p)
                        std("pre", p)
                        make_h(p)
                elif s["kind"] == "F":
                    def silu(i, m):
                        wait(act, unit_done, s["U"] + 4 * i + 2 * m + 1)
                        wait(act, bank_free[2 * m + 1], s["G"] // 4 + i)
                        act.activation(sil[:, m], bank[2 * m][:], ACT.Silu).then_inc(silu_ready, 1)
                    silu(0, 0)
                    post(p)
                    for i, m in ((0, 1), (1, 0), (1, 1), (2, 0)):
                        silu(i, m)
                    if not p["final"]:
                        std("pre", p)
                    silu(2, 1)
                    with act.Fori(3, HT // 2) as i:
                        for m in range(2):
                            silu(i, m)
                    if not p["final"]:
                        make_h(p)
                else:
                    if s["half"] == 0:
                        act.wait_ge(unit_done, p["U_end"])
                        act.dma_start(rows[:], a["rows"]).then_inc(rows_in, 16)
                        act.dma_start(bsp[:], a["b_spatial"]).then_inc(rows_in, 16)
                        act.dma_start(wsp[:], a["w_spatialT"]).then_inc(rows_in, 16)

                    def gelu_v(half, n):
                        act.wait_ge(bank_free[n], s["G"] // 4 + half + 1)
                        x = v[:, n, half * HALF:(half + 1) * HALF]
                        act.activation(x, x, ACT.Gelu).then_inc(v_ready, 1)
                    gelu_v(0, 0)
                    gelu_v(0, 1)
                    post(p)
                    for half, n in ((0, 2), (0, 3), (1, 0), (1, 1), (1, 2), (1, 3)):
                        gelu_v(half, n)
                    std("pre", p)
                    for ft in range(KT):
                        if ft == 2:
                            act.wait_ge(var_ready, s["half"] + 1)
                            act.activation(rln[:], mv[:, :, 1], ACT.Sqrt, bias=c["eps"][:]).then_inc(var_std, 1)
                        act.wait_ge(unit_done, s["U"] + KT + ft + 1)
                        act.activation(u[:, ft], bank[ft % 4][:], ACT.Gelu,
                                       bias=c["vecs"][:, V_BU + ft:V_BU + ft + 1]).then_inc(bank_free[ft % 4], 1)
                    make_h(p)

                def squares(i):
                    for f in range(4):
                        wait(act, bank_free[f], s["G_out"] // 4 + i + 1)
                        n = n_norm["post", s["j"]]
                        wait(act, sq_used, KT * n + 4 * i + f - 1)
                        act.activation(sq[:, f % 2], y[:, bass.ds(4 * i + f, 1)], ACT.Square).then_inc(sq_ready, 1)
                for i in range(2):
                    squares(i)
            s = stages[-1]
            load_x(s, 0)
            load_x(s, 1)
            post(s)
            act.wait_ge(x_out, 16 * len(stages))

        @block.vector
        def _(dve):
            steps = Steps(dve, dve_step)

            def add_square(n, ft):
                dve.wait_ge(sq_ready, KT * n + ft + 1)
                wait(dve, sq_used, KT * n + ft)
                dve.tensor_tensor(acc[:], acc[:], sq[:, ft % 2], ALU.add).then_inc(sq_used, 1)

            def clear_acc(n):
                wait(dve, stat_ready, n)
                steps.did(dve.memset(acc[:], 0.0))
                steps.sync()

            def inverse(which, s):
                dve.wait_ge(std_ready, n_norm[which, s["j"]] + 1)
                steps.did(dve.reciprocal(rstd[:], rstd[:]))
                steps.sync()

            def post(s):
                inverse("post", s)
                n = n_norm.get(("pre", s["j"]))
                if n is not None:
                    clear_acc(n)
                for ft in range(KT):
                    steps.did(dve.tensor_tensor(y[:, ft], y[:, ft], rstd[:], ALU.mult))
                    steps.sync()
                    dve.wait_ge(x_in[ft % 2], 16 * (KT // 2 * s["j"] + ft // 2 + 1))
                    dve.scalar_tensor_tensor(out=y[:, ft], in0=y[:, ft], scalar=c["G"][:, s["vec"], ft:ft + 1],
                                             in1=xr[:, ft % 2], op0=ALU.mult, op1=ALU.add).then_inc(x_new, 1)
                    if n is not None and ft:
                        add_square(n, ft - 1)
                if n is not None:
                    add_square(n, KT - 1)

            def make_h(s, h_free):
                wait(dve, unit_done, h_free)
                wait(dve, hid_ready, s["H_end"])

                def scaled(ft):
                    wait(dve, h_ready, KT * s["j"] + ft - 1)
                    dve.tensor_tensor(t[:, ft % 2], y[:, ft], rstd[:], ALU.mult).then_inc(t_ready, 1)
                scaled(0)
                for ft in range(KT):
                    if ft + 1 < KT:
                        scaled(ft + 1)
                    dve.wait_ge(hf_ready, KT * s["j"] + ft + 1)
                    steps.did(dve.tensor_copy(h[:, 0, ft], t[:, ft % 2]))
                    steps.sync()
                    dve.tensor_tensor(h[:, 1, ft], t[:, ft % 2], h[:, 0, ft].bitcast(F32),
                                      ALU.subtract).then_inc(h_ready, 1)

            for s in stages:
                p = prev(s)
                if s["kind"] == "O":
                    if p:
                        post(p)
                        inverse("pre", p)
                        make_h(p, 0)
                elif s["kind"] == "F":
                    dve.wait_ge(unit_done, p["U_end"])

                    def hidden_tile(i, m):
                        full, up = t[:, m], 2 * m + 1
                        dve.wait_ge(silu_ready, s["S"] + 2 * i + m + 1)
                        dve.wait_ge(unit_done, s["U"] + 4 * i + 2 * m + 2)
                        wait(dve, hid_ready, s["H"] + 2 * i + m - 1)
                        dve.tensor_tensor(full, sil[:, m], bank[up][:], ALU.mult).then_inc(bank_free[up], 1)
                        dve.wait_ge(bank_free[up], s["G"] // 4 + i + 1)
                        hi = hid[:, bass.ds(2 * i + m, 1), 0]
                        lo = hid[:, bass.ds(2 * i + m, 1), 1]
                        dve.tensor_copy(hi, full).then_inc(bank_free[2 * m], 1)
                        dve.wait_ge(bank_free[2 * m], s["G"] // 4 + i + 1)
                        dve.tensor_tensor(lo, full, hi.bitcast(F32), ALU.subtract).then_inc(hid_ready, 1)
                    hidden_tile(0, 0)
                    post(p)
                    for i, m in ((0, 1), (1, 0), (1, 1), (2, 0)):
                        hidden_tile(i, m)
                    if not p["final"]:
                        inverse("pre", p)
                    hidden_tile(2, 1)
                    with dve.Fori(3, HT // 2) as i:
                        for m in range(2):
                            hidden_tile(i, m)
                    if not p["final"]:
                        dve.wait_ge(hid_ready, s["H_end"])
                        make_h(p, s["U_out"])
                else:
                    dve.wait_ge(unit_done, p["U_end"])
                    dve.wait_ge(rows_in, 48)

                    def add_bias(half, n):
                        dve.wait_ge(unit_done, s["U"] + 4 * half + n + 1)
                        cols = slice(half * HALF, (half + 1) * HALF)
                        dve.tensor_tensor(v[:, n, cols], bank[n][:], rows[:, 0, cols],
                                          ALU.add).then_inc(bank_free[n], 1)
                    add_bias(0, 0)
                    add_bias(0, 1)
                    post(p)
                    for half, n in ((0, 2), (0, 3), (1, 0), (1, 1), (1, 2), (1, 3)):
                        add_bias(half, n)
                    inverse("pre", p)
                    for n in range(CH):
                        dve.wait_ge(v_ready, 2 * CH * s["half"] + CH + n + 1)
                        for half in range(2):
                            steps.did(dve.bn_stats(st6[:, n, half], v[:, n, half * HALF:(half + 1) * HALF]))
                        steps.sync()
                        if n < CH - 1:
                            steps.did(dve.bn_aggr(mv[:, n], st6[:, n]))
                        else:
                            dve.bn_aggr(mv[:, n], st6[:, n]).then_inc(var_ready, 1)
                    dve.wait_ge(var_std, s["half"] + 1)
                    steps.did(dve.reciprocal(rln[:], rln[:]))
                    steps.sync()
                    for n in range(CH):
                        steps.did(dve.tensor_scalar(v[:, n], v[:, n], mv[:, n, 0:1], rln[:, n:n + 1],
                                                    ALU.subtract, ALU.mult))
                        steps.sync()
                        steps.did(dve.tensor_tensor(v[:, n], v[:, n], rows[:, 1], ALU.mult))
                        steps.sync()
                        dve.tensor_tensor(v[:, n], v[:, n], rows[:, 2], ALU.add).then_inc(ln_ready, 1)
                    for g in range(KT):
                        k = g % 4
                        dve.wait_ge(mix_ready, KT * s["half"] + g + 1)
                        wait(dve, hid_ready, s["H"] + g)
                        full = t[:, g % 2].rearrange("p (n q) -> p n q", n=CH)
                        dve.tensor_tensor(full, bank[k][:].rearrange("p (n q) -> p n q", n=CH),
                                          bsp[:, g:g + 1].to_broadcast([P, CH, P]),
                                          ALU.add).then_inc(bank_free[k], 1)
                        dve.wait_ge(bank_free[k], (s["G"] + 2 * KT) // 4 + g // 4 + 1)
                        steps.did(dve.tensor_tensor(t[:, g % 2], t[:, g % 2], u[:, g], ALU.mult))
                        steps.sync()
                        steps.did(dve.tensor_copy(hid[:, g, 0], t[:, g % 2]))
                        steps.sync()
                        dve.tensor_tensor(hid[:, g, 1], t[:, g % 2], hid[:, g, 0].bitcast(F32),
                                          ALU.subtract).then_inc(hid_ready, 1)
                    dve.wait_ge(hid_ready, s["H_end"])
                    make_h(p, s["U_out"])

                n = n_norm["post", s["j"]]
                if p:
                    dve.wait_ge(x_out, 16 * s["j"])
                    wait(dve, h_ready, KT * min(s["j"], len(stages) - 2))
                clear_acc(n)
                for ft in range(KT):
                    dve.wait_ge(unit_done, y_done(s, ft // 4, ft % 4))
                    dve.tensor_copy(y[:, ft], bank[ft % 4][:]).then_inc(bank_free[ft % 4], 1)
                    if ft:
                        add_square(n, ft - 1)
                add_square(n, KT - 1)
            post(stages[-1])


def launch_tables():
    axis = DH // 2
    inv = np.float32(10000.0) ** (-np.arange(0, axis, 2, dtype=np.float32) / np.float32(axis))
    row = np.repeat(np.arange(T // 64, dtype=np.float32), 64)
    col = np.tile(np.arange(64, dtype=np.float32), T // 64)
    cos, sin = np.zeros((P, T), np.float32), np.zeros((P, T), np.float32)
    for p in range(P):
        pos = row if p % DH < axis else col
        f = p % axis
        ang = (pos * inv[f % (axis // 2)]).astype(np.float32)
        cos[p] = np.cos(ang)
        sin[p] = np.sin(ang) if f >= axis // 2 else -np.sin(ang)
    return np.ascontiguousarray(np.stack([cos, sin], 1))


def kernel(x, c, ctx, c_ctx, w_ada, b_ada, g_mix_pre, g_mix_post, g_ffn_pre, g_ffn_post, w_qkv, w_attn_out,
           lam_q1, lam_k1, lam_q2, lam_k2, g_subln, w_uv, b_uv, g_sgu, b_sgu, w_spatial, b_spatial,
           w_cmlp_out, w_ffn_in, w_ffn_out):
    import concourse.bacc as bacc
    from concourse.bass_utils import run_bass_kernel_spmd

    def arr(v):
        return np.asarray(v)

    def tiles(w):
        w = arr(w)
        K, N = w.shape
        return np.ascontiguousarray(w.reshape(K // P, P, N // P, P).transpose(2, 1, 0, 3)).reshape(N // P, P, K)

    def cols(v):
        return arr(v).reshape(-1, P).T

    def row(v):
        return np.broadcast_to(arr(v).reshape(1, -1), (P, arr(v).size))

    ada = np.concatenate([tiles(arr(w_ada)[i]) for i in range(2)])
    vecs = np.concatenate([cols(b_ada), cols(g_mix_pre), cols(g_mix_post), cols(g_ffn_pre), cols(g_ffn_post),
                           cols(c), cols(c_ctx), cols(arr(b_uv)[0, :D]), cols(g_subln)], axis=1)
    uv = tiles(arr(w_uv)[0])
    arrays = {
        "xT": arr(x)[0].T.reshape(KT, P, T),
        "ctxT": arr(ctx)[0].T.reshape(KT, P, C),
        "vecs": vecs,
        "lamv": np.stack([row(lam_q1), row(lam_k1), row(lam_q2), row(lam_k2)], 1),
        "trig": launch_tables(),
        "ident": np.eye(P, dtype=np.float32),
        "w_ada": ada,
        "w_qkv": tiles(arr(w_qkv)[0]),
        "w_attn_out": tiles(arr(w_attn_out)[0]),
        "w_uv": np.concatenate([uv[KT:], uv[:KT]]),
        "w_cmlp_out": tiles(arr(w_cmlp_out)[0]),
        "rows": np.stack([row(arr(b_uv)[0, D:]), row(g_sgu), row(b_sgu)], 1),
        "b_spatial": np.broadcast_to(arr(b_spatial)[0][None], (P, KT, P)),
        "w_spatialT": arr(w_spatial)[0].transpose(2, 0, 1),
    }
    for i in range(2):
        w = tiles(arr(w_ffn_in)[i])
        arrays[f"w_ffn_in{i}"] = np.stack([w[:HT], w[HT:]], 1).reshape(2 * HT, P, D)
        arrays[f"w_ffn_out{i}"] = tiles(arr(w_ffn_out)[i])
    nc = bacc.Bacc("TRN2", target_bir_lowering=False, num_devices=1)
    feed, aps = {}, {}
    for name, v in arrays.items():
        feed[f"in_{name}"] = v = np.ascontiguousarray(v)
        aps[name] = nc.dram_tensor(f"in_{name}", list(v.shape), F32, kind="ExternalInput").ap()
    out = nc.dram_tensor("out_xT", [KT, P, T], F32, kind="ExternalOutput").ap()
    build(nc, aps, out)
    got = run_bass_kernel_spmd(nc, [feed], core_ids=[0]).results[0]["out_xT"]
    return np.ascontiguousarray(got.reshape(D, T).T).reshape(1, T, D)
```

```python
import math
from contextlib import ExitStack

import numpy as np
import concourse.bass as bass
from concourse import mybir
from concourse.alu_op_type import AluOpType as ALU

ACT = mybir.ActivationFunctionType
AX = mybir.AxisListType
F32 = mybir.dt.float32
F32R = mybir.dt.float32r

P = 128
D = 1024
KT = D // P
T = 1024
C = 256
TA = T + C
HALF = T // 2
FH = 2816
HT = FH // P
DH = 64
NPAIR = 8
NADA = 2 * 6 * KT
EPS = 1e-6
LAM_INIT = 0.8 - 0.6 * math.exp(-0.3 * 0)
NRING = 4
GROUPS_KT = [(0, 8), (8, 16), (16, HT)]

V_BADA = 0
V_MIXPRE = V_BADA + NADA
V_MIXPOST = V_MIXPRE + 2 * KT
V_FFNPRE = V_MIXPOST + 2 * KT
V_FFNPOST = V_FFNPRE + 2 * KT
V_C = V_FFNPOST + 2 * KT
V_CCTX = V_C + KT
V_BU = V_CCTX + KT
V_SUBLN = V_BU + KT
NV = V_SUBLN + 1
SH_M, SC_M, G_M, SH_F, SC_F, G_F = range(6)


def wait(eng, sem, value):
    if isinstance(value, int) and value <= 0:
        return
    eng.wait_ge(sem, value)


def opens(i):
    return isinstance(i, int) and i == 0


def loop(eng, n, body):
    body(0)
    if n > 1:
        with eng.Fori(1, n) as i:
            body(i)


class Steps:

    def __init__(self, eng, sem):
        self.eng, self.sem, self.n, self.base = eng, sem, 0, 0

    def did(self, ins):
        ins.then_inc(self.sem, 1)
        self.n += 1

    def sync(self):
        self.eng.wait_ge(self.sem, self.base + self.n)

    def loop(self, n, per, body):
        start = self.n
        body(0)
        assert self.n - start == per, (self.n - start, per)
        if n > 1:
            with self.eng.Fori(1, n) as i:
                self.n, self.base = start, i * per
                body(i)
            self.base = 0
        self.n = start + n * per


def product(pe, out, n_kt, weight, x):
    for kt in range(n_kt):
        for a, b in ((0, 0), (0, 1), (1, 0)):
            last = pe.matmul(out, weight(a, kt), x(b, kt), start=weight.first and kt == 0 and a == b == 0,
                             stop=weight.last and kt == n_kt - 1 and a == 1)
    return last


class W:

    def __init__(self, at, first=True, last=True):
        self.at, self.first, self.last = at, first, last

    def __call__(self, a, kt):
        return self.at(a, kt)


def split_weights(pool, turn, steps, raw, ws, slot, n_kt, split_ready):
    pool.sem_inc(turn, 1)
    steps.did(pool.tensor_scalar(ws[:, slot, 0, 0:n_kt, :], raw[:, slot, 0:n_kt, :], 1.0, 1.0, ALU.mult, ALU.mult))
    steps.sync()
    pool.tensor_tensor(ws[:, slot, 1, 0:n_kt, :], raw[:, slot, 0:n_kt, :],
                       ws[:, slot, 0, 0:n_kt, :].bitcast(F32), ALU.subtract).then_inc(split_ready, 1)


def build(nc, a, out):
    with ExitStack() as keep:
        def sb(name, shape, dt=F32):
            return keep.enter_context(nc.sbuf_tensor(name, shape, dt))

        qT = nc.dram_tensor("q_scratch", [KT, P, 2, T], F32, kind="Internal").ap()
        kT = nc.dram_tensor("k_scratch", [KT, P, 2, TA], F32, kind="Internal").ap()
        vS = nc.dram_tensor("v_scratch", [TA // P, P, D], F32, kind="Internal").ap()
        oT = nc.dram_tensor("o_scratch", [NPAIR, P, 2, T], F32, kind="Internal").ap()
        xS = nc.dram_tensor("x_scratch", [KT, P, T], F32, kind="Internal").ap()
        c = {
            "vecs": sb("vecs", [P, NV]),
            "mod": sb("mod", [P, NADA]),
            "modc": sb("modc", [P, 2 * KT]),
            "A": sb("A", [P, 5, KT]),
            "G": sb("G", [P, 4, KT]),
            "neglam": sb("neglam", [P, 1]),
            "gsub": sb("gsub", [P, 1]),
            "ones": sb("ones", [P, P]),
            "eps": sb("eps", [P, 1]),
        }
        block1(nc, a, c, qT, kT, vS)
        block2(nc, a, c, qT, kT, vS, oT)
        block3(nc, a, c, oT, xS, out)


def block1(nc, a, c, qT, kT, vS):
    with ExitStack() as ctx:
        def sb(name, shape, dt=F32):
            return ctx.enter_context(nc.sbuf_tensor(name, shape, dt))

        def sem(name):
            return ctx.enter_context(nc.semaphore(name))

        W_ADA = T
        h = sb("h_all", [P, 2, KT, TA], F32R)
        base = -(-nc.sbuf_base // 32) * 32
        ctx.enter_context(nc.sbuf_tensor("shared_region", [P, 72 * 256 + 8], F32))

        def at(name, shape, kb, dt=F32):
            return nc.alloc_sbuf_tensor_at(name, shape, dt, offset=base + kb * 1024)

        ws = at("wsplit1", [P, NRING, 2, KT, P], 0, F32R)
        first_sum = at("first_sum", [P, 2, W_ADA], 16)
        y = at("x_in", [P, 2, KT, HALF], 32)
        xc = at("ctx_in", [P, KT, C], 32)
        late = at("ctx_tmp", [P, 5, C], 40)
        late_sum = at("late_sum", [P, 2, 2, W_ADA], 48)
        ws_v = at("wsplit_v", [P, NRING, 2, KT, P], 32, F32R)
        st = at("qk_out", [P, 2, 2, HALF], 64, F32R)
        raw = sb("wraw1", [P, NRING, KT, P])
        ada = sb("ada_raw", [P, 4, W_ADA])
        trig = sb("trig", [P, 2, T])
        sq = sb("sq1", [P, 2, HALF])
        t = sb("t1", [P, 2, HALF])
        cosp = sb("cos_part", [P, HALF])
        rstd = sb("rstd1", [P, HALF])
        lamv = sb("lamv", [P, 4, DH])
        lams = sb("lams", [P, 4])
        sx = sb("silu_c", [P, 2, KT])
        bank = [ctx.enter_context(nc.psum_tensor(f"acc1_{b}", [P, HALF], F32)) for b in range(4)]
        pstat = ctx.enter_context(nc.psum_tensor("stat1", [P, HALF], F32))
        pada = ctx.enter_context(nc.psum_tensor("ada_ps", [P, HALF], F32))

        last_sum = trig
        vecs_in, lam_in, trig_in = sem("vecs_in"), sem("lam_in"), sem("trig_in")
        x_in = [sem(f"x_in{s}") for s in range(3)]
        raw_full = [sem(f"b1_raw_full{s}") for s in range(NRING)]
        ada_full = [sem(f"ada_full{s}") for s in range(4)]
        split_ready = sem("b1_split_ready")
        ada_dve, ada_pool = sem("ada_dve"), sem("ada_pool")
        ada_scaled = sem("ada_scaled")
        sum_ready, mod_out = sem("sum_ready"), sem("mod_out")
        silu_ready, const_ready, mods_ready = sem("silu_ready"), sem("const_ready"), sem("mods_ready")
        sq_ready, sq_used = sem("b1_sq_ready"), sem("b1_sq_used")
        std_ready, y_ready, t_ready = sem("b1_std_ready"), sem("b1_y_ready"), sem("b1_t_ready")
        hi_ready, h_ready = sem("b1_hi_ready"), sem("b1_h_ready")
        group_ready = sem("b1_group_ready")
        bank_free = [sem(f"b1_bank_free{b}") for b in range(4)]
        rope_done, qk_hi, qk_lo = sem("rope_done"), sem("qk_hi"), sem("qk_lo")
        st_out = [sem(f"st_out{s}") for s in range(2)]
        v_out = [sem(f"v_out{s}") for s in range(2)]
        dve_step, pool_step, turn = sem("b1_dve_step"), sem("b1_pool_step"), sem("b1_turn")
        lam_exp = sem("lam_exp")

        SEG = [(y[:, 0], HALF, C, sq, t, rstd), (y[:, 1], HALF, C + HALF, sq, t, rstd),
               (xc, C, 0, late[:, 0:2], late[:, 2:4], late[:, 4])]
        FIRST = 2
        QKG = [[1, 2], [0, 1, 2]]
        G_K, G_V = 2 * KT, 2 * KT + 3 * KT
        VT = TA // P

        def cols(g):
            return (0, C) if g == 0 else (C + (g - 1) * HALF, C + g * HALF)

        def before(kind, i, k, n):
            if n > 0:
                return kind, i, k, n - 1
            if k > 0:
                return kind, i, k - 1, len(QKG[kind]) - 1
            if opens(i):
                return (0, 1, 3, 1) if kind else None
            return kind, i - 1, 3, len(QKG[kind]) - 1

        def number(kind, i, k, n):
            ng = len(QKG[kind])
            return (G_K if kind else 0) + 4 * ng * i + ng * k + n, ng * k + n

        def first_of_all(kind, i, k):
            return kind == 0 and opens(i) and k == 0

        block = ctx.enter_context(nc.Block())

        def sums_of(j):
            return last_sum if j >= 4 else late_sum[:, j % 2]

        def wait_sums_free(eng, j):
            wait(eng, sum_ready, FIRST + 5 if j == 5 else FIRST + j - 1)

        @block.sync
        def _(sp):
            def load_first_ada(n):
                wait(sp, ada_dve, n - 3)
                sp.dma_start(ada[:, n % 4], a["w_ada"][n // KT, n % KT]).then_inc(ada_full[n % 4], 16)

            def load_ada(j, kt):
                for e, (used, before) in enumerate(((ada_dve, FIRST * KT), (ada_pool, 0))):
                    wait(sp, used, before + KT * j + kt - 1)
                    s = 2 * e + kt % 2
                    sp.dma_start(ada[:, s], a["w_ada"][2 * j + e, kt]).then_inc(ada_full[s], 16)

            def load_w(u, s):
                wait(sp, split_ready, u - NRING + 1)
                sp.dma_start(raw[:, s], a["w_qkv"][u].rearrange("p (k c) -> p k c", k=KT)).then_inc(raw_full[s], 16)

            sp.dma_start(c["vecs"][:], a["vecs"]).then_inc(vecs_in, 16)
            sp.dma_start(lamv[:], a["lamv"]).then_inc(lam_in, 16)
            for half in range(2):
                sp.dma_start(y[:, half], a["xT"][:, :, half * HALF:(half + 1) * HALF].rearrange(
                    "k p t -> p k t")).then_inc(x_in[half], 16)
                for kt in range(KT):
                    load_first_ada(half * KT + kt)
            for u in range(NRING):
                load_w(u, u)
            sp.dma_start(trig[:], a["trig"]).then_inc(trig_in, 16)
            sp.wait_ge(t_ready, KT)
            sp.dma_start(xc[:], a["ctxT"].rearrange("k p t -> p k t")).then_inc(x_in[2], 16)
            sp.wait_ge(ada_dve, FIRST * KT)

            def body(j):
                for k in range(4):
                    load_ada(j, 2 * k)
                    load_ada(j, 2 * k + 1)
                    load_w(4 * j + k + NRING, k)
            loop(sp, 5, body)
            for kt in range(KT):
                load_ada(5, kt)

        @block.gpsimd
        def _(pool):
            steps = Steps(pool, pool_step)
            def modulation(j, kt):
                m = KT * j + kt
                total, term = sums_of(j)[:, 1], ada[:, 2 + kt % 2]
                wait(pool, ada_scaled, m + 1)
                wait(pool, ada_pool, m)
                if kt == 0:
                    wait_sums_free(pool, j)
                pool.sem_inc(turn, 1)
                if kt == 0:
                    pool.tensor_scalar(total, term, 1.0, 1.0, ALU.mult, ALU.mult).then_inc(ada_pool, 1)
                else:
                    pool.tensor_tensor(total, total, term, ALU.add).then_inc(ada_pool, 1)

            def split(turn_, k, into):
                pool.wait_ge(raw_full[k], 16 * turn_)
                split_weights(pool, turn, steps, raw, into, k, KT, split_ready)

            for k in range(NRING):
                if k == 2:
                    pool.wait_ge(sum_ready, FIRST)
                split(1, k, ws)
            pool.wait_ge(t_ready, 2 * KT)

            for kind in range(2):
                def unit(i, k):
                    modulation(2 * kind + i, 2 * k)
                    modulation(2 * kind + i, 2 * k + 1)
                    last, _ = number(kind, i, k, len(QKG[kind]) - 1)
                    pool.wait_ge(group_ready, last + 1)
                    split(2 * kind + i + 2, k, ws)
                steps.loop(2, 4, lambda i: [unit(i, k) for k in range(4)])
            pool.wait_ge(qk_lo, G_V)
            for kt in range(KT):
                modulation(4, kt)
            pool.wait_ge(sum_ready, FIRST + 4)
            for k in range(NRING):
                split(6, k, ws_v)
            for kt in range(KT):
                modulation(5, kt)

        @block.tensor
        def _(pe):
            def statistics(s):
                w = SEG[s][1]
                wait(pe, std_ready, s)
                for kt in range(KT):
                    pe.wait_ge(sq_ready, KT * s + kt + 1)
                    pe.matmul(pstat[:, 0:w], c["ones"][:], SEG[s][3][:, kt % 2, 0:w], start=kt == 0,
                              stop=kt == KT - 1).then_inc(sq_used, 1)

            def partition_sums(sums, col0):
                for n in range(KT):
                    last = pe.matmul(pada[:, col0 + n:col0 + n + 1], sums[:, n * P:(n + 1) * P], c["ones"][:, 0:1],
                                     start=True, stop=True)
                return last

            def late_sums(j):
                pe.wait_ge(ada_dve, FIRST * KT + KT * (j + 1))
                pe.wait_ge(ada_pool, KT * (j + 1))
                pe.wait_ge(mod_out, 1 + j)
                partition_sums(sums_of(j)[:, 0], 0)
                partition_sums(sums_of(j)[:, 1], KT).then_inc(sum_ready, 1)

            pe.wait_ge(const_ready, 1)
            for s in range(2):
                statistics(s)
            for s in range(FIRST):
                pe.wait_ge(ada_dve, KT * (s + 1))
                partition_sums(first_sum[:, s], KT * s).then_inc(sum_ready, 1)

            def unit(i, k, kind):
                u = kind * KT + 4 * i + k
                wait(pe, split_ready, u + 1)
                first = first_of_all(kind, i, k)
                for n, g in enumerate(QKG[kind]):
                    G, at = number(kind, i, k, n)
                    b = at % 4
                    wait(pe, bank_free[b], (G_K if kind else 0) // 4 + len(QKG[kind]) * i + at // 4)
                    lo, hi = cols(g)
                    if kind == 1 and opens(i) and k == 0 and n == 0:
                        pe.wait_ge(h_ready, 3 * KT)
                    if first:
                        for kt in range(KT):
                            pe.wait_ge(h_ready, KT * (g - 1) + kt + 1)
                            last = product(pe, bank[b][:, 0:hi - lo], 1,
                                           W(lambda p, _: ws[:, k, p, kt], kt == 0, kt == KT - 1),
                                           lambda p, _: h[:, p, kt, lo:hi])
                    else:
                        last = product(pe, bank[b][:, 0:hi - lo], KT, W(lambda p, kt: ws[:, k, p, kt]),
                                       lambda p, kt: h[:, p, kt, lo:hi])
                    last.then_inc(group_ready, 1)
                    if k == 1 and n == 0 and not (kind == 0 and opens(i)):
                        late_sums(2 * kind + i - 1)
                if kind == 0 and opens(i) and k == 3:
                    statistics(2)

            for kind in range(2):
                loop(pe, 2, lambda i: [unit(i, k, kind) for k in range(4)])
            for half in range(2):
                pe.wait_ge(split_ready, 2 * KT + 4 * half + 4)
                wv = ws_v if half else ws
                for n in range(VT):
                    g = G_V + VT * half + n
                    pe.wait_ge(bank_free[g % 4], g // 4)
                    last = product(pe, bank[g % 4][:], KT, W(lambda p, kt: h[:, p, kt, n * P:(n + 1) * P]),
                                   lambda p, kt: wv[:, 0:4, p, kt])
                    last.then_inc(group_ready, 1)
                    if n == 1:
                        late_sums(3 + half)
                    if half == 1 and n == KT:
                        late_sums(5)

        @block.scalar
        def _(act):
            act.wait_ge(vecs_in, 16)
            act.activation(sx[:, 0], c["vecs"][:, V_C:V_C + KT], ACT.Silu).then_inc(silu_ready, 1)
            act.activation(sx[:, 1], c["vecs"][:, V_CCTX:V_CCTX + KT], ACT.Silu).then_inc(silu_ready, 1)
            act.wait_ge(dve_step, 4)
            act.activation(lams[:, 2:4], lams[:, 0:2], ACT.Exp).then_inc(lam_exp, 1)
            act.wait_ge(const_ready, 2)

            def squares(s):
                x, w, _, sq_, _, _ = SEG[s]
                act.wait_ge(x_in[s], 16)
                for kt in range(KT):
                    wait(act, sq_used, KT * s + kt - 1)
                    act.activation(sq_[:, kt % 2, 0:w], x[:, kt], ACT.Square).then_inc(sq_ready, 1)

            def std(s):
                act.wait_ge(sq_used, KT * (s + 1))
                wait(act, y_ready, KT * s)
                act.activation(SEG[s][5][:, 0:SEG[s][1]], pstat[:, 0:SEG[s][1]], ACT.Sqrt,
                               bias=c["eps"][:]).then_inc(std_ready, 1)

            def modulate(s):
                x, w, col0, _, t_, _ = SEG[s]
                scale = c["A"][:, 4 if s == 2 else 0]
                shift = c["modc"] if s == 2 else c["mod"]

                def full(kt):
                    act.wait_ge(y_ready, KT * s + kt + 1)
                    wait(act, h_ready, KT * s + kt - 1)
                    act.activation(t_[:, kt % 2, 0:w], x[:, kt], ACT.Identity, bias=shift[:, kt:kt + 1],
                                   scale=scale[:, kt:kt + 1]).then_inc(t_ready, 1)
                full(0)
                for kt in range(KT):
                    if kt + 1 < KT:
                        full(kt + 1)
                    act.wait_ge(t_ready, KT * s + kt + 1)
                    act.activation(h[:, 0, kt, col0:col0 + w], t_[:, kt % 2, 0:w], ACT.Copy).then_inc(hi_ready, 1)

            def modulation_product(j, kt):
                act.wait_ge(ada_full[2 + kt % 2], 16 * (FIRST * 2 + 4 * j + kt // 2 + 1))
                act.activation(ada[:, 2 + kt % 2], ada[:, 2 + kt % 2], ACT.Copy,
                               scale=sx[:, 1 if j == 0 else 0, kt:kt + 1]).then_inc(ada_scaled, 1)

            for s in range(2):
                squares(s)
                std(s)
            act.wait_ge(sum_ready, FIRST)
            act.activation(c["mod"][:, 0:FIRST * KT], pada[:, 0:FIRST * KT], ACT.Copy, scale=float(D)).then_inc(mod_out, 1)
            act.wait_ge(mods_ready, 1)
            for s in range(2):
                modulate(s)
            act.wait_ge(h_ready, 2 * KT)

            def write(kind, i, k, n):
                G, at = number(kind, i, k, n)
                lo, hi = cols(QKG[kind][n])
                wait(act, qk_lo, G + 1)
                dst = kT[4 * i + k][:, :, lo:hi] if kind else qT[4 * i + k][:, :, lo - C:hi - C]
                act.dma_start(dst, st[:, at % 2, :, 0:hi - lo].bitcast(F32)).then_inc(st_out[at % 2], 16)

            def modulation_out(j):
                act.wait_ge(sum_ready, FIRST + j + 1)
                dst = c["modc"][:] if j == 0 else c["mod"][:, 2 * KT * j:2 * KT * (j + 1)]
                act.activation(dst, pada[:, 0:2 * KT], ACT.Copy, scale=float(D)).then_inc(mod_out, 1)

            def unit(i, k, kind):
                ng = len(QKG[kind])
                for n, g in enumerate(QKG[kind]):
                    G, at = number(kind, i, k, n)
                    lo, hi = cols(g)
                    w = hi - lo
                    wait(act, group_ready, G + 1)
                    wait(act, rope_done, G - 1)
                    act.activation(sq[:, at % 2, 0:w], bank[at % 4][:, 0:w], ACT.Copy,
                                   scale=1.0 if kind else DH ** -0.5).then_inc(bank_free[at % 4], 1)
                    prev = before(kind, i, k, n)
                    if prev:
                        write(*prev)
                    wait(act, rope_done, G + 1)
                    wait(act, st_out[at % 2], 16 * ((G_K if kind else 0) // 2 + 2 * ng * i + at // 2))
                    act.activation(st[:, at % 2, 0, 0:w], t[:, at % 2, 0:w], ACT.Copy).then_inc(qk_hi, 1)
                    if g > 0:
                        modulation_product(2 * kind + i, 2 * k + g - 1)
                if k == 1 and not (kind == 0 and opens(i)):
                    modulation_out(2 * kind + i - 1)
                if kind == 0:
                    if opens(i) and k == 2:
                        squares(2)
                    if opens(i) and k == 3:
                        std(2)
                    if not opens(i) and k == 2:
                        act.wait_ge(mods_ready, 2)
                        modulate(2)

            for kind in range(2):
                loop(act, 2, lambda i: [unit(i, k, kind) for k in range(4)])
            write(1, 1, 3, 2)
            for half in range(2):
                for n in range(VT):
                    m = VT * half + n
                    g = G_V + m
                    act.wait_ge(group_ready, g + 1)
                    wait(act, v_out[m % 2], 16 * (m // 2))
                    act.activation(t[:, m % 2], bank[g % 4][:], ACT.Copy).then_inc(bank_free[g % 4], 1)
                    act.wait_ge(bank_free[g % 4], g // 4 + 1)
                    act.dma_start(vS[n][:, half * HALF:(half + 1) * HALF], t[:, m % 2]).then_inc(v_out[m % 2], 16)
                    if n < KT:
                        modulation_product(4 + half, n)
                    if n == 1:
                        modulation_out(3 + half)
                    if half == 1 and n == KT:
                        modulation_out(5)
            for s in range(2):
                act.wait_ge(st_out[s], 16 * (2 * KT + 3 * KT) // 2)
                act.wait_ge(v_out[s], 16 * VT)

        @block.vector
        def _(dve):
            steps = Steps(dve, dve_step)
            vec = c["vecs"]
            swap = [(p + 16) % 32 for p in range(32)]
            dve.memset(c["ones"][:], 1.0 / D).then_inc(const_ready, 1)
            dve.memset(c["eps"][:], EPS).then_inc(const_ready, 1)
            dve.wait_ge(lam_in, 16)
            for j in range(2):
                steps.did(dve.tensor_tensor(lamv[:, 2 * j], lamv[:, 2 * j], lamv[:, 2 * j + 1], ALU.mult))
                steps.sync()
                steps.did(dve.tensor_reduce(lams[:, j:j + 1], lamv[:, 2 * j], AX.X, ALU.add))

            def first_modulation(n):
                dve.wait_ge(ada_full[n % 4], 16 * (n // 4 + 1))
                out_, w = first_sum[:, n // KT], ada[:, n % 4]
                if n % KT == 0:
                    dve.tensor_scalar(out_, w, sx[:, 0, 0:1], None, ALU.mult).then_inc(ada_dve, 1)
                else:
                    dve.wait_ge(ada_dve, n)
                    dve.scalar_tensor_tensor(out=out_, in0=w, scalar=sx[:, 0, n % KT:n % KT + 1], in1=out_,
                                             op0=ALU.mult, op1=ALU.add).then_inc(ada_dve, 1)

            def modulation(j, kt):
                dve.wait_ge(ada_full[kt % 2], 16 * (FIRST * 2 + 4 * j + kt // 2 + 1))
                dve.wait_ge(ada_dve, FIRST * KT + KT * j + kt)
                out_, w = sums_of(j)[:, 0], ada[:, kt % 2]
                stream = 1 if j == 0 else 0
                if kt == 0:
                    wait_sums_free(dve, j)
                    dve.tensor_scalar(out_, w, sx[:, stream, 0:1], None, ALU.mult).then_inc(ada_dve, 1)
                else:
                    dve.scalar_tensor_tensor(out=out_, in0=w, scalar=sx[:, stream, kt:kt + 1], in1=out_,
                                             op0=ALU.mult, op1=ALU.add).then_inc(ada_dve, 1)

            def inverse_rms(s):
                r = SEG[s][5][:, 0:SEG[s][1]]
                dve.wait_ge(std_ready, s + 1)
                steps.did(dve.reciprocal(r, r))
                steps.sync()

            def normalize(s, kt):
                x, w, _, _, _, r = SEG[s]
                dve.tensor_tensor(x[:, kt], x[:, kt], r[:, 0:w], ALU.mult).then_inc(y_ready, 1)

            def low_part(s, kt):
                _, w, col0, _, t_, _ = SEG[s]
                dve.wait_ge(hi_ready, KT * s + kt + 1)
                dve.tensor_tensor(h[:, 1, kt, col0:col0 + w], t_[:, kt % 2, 0:w],
                                  h[:, 0, kt, col0:col0 + w].bitcast(F32), ALU.subtract).then_inc(h_ready, 1)

            def modulation_vectors(shift_scale, A):
                steps.did(dve.tensor_tensor(shift_scale, shift_scale, vec[:, V_BADA:V_BADA + FIRST * KT], ALU.add))
                steps.sync()
                dve.scalar_tensor_tensor(out=A, in0=shift_scale[:, KT:2 * KT], scalar=1.0,
                                         in1=vec[:, V_MIXPRE:V_MIXPRE + KT], op0=ALU.add,
                                         op1=ALU.mult).then_inc(mods_ready, 1)

            dve.wait_ge(silu_ready, 2)
            for n in range(FIRST * KT):
                first_modulation(n)
                if n == 3:
                    inverse_rms(0)
                    for kt in range(KT):
                        normalize(0, kt)
            inverse_rms(1)
            dve.wait_ge(mod_out, 1)
            modulation_vectors(c["mod"][:, 0:FIRST * KT], c["A"][:, 0])
            for kt in range(KT):
                normalize(1, kt)
                low_part(0, kt)
            for kt in range(KT):
                low_part(1, kt)
            dve.wait_ge(lam_exp, 1)
            steps.did(dve.tensor_tensor(lams[:, 0:1], lams[:, 3:4], lams[:, 2:3], ALU.subtract))
            steps.sync()
            steps.did(dve.tensor_scalar(c["neglam"][:], lams[:, 0:1], -LAM_INIT, None, ALU.add))
            steps.did(dve.tensor_scalar(c["gsub"][:], vec[:, V_SUBLN:V_SUBLN + 1], 1.0 - LAM_INIT, None, ALU.mult))
            dve.wait_ge(trig_in, 16)
            dve.wait_ge(t_ready, 2 * KT)

            def unit(i, k, kind):
                for n, g in enumerate(QKG[kind]):
                    G, at = number(kind, i, k, n)
                    lo, hi = cols(g)
                    w = hi - lo
                    wait(dve, qk_lo, G - 1)
                    src, dst = sq[:, at % 2, 0:w], t[:, at % 2, 0:w]
                    wait(dve, bank_free[at % 4], (G_K if kind else 0) // 4 + len(QKG[kind]) * i + at // 4 + 1)
                    if g > 0:
                        cos, sin = (trig[:, m, lo - C:hi - C] for m in range(2))
                        partner, cp = rstd[:, 0:w], cosp[:, 0:w]
                        wait(dve, rope_done, G)
                        steps.did(dve.stream_shuffle(partner, src, swap))
                        steps.did(dve.tensor_tensor(cp, src, cos, ALU.mult))
                        steps.sync()
                        steps.did(dve.tensor_tensor(partner, partner, sin, ALU.mult))
                        steps.sync()
                        dve.tensor_tensor(dst, cp, partner, ALU.add).then_inc(rope_done, 1)
                        modulation(2 * kind + i, 2 * k + g - 1)
                    else:
                        dve.tensor_copy(dst, src).then_inc(rope_done, 1)
                    wait(dve, qk_hi, G + 1)
                    dve.tensor_tensor(st[:, at % 2, 1, 0:w], dst, st[:, at % 2, 0, 0:w].bitcast(F32),
                                      ALU.subtract).then_inc(qk_lo, 1)
                if kind == 0:
                    if not opens(i) and k == 0:
                        inverse_rms(2)
                    if not opens(i) and k in (0, 1):
                        for kt in range(4 * k, 4 * k + 4):
                            normalize(2, kt)
                    if not opens(i) and k == 1:
                        dve.wait_ge(mod_out, 2)
                        modulation_vectors(c["modc"][:], c["A"][:, 4])
                    if not opens(i) and k == 2:
                        for kt in range(KT):
                            low_part(2, kt)

            for kind in range(2):
                for i in range(2):
                    for k in range(4):
                        unit(i, k, kind)
            dve.wait_ge(rope_done, G_V)
            for j in (4, 5):
                for kt in range(KT):
                    modulation(j, kt)

            dve.wait_ge(mod_out, 7)
            late_mod = c["mod"][:, FIRST * KT:NADA]
            steps.did(dve.tensor_tensor(late_mod, late_mod, vec[:, V_BADA + FIRST * KT:V_BADA + NADA], ALU.add))
            steps.sync()
            for n in range(4):
                layer, ffn = divmod(n, 2)
                m0 = layer * 6 * KT
                sc, gate = (SC_F, G_F) if ffn else (SC_M, G_M)
                pre = (V_FFNPRE if ffn else V_MIXPRE) + layer * KT
                post = (V_FFNPOST if ffn else V_MIXPOST) + layer * KT
                if n:
                    steps.did(dve.scalar_tensor_tensor(
                        out=c["A"][:, n], in0=c["mod"][:, m0 + sc * KT:m0 + (sc + 1) * KT], scalar=1.0,
                        in1=vec[:, pre:pre + KT], op0=ALU.add, op1=ALU.mult))
                steps.did(dve.tensor_tensor(c["G"][:, n], c["mod"][:, m0 + gate * KT:m0 + (gate + 1) * KT],
                                            vec[:, post:post + KT], ALU.mult))


def block2(nc, a, c, qT, kT, vS, oT):
    with ExitStack() as ctx:
        def sb(name, shape, dt=F32):
            return ctx.enter_context(nc.sbuf_tensor(name, shape, dt))

        def sem(name):
            return ctx.enter_context(nc.semaphore(name))

        QT = T // P
        NT = NPAIR * QT
        BODY = 2 * QT
        KEYS = TA // P
        LAST = NT // BODY - 1

        q = sb("q_stack", [P, 2, 2, T], F32R)
        kd = sb("k_double", [P, 2, 2, 2, TA], F32R)
        v = sb("v_pair", [P, 2, KEYS, P])
        prob = sb("prob", [P, 2, 2, TA])
        w = sb("w_diff", [P, 2, TA])
        wT = sb("w_diffT", [P, 2, KEYS, P])
        negmax = sb("negmax", [P, 2, 2])
        sums = sb("sums", [P, 2, 2])
        rsum = sb("rsum", [P, 2, 2])
        junk = sb("junk", [P, P])
        ss = sb("ss", [P, 2])
        ms = sb("ms", [P, 2])
        half = sb("minus_half", [P, 1])
        rstd = sb("rstd2", [P, 2])
        on = sb("o_norm", [P, 2, P])
        osb = sb("o_copy", [P, 4, P])
        of = sb("o_full", [P, 2, 2 * P])
        ost = sb("o_out", [P, 2, 2, 2 * P], F32R)
        ident = sb("ident", [P, P])

        s_ps = [ctx.enter_context(nc.psum_tensor(f"scores{e}", [P, 3 * 512], F32)) for e in range(2)]
        t_ps = ctx.enter_context(nc.psum_tensor("transposed", [P, 512], F32))
        o_ps = ctx.enter_context(nc.psum_tensor("o_ps", [P, 512], F32))

        ident_in, half_set = sem("ident_in"), sem("half_set")
        pair_in = [sem(f"pair_in{s}") for s in range(2)]
        s_ready, max_ready, exp_done = sem("s_ready"), sem("max_ready"), sem("exp_done")
        rsum_ready, p1_scaled, w_ready = sem("rsum_ready"), sem("p1_scaled"), sem("w_ready")
        t_ready, wT_ready, o_ready = sem("t_ready"), sem("wT_ready"), sem("o_ready")
        o_copied = sem("o_copied")
        ss_ready, rstd_ready, on_ready = sem("ss_ready"), sem("rstd_ready"), sem("on_ready")
        oT_ready, of_ready, ost_ready = sem("oT_ready"), sem("of_ready"), sem("ost_ready")
        o_out = [sem(f"o_out{s}") for s in range(2)]
        pool_step, dve_step, turn = sem("b2_pool_step"), sem("b2_dve_step"), sem("b2_turn")

        BANK = 512
        CUTS = [0, BANK, 2 * BANK, TA]
        CHUNKS = [(0, 4), (4, 8), (8, KEYS)]

        class Tile:

            def __init__(self, i, at, first=False, last=False):
                self.exists = not (first and at < 0) and not (last and at >= BODY)
                self.n = BODY * i + at
                self.s = at % 2
                self.q = at % QT
                self.pair = BODY // QT * i + at // QT
                self.buf = at // QT % 2
                self.fill = i + at // BODY
                self.duo = BODY // 2 * i + at // 2
                self.duo_slot = at // 2 % 2
                self.duo_fill = BODY // 4 * i + at // 4
                self.s4 = at % 4

        def steps_of(eng, step):
            for at in range(-2, BODY):
                step(lambda k: Tile(0, at + k, first=True))
            with eng.Fori(1, LAST) as i:
                for at in range(BODY):
                    step(lambda k: Tile(i, at + k))
            for at in range(BODY + 5):
                step(lambda k: Tile(LAST, at + k, last=True))

        block = ctx.enter_context(nc.Block())

        @block.sync
        def _(sp):
            def load_pair(p, s):
                for e in range(2):
                    rows = slice(e * DH, (e + 1) * DH)
                    for part in range(2):
                        sp.dma_start(q[part * DH:(part + 1) * DH, s, e].bitcast(F32), qT[p][rows, part]).then_inc(pair_in[s], 16)
                        for copy in range(2):
                            sp.dma_start(kd[copy * DH:(copy + 1) * DH, s, e, part].bitcast(F32),
                                         kT[p][rows, part]).then_inc(pair_in[s], 16)
                sp.dma_start(v[:, s], vS.rearrange("n p (h e) -> h p n e", h=NPAIR)[p]).then_inc(pair_in[s], 16)

            sp.dma_start(ident[:], a["ident"]).then_inc(ident_in, 16)
            load_pair(0, 0)
            load_pair(1, 1)

            def tile_done(o):
                if o.q == QT - 1 and not (isinstance(o.pair, int) and o.pair + 2 >= NPAIR) and not o.last:
                    sp.wait_ge(o_ready, o.n + 1)
                    load_pair(o.pair + 2, o.buf)
                if o.s == 1:
                    sp.wait_ge(ost_ready, o.duo + 1)
                    sp.dma_start(oT[o.pair][:, :, (o.q - 1) * P:(o.q + 1) * P],
                                 ost[:, o.duo_slot].bitcast(F32)).then_inc(o_out[o.duo_slot], 16)

            def body(i, last=False):
                for at in range(BODY):
                    o = Tile(i, at)
                    o.last = last
                    tile_done(o)
            body(0)
            with sp.Fori(1, LAST) as i:
                body(i)
            body(LAST, True)
            for s in range(2):
                sp.wait_ge(o_out[s], 16 * NT // 4)

        @block.tensor
        def _(pe):
            pe.wait_ge(ident_in, 16)

            def scores(new, e):
                if new.q == 0 and e == 0:
                    wait(pe, pair_in[new.buf], 16 * 13 * (new.fill + 1))
                wait(pe, exp_done, 2 * (new.n - 1) + e + 1)
                for lo, hi in zip(CUTS, CUTS[1:]):
                    for part in range(2):
                        last = pe.matmul(s_ps[e][:, lo:hi], q[:, new.buf, e, new.q * P:(new.q + 1) * P],
                                         kd[:, new.buf, e, part, lo:hi], start=part == 0, stop=part == 1)
                last.then_inc(s_ready, 1)

            def transposes(tr, ch):
                k0, k1 = CHUNKS[ch]
                wait(pe, wT_ready, 3 * tr.n + ch)
                for kt in range(k0, k1):
                    last = pe.transpose(t_ps[:, (kt - k0) * P:(kt - k0 + 1) * P],
                                        w[:, tr.s, kt * P:(kt + 1) * P], ident[:])
                last.then_inc(t_ready, 1)

            def step(tile):
                new, tr, pv, ot = tile(2), tile(0), tile(-1), tile(-4)
                if tr.exists:
                    wait(pe, w_ready, tr.n + 1)
                    wait(pe, of_ready, tr.n - 4)
                    transposes(tr, 0)
                if new.exists:
                    scores(new, 0)
                if tr.exists:
                    transposes(tr, 1)
                if new.exists:
                    scores(new, 1)
                if ot.exists:
                    wait(pe, on_ready, ot.n + 1)
                    wait(pe, wT_ready, 3 * tr.n + 2 if tr.exists else 3 * NT)
                    wait(pe, of_ready, ot.n)
                    pe.transpose(t_ps[:, 3 * P:4 * P], on[:, ot.s], ident[:]).then_inc(oT_ready, 1)
                if tr.exists:
                    transposes(tr, 2)
                if pv.exists:
                    wait(pe, wT_ready, 3 * pv.n + 3)
                    wait(pe, o_copied, pv.n)
                    for kt in range(KEYS):
                        last = pe.matmul(o_ps[:, 0:P], wT[:, pv.s, kt], v[:, pv.buf, kt],
                                         start=kt == 0, stop=kt == KEYS - 1)
                    last.then_inc(o_ready, 1)

            steps_of(pe, step)

        @block.scalar
        def _(act):
            def copy_wT(tr, ch):
                k0, k1 = CHUNKS[ch]
                wait(act, t_ready, 3 * tr.n + ch + 1)
                act.activation(wT[:, tr.s, k0:k1], t_ps[:, 0:(k1 - k0) * P], ACT.Copy).then_inc(wT_ready, 1)

            def exponentials(new, e):
                wait(act, max_ready, 2 * new.n + e + 1)
                wait(act, w_ready, new.n - 1)
                act.activation(prob[:, new.s, e], s_ps[e][:, 0:TA], ACT.Exp, bias=negmax[:, new.s, e:e + 1],
                               accum_out=sums[:, new.s, e:e + 1]).then_inc(exp_done, 1)

            def step(tile):
                new, tr, pv, ot = tile(2), tile(0), tile(-1), tile(-4)
                if tr.exists:
                    wait(act, o_ready, tr.n - 1)
                    copy_wT(tr, 0)
                if new.exists:
                    exponentials(new, 0)
                if tr.exists:
                    copy_wT(tr, 1)
                if new.exists:
                    exponentials(new, 1)
                if tr.exists:
                    copy_wT(tr, 2)
                if ot.exists:
                    wait(act, oT_ready, ot.n + 1)
                    wait(act, ost_ready, ot.duo - 1)
                    act.activation(of[:, ot.duo_slot, ot.s * P:(ot.s + 1) * P], t_ps[:, 3 * P:4 * P], ACT.Copy,
                                   scale=c["gsub"][:]).then_inc(of_ready, 1)
                if pv.exists:
                    wait(act, o_ready, pv.n + 1)
                    wait(act, on_ready, pv.n - 3)
                    act.activation(osb[:, pv.s4], o_ps[:, 0:P], ACT.Copy).then_inc(o_copied, 1)

            steps_of(act, step)

        @block.vector
        def _(dve):
            dve.memset(half[:], -0.5).then_inc(half_set, 1)

            def step(tile):
                new, nx, sq_t, on_t, ot = tile(2), tile(1), tile(-2), tile(-3), tile(-5)
                if nx.exists:
                    wait(dve, exp_done, 2 * nx.n + 2)
                    wait(dve, p1_scaled, nx.n - 1)
                    dve.reciprocal(rsum[:, nx.s], sums[:, nx.s]).then_inc(rsum_ready, 1)
                if new.exists:
                    for e in range(2):
                        wait(dve, s_ready, 2 * new.n + e + 1)
                        dve.tensor_reduce(negmax[:, new.s, e:e + 1], s_ps[e][:, 0:TA], AX.X,
                                          ALU.max, negate=True).then_inc(max_ready, 1)
                if sq_t.exists:
                    wait(dve, o_copied, sq_t.n + 1)
                    wait(dve, rstd_ready, sq_t.n - 1)
                    wait(dve, ss_ready, sq_t.n)
                    o = osb[:, sq_t.s4]
                    dve.tensor_tensor_reduce(junk[:], o, o, 1.0, 0.0, ALU.mult, ALU.add,
                                             ss[:, sq_t.s:sq_t.s + 1]).then_inc(ss_ready, 1)
                if nx.exists:
                    wait(dve, p1_scaled, nx.n + 1)
                    wait(dve, t_ready, 3 * (nx.n - 2) + 3)
                    wait(dve, rsum_ready, nx.n + 1)
                    dve.scalar_tensor_tensor(out=w[:, nx.s], in0=prob[:, nx.s, 0], scalar=rsum[:, nx.s, 0:1],
                                             in1=prob[:, nx.s, 1], op0=ALU.mult, op1=ALU.add).then_inc(w_ready, 1)
                if on_t.exists:
                    wait(dve, rstd_ready, on_t.n + 1)
                    wait(dve, oT_ready, on_t.n - 1)
                    dve.tensor_scalar(on[:, on_t.s], osb[:, on_t.s4], rstd[:, on_t.s:on_t.s + 1], None,
                                      ALU.mult).then_inc(on_ready, 1)
                if ot.exists and ot.s == 1:
                    full, part = of[:, ot.duo_slot], ost[:, ot.duo_slot]
                    wait(dve, of_ready, ot.n + 1)
                    wait(dve, o_out[ot.duo_slot], 16 * ot.duo_fill)
                    dve.tensor_copy(part[:, 0], full).then_inc(dve_step, 1)
                    wait(dve, dve_step, ot.duo + 1)
                    dve.tensor_tensor(part[:, 1], full, part[:, 0].bitcast(F32), ALU.subtract).then_inc(ost_ready, 1)

            steps_of(dve, step)

        @block.gpsimd
        def _(pool):
            pool.wait_ge(half_set, 1)

            def step(tile):
                nx, pv = tile(1), tile(-2)
                if nx.exists:
                    wait(pool, rsum_ready, nx.n + 1)
                    pool.sem_inc(turn, 1)
                    pool.tensor_scalar(prob[:, nx.s, 1], prob[:, nx.s, 1], rsum[:, nx.s, 1:2], c["neglam"][:],
                                       ALU.mult, ALU.mult).then_inc(p1_scaled, 1)
                if pv.exists:
                    wait(pool, ss_ready, pv.n + 1)
                    wait(pool, on_ready, pv.n - 1)
                    pool.sem_inc(turn, 1)
                    pool.tensor_scalar(ms[:, pv.s:pv.s + 1], ss[:, pv.s:pv.s + 1], 1.0 / P, EPS,
                                       ALU.mult, ALU.add).then_inc(pool_step, 1)
                    wait(pool, pool_step, pv.n + 1)
                    pool.tensor_tensor(rstd[:, pv.s:pv.s + 1], ms[:, pv.s:pv.s + 1], half[:],
                                       ALU.pow).then_inc(rstd_ready, 1)

            steps_of(pool, step)


def block3(nc, a, c, oT, xS, out):
    with ExitStack() as ctx:
        def sb(name, shape, dt=F32):
            return ctx.enter_context(nc.sbuf_tensor(name, shape, dt))

        def sem(name):
            return ctx.enter_context(nc.semaphore(name))

        CH = HALF // P

        base = -(-nc.sbuf_base // 32) * 32
        ctx.enter_context(nc.sbuf_tensor("hid_region", [P, HT * 2 * HALF + 8], F32))

        def at(name, shape, kb, dt=F32):
            return nc.alloc_sbuf_tensor_at(name, shape, dt, offset=base + kb * 1024)

        hid = at("hid", [P, HT, 2, HALF], 0, F32R)
        u = at("u", [P, KT, HALF], 32)
        v = at("v", [P, CH, D], 48)
        rows = at("rows", [P, 3, D], 64)
        bsp = at("bsp", [P, KT, P], 76)
        wsp = at("wsp", [P, KT, P], 80)

        h = sb("h", [P, 2, KT, HALF], F32R)
        ws = sb("wsplit3", [P, NRING, 2, KT, P], F32R)
        raw = sb("wraw3", [P, NRING, KT, P])
        y = sb("y", [P, KT, HALF])
        sq = sb("sq3", [P, 2, HALF])
        sil = sb("silu3", [P, 2, HALF])
        t = sb("t3", [P, 2, HALF])
        acc = sb("acc3", [P, HALF])
        rstd = sb("rstd3", [P, HALF])
        xr = sb("x_ring", [P, 2, HALF])
        st6 = sb("bn6", [P, CH, 2, 6])
        mv = sb("mv", [P, CH, 2])
        rln = sb("rln", [P, CH])
        bank = [ctx.enter_context(nc.psum_tensor(f"acc3_{b}", [P, HALF], F32)) for b in range(4)]
        pstat = ctx.enter_context(nc.psum_tensor("stat3", [P, HALF], F32))

        o_in, rows_in = [sem("o_in0"), sem("o_in1")], sem("rows_in")
        raw_full = [sem(f"b3_raw_full{s}") for s in range(NRING)]
        split_ready = sem("b3_split_ready")
        unit_done = sem("unit_done")
        mix_ready = sem("mix_ready")
        bank_free = [sem(f"b3_bank_free{b}") for b in range(4)]
        silu_ready, hid_ready = sem("silu_ready3"), sem("hid_ready")
        sq_ready, sq_used = sem("b3_sq_ready"), sem("b3_sq_used")
        stat_ready, std_ready = sem("b3_stat_ready"), sem("b3_std_ready")
        x_in = [sem(f"b3_x_in{s}") for s in range(2)]
        x_new, x_out = sem("x_new"), sem("x_out")
        t_ready, hf_ready, h_ready = sem("b3_t_ready"), sem("b3_hf_ready"), sem("b3_h_ready")
        u_ready, v_ready, var_std, ln_ready = sem("u_ready"), sem("v_ready"), sem("var_std"), sem("ln_ready")
        var_ready = sem("var_ready")
        dve_step, pool_step, turn = sem("b3_dve_step"), sem("b3_pool_step"), sem("b3_turn")

        stages = []
        U = G = H = S = 0
        for kind, layer in (("O", 0), ("F", 0), ("C", 1), ("F", 1)):
            for half in range(2):
                units = {"O": (0, KT), "F": (2 * HT, 3 * KT), "C": (2 * KT, KT)}[kind]
                groups = {"O": (0, KT), "F": (2 * HT, KT), "C": (3 * KT, KT)}[kind]
                s = dict(kind=kind, layer=layer, half=half, j=len(stages), U=U, G=G, H=H, S=S,
                         vec=2 * layer + (kind == "F"),
                         U_out=U + units[0], G_out=G + groups[0],
                         final=kind == "F" and layer == 1)
                U, G = U + sum(units), G + sum(groups)
                H += {"O": 0, "F": HT, "C": KT}[kind]
                S += HT if kind == "F" else 0
                s.update(U_end=U, H_end=H)
                stages.append(s)
        n_norm = {}
        for s in stages:
            n_norm["post", s["j"]] = len(n_norm)
            if not s["final"]:
                n_norm["pre", s["j"]] = len(n_norm)

        def prev(s):
            return stages[s["j"] - 1] if s["j"] else None

        def y_done(s, i4, f):
            per = 3 if s["kind"] == "F" else 1
            return s["U_out"] + per * (4 * i4 + f + 1)

        block = ctx.enter_context(nc.Block())

        @block.sync
        def _(sp):
            for half in range(2):
                for k in range(KT):
                    sp.dma_start(hid[:, half * KT + k].bitcast(F32), oT[k][:, :, half * HALF:(half + 1) * HALF]
                                 ).then_inc(o_in[half], 16)

            def load(u, slot, n_kt, src):
                wait(sp, split_ready, u - NRING + 1)
                sp.dma_start(raw[:, slot, 0:n_kt], src).then_inc(raw_full[slot], 16)

            def plain(name, u0, n):
                def body(i):
                    for k in range(4):
                        load(u0 + 4 * i + k, k, KT, a[name][4 * i + k].rearrange("p (k c) -> p k c", k=KT))
                loop(sp, n, body)

            for s in stages:
                if s["kind"] == "O":
                    plain("w_attn_out", s["U"], 2)
                elif s["kind"] == "C":
                    plain("w_uv", s["U"], 4)
                    plain("w_cmlp_out", s["U_out"], 2)
                else:
                    plain(f"w_ffn_in{s['layer']}", s["U"], HT // 2)

                    def body(i):
                        for f in range(4):
                            w = a[f"w_ffn_out{s['layer']}"][4 * i + f].rearrange("p (k c) -> p k c", k=HT)
                            for m, (k0, k1) in enumerate(GROUPS_KT):
                                n = 3 * f + m
                                load(s["U_out"] + 12 * i + n, n % NRING, k1 - k0, w[:, k0:k1])
                    loop(sp, 2, body)

        @block.gpsimd
        def _(pool):
            steps = Steps(pool, pool_step)

            def unit(u0, i4, k, n_kt, done=None):
                pool.wait_ge(raw_full[k % NRING], 16 * (u0 // NRING + i4 + k // NRING + 1))
                wait(pool, unit_done, u0 + 4 * i4 + k - NRING + 1 if done is None else done)
                split_weights(pool, turn, steps, raw, ws, k % NRING, n_kt, split_ready)

            for s in stages:
                if s["kind"] == "O":
                    steps.loop(2, 4, lambda i: [unit(s["U"], i, k, KT) for k in range(4)])
                elif s["kind"] == "C":
                    for i in range(3):
                        for k in range(4):
                            unit(s["U"], i, k, KT, s["U"] + 4 * i if i else None)
                    steps.loop(3, 4, lambda i: [unit(s["U"] + 12, i, k, KT) for k in range(4)])
                else:
                    steps.loop(HT // 2, 4, lambda i: [unit(s["U"], i, k, KT) for k in range(4)])
                    steps.loop(2, 12, lambda i: [unit(s["U_out"], 3 * i, 3 * f + m, k1 - k0)
                                                 for f in range(4) for m, (k0, k1) in enumerate(GROUPS_KT)])

        @block.tensor
        def _(pe):
            def bank_wait(g0, i4, at):
                wait(pe, bank_free[at % 4], g0 // 4 + i4 + at // 4)

            def stat(which, s):
                if s is None or (which, s["j"]) not in n_norm:
                    return
                n = n_norm[which, s["j"]]
                pe.wait_ge(sq_used, KT * (n + 1))
                wait(pe, std_ready, n)
                pe.matmul(pstat[:], c["ones"][:], acc[:], start=True, stop=True).then_inc(stat_ready, 1)

            def one(u0, g0, i, k, x):
                wait(pe, split_ready, u0 + 4 * i + k + 1)
                bank_wait(g0, i, k)
                product(pe, bank[k][:], KT, W(lambda p, kt: ws[:, k, p, kt]), x).then_inc(unit_done, 1)

            for s in stages:
                if s["kind"] == "O":
                    pe.wait_ge(o_in[s["half"]], 16 * KT)
                    for n in range(KT):
                        one(s["U"], s["G"], n // 4, n % 4, lambda p, kt: hid[:, s["half"] * KT + kt, p])
                        if n == 0:
                            stat("post", prev(s))
                        if n == 2:
                            stat("pre", prev(s))
                    continue

                pe.wait_ge(h_ready, KT * (s["j"] - 1))
                if s["kind"] == "F":
                    def hidden_tile(i, m):
                        for k in (2 * m, 2 * m + 1):
                            one(s["U"], s["G"], i, k, lambda p, kt: h[:, p, kt])
                    for i in range(3):
                        for m in range(2):
                            hidden_tile(i, m)
                            if (i, m) == (0, 0):
                                stat("post", prev(s))
                            if (i, m) == (2, 0):
                                stat("pre", prev(s))
                    with pe.Fori(3, HT // 2) as i:
                        for m in range(2):
                            hidden_tile(i, m)

                    def body(i):
                        for f in range(4):
                            bank_wait(s["G_out"], i, f)
                            for m, (k0, k1) in enumerate(GROUPS_KT):
                                n = 3 * f + m
                                wait(pe, split_ready, s["U_out"] + 12 * i + n + 1)
                                pe.wait_ge(hid_ready, s["H"] + k1)
                                product(pe, bank[f][:], k1 - k0,
                                        W(lambda p, kt: ws[:, n % NRING, p, kt], m == 0, m == 2),
                                        lambda p, kt: hid[:, k0 + kt, p]).then_inc(unit_done, 1)
                    loop(pe, 2, body)
                else:
                    for half in range(2):
                        pe.wait_ge(split_ready, s["U"] + 4 * half + 4)
                        for n in range(CH):
                            bank_wait(s["G"], half, n)
                            product(pe, bank[n][:], KT, W(lambda p, kt: h[:, p, kt, n * P:(n + 1) * P]),
                                    lambda p, kt: ws[:, 0:4, p, kt]).then_inc(unit_done, 1)
                            if (half, n) == (0, 1):
                                stat("post", prev(s))
                    stat("pre", prev(s))
                    loop(pe, 2, lambda i: [one(s["U"] + KT, s["G"] + KT, i, k, lambda p, kt: h[:, p, kt])
                                           for k in range(4)])
                    pe.wait_ge(ln_ready, CH * (s["half"] + 1))
                    for g in range(KT):
                        bank_wait(s["G"] + 2 * KT, 0, g)
                        for n in range(CH):
                            last = pe.matmul(bank[g % 4][:, n * P:(n + 1) * P], v[:, n, g * P:(g + 1) * P],
                                             wsp[:, g], start=True, stop=True)
                        last.then_inc(mix_ready, 1)
                    pe.wait_ge(hid_ready, s["H_end"])
                    loop(pe, 2, lambda i: [one(s["U_out"], s["G_out"], i, k, lambda p, kt: hid[:, kt, p])
                                           for k in range(4)])
            stat("post", stages[-1])

        @block.scalar
        def _(act):
            def square(n, ft):
                wait(act, sq_used, KT * n + ft - 1)
                act.activation(sq[:, ft % 2], y[:, ft], ACT.Square).then_inc(sq_ready, 1)

            def load_x(s, ft):
                j = s["j"]
                if j >= 2 and ft == 0:
                    act.wait_ge(x_out, 16 * (j - 1))
                wait(act, x_new, KT * j + ft - 1)
                src = a["xT"] if s["kind"] == "O" else xS
                act.dma_start(xr[:, ft % 2], src[ft][:, s["half"] * HALF:(s["half"] + 1) * HALF]
                              ).then_inc(x_in[ft % 2], 16)

            def std(which, s):
                n = n_norm[which, s["j"]]
                act.wait_ge(stat_ready, n + 1)
                if which == "post":
                    wait(act, t_ready, KT * min(s["j"], len(stages) - 2))
                else:
                    act.wait_ge(x_new, KT * (s["j"] + 1))
                act.activation(rstd[:], pstat[:], ACT.Sqrt, bias=c["eps"][:]).then_inc(std_ready, 1)

            def post(s):
                std("post", s)
                for ft in range(KT):
                    act.wait_ge(x_new, KT * s["j"] + ft + 1)
                    if ft + 2 < KT:
                        load_x(s, ft + 2)
                    if not s["final"]:
                        square(n_norm["pre", s["j"]], ft)
                cols = slice(s["half"] * HALF, (s["half"] + 1) * HALF)
                dst = out if s["final"] else xS
                act.dma_start(dst[:, :, cols].rearrange("k p t -> p k t"), y[:]).then_inc(x_out, 16)

            def make_h(s):
                m = s["vec"] + 1
                shift0 = (m // 2) * 6 * KT + (SH_F if m % 2 else SH_M) * KT
                for ft in range(KT):
                    act.wait_ge(t_ready, KT * s["j"] + ft + 1)
                    act.activation(t[:, ft % 2], t[:, ft % 2], ACT.Identity,
                                   bias=c["mod"][:, shift0 + ft:shift0 + ft + 1],
                                   scale=c["A"][:, m, ft:ft + 1]).then_inc(hf_ready, 1)

            for s in stages:
                p = prev(s)
                if p:
                    load_x(p, 0)
                    load_x(p, 1)
                if s["kind"] == "O":
                    if p:
                        post(p)
                        std("pre", p)
                        make_h(p)
                elif s["kind"] == "F":
                    def silu(i, m):
                        wait(act, unit_done, s["U"] + 4 * i + 2 * m + 1)
                        wait(act, bank_free[2 * m + 1], s["G"] // 4 + i)
                        act.activation(sil[:, m], bank[2 * m][:], ACT.Silu).then_inc(silu_ready, 1)
                    silu(0, 0)
                    post(p)
                    for i, m in ((0, 1), (1, 0), (1, 1), (2, 0)):
                        silu(i, m)
                    if not p["final"]:
                        std("pre", p)
                    silu(2, 1)
                    with act.Fori(3, HT // 2) as i:
                        for m in range(2):
                            silu(i, m)
                    if not p["final"]:
                        make_h(p)
                else:
                    if s["half"] == 0:
                        act.wait_ge(unit_done, p["U_end"])
                        act.dma_start(rows[:], a["rows"]).then_inc(rows_in, 16)
                        act.dma_start(bsp[:], a["b_spatial"]).then_inc(rows_in, 16)
                        act.dma_start(wsp[:], a["w_spatialT"]).then_inc(rows_in, 16)

                    def gelu_v(half, n):
                        act.wait_ge(bank_free[n], s["G"] // 4 + half + 1)
                        x = v[:, n, half * HALF:(half + 1) * HALF]
                        act.activation(x, x, ACT.Gelu).then_inc(v_ready, 1)
                    gelu_v(0, 0)
                    gelu_v(0, 1)
                    post(p)
                    for half, n in ((0, 2), (0, 3), (1, 0), (1, 1), (1, 2), (1, 3)):
                        gelu_v(half, n)
                    std("pre", p)
                    for ft in range(KT):
                        if ft == 2:
                            act.wait_ge(var_ready, s["half"] + 1)
                            act.activation(rln[:], mv[:, :, 1], ACT.Sqrt, bias=c["eps"][:]).then_inc(var_std, 1)
                        act.wait_ge(unit_done, s["U"] + KT + ft + 1)
                        act.activation(u[:, ft], bank[ft % 4][:], ACT.Gelu,
                                       bias=c["vecs"][:, V_BU + ft:V_BU + ft + 1]).then_inc(bank_free[ft % 4], 1)
                    make_h(p)

                def squares(i):
                    for f in range(4):
                        wait(act, bank_free[f], s["G_out"] // 4 + i + 1)
                        n = n_norm["post", s["j"]]
                        wait(act, sq_used, KT * n + 4 * i + f - 1)
                        act.activation(sq[:, f % 2], y[:, bass.ds(4 * i + f, 1)], ACT.Square).then_inc(sq_ready, 1)
                for i in range(2):
                    squares(i)
            s = stages[-1]
            load_x(s, 0)
            load_x(s, 1)
            post(s)
            act.wait_ge(x_out, 16 * len(stages))

        @block.vector
        def _(dve):
            steps = Steps(dve, dve_step)

            def add_square(n, ft):
                dve.wait_ge(sq_ready, KT * n + ft + 1)
                wait(dve, sq_used, KT * n + ft)
                dve.tensor_tensor(acc[:], acc[:], sq[:, ft % 2], ALU.add).then_inc(sq_used, 1)

            def clear_acc(n):
                wait(dve, stat_ready, n)
                steps.did(dve.memset(acc[:], 0.0))
                steps.sync()

            def inverse(which, s):
                dve.wait_ge(std_ready, n_norm[which, s["j"]] + 1)
                steps.did(dve.reciprocal(rstd[:], rstd[:]))
                steps.sync()

            def post(s):
                inverse("post", s)
                n = n_norm.get(("pre", s["j"]))
                if n is not None:
                    clear_acc(n)
                for ft in range(KT):
                    steps.did(dve.tensor_tensor(y[:, ft], y[:, ft], rstd[:], ALU.mult))
                    steps.sync()
                    dve.wait_ge(x_in[ft % 2], 16 * (KT // 2 * s["j"] + ft // 2 + 1))
                    dve.scalar_tensor_tensor(out=y[:, ft], in0=y[:, ft], scalar=c["G"][:, s["vec"], ft:ft + 1],
                                             in1=xr[:, ft % 2], op0=ALU.mult, op1=ALU.add).then_inc(x_new, 1)
                    if n is not None and ft:
                        add_square(n, ft - 1)
                if n is not None:
                    add_square(n, KT - 1)

            def make_h(s, h_free):
                wait(dve, unit_done, h_free)
                wait(dve, hid_ready, s["H_end"])

                def scaled(ft):
                    wait(dve, h_ready, KT * s["j"] + ft - 1)
                    dve.tensor_tensor(t[:, ft % 2], y[:, ft], rstd[:], ALU.mult).then_inc(t_ready, 1)
                scaled(0)
                for ft in range(KT):
                    if ft + 1 < KT:
                        scaled(ft + 1)
                    dve.wait_ge(hf_ready, KT * s["j"] + ft + 1)
                    steps.did(dve.tensor_copy(h[:, 0, ft], t[:, ft % 2]))
                    steps.sync()
                    dve.tensor_tensor(h[:, 1, ft], t[:, ft % 2], h[:, 0, ft].bitcast(F32),
                                      ALU.subtract).then_inc(h_ready, 1)

            for s in stages:
                p = prev(s)
                if s["kind"] == "O":
                    if p:
                        post(p)
                        inverse("pre", p)
                        make_h(p, 0)
                elif s["kind"] == "F":
                    dve.wait_ge(unit_done, p["U_end"])

                    def hidden_tile(i, m):
                        full, up = t[:, m], 2 * m + 1
                        dve.wait_ge(silu_ready, s["S"] + 2 * i + m + 1)
                        dve.wait_ge(unit_done, s["U"] + 4 * i + 2 * m + 2)
                        wait(dve, hid_ready, s["H"] + 2 * i + m - 1)
                        dve.tensor_tensor(full, sil[:, m], bank[up][:], ALU.mult).then_inc(bank_free[up], 1)
                        dve.wait_ge(bank_free[up], s["G"] // 4 + i + 1)
                        hi = hid[:, bass.ds(2 * i + m, 1), 0]
                        lo = hid[:, bass.ds(2 * i + m, 1), 1]
                        dve.tensor_copy(hi, full).then_inc(bank_free[2 * m], 1)
                        dve.wait_ge(bank_free[2 * m], s["G"] // 4 + i + 1)
                        dve.tensor_tensor(lo, full, hi.bitcast(F32), ALU.subtract).then_inc(hid_ready, 1)
                    hidden_tile(0, 0)
                    post(p)
                    for i, m in ((0, 1), (1, 0), (1, 1), (2, 0)):
                        hidden_tile(i, m)
                    if not p["final"]:
                        inverse("pre", p)
                    hidden_tile(2, 1)
                    with dve.Fori(3, HT // 2) as i:
                        for m in range(2):
                            hidden_tile(i, m)
                    if not p["final"]:
                        dve.wait_ge(hid_ready, s["H_end"])
                        make_h(p, s["U_out"])
                else:
                    dve.wait_ge(unit_done, p["U_end"])
                    dve.wait_ge(rows_in, 48)

                    def add_bias(half, n):
                        dve.wait_ge(unit_done, s["U"] + 4 * half + n + 1)
                        cols = slice(half * HALF, (half + 1) * HALF)
                        dve.tensor_tensor(v[:, n, cols], bank[n][:], rows[:, 0, cols],
                                          ALU.add).then_inc(bank_free[n], 1)
                    add_bias(0, 0)
                    add_bias(0, 1)
                    post(p)
                    for half, n in ((0, 2), (0, 3), (1, 0), (1, 1), (1, 2), (1, 3)):
                        add_bias(half, n)
                    inverse("pre", p)
                    for n in range(CH):
                        dve.wait_ge(v_ready, 2 * CH * s["half"] + CH + n + 1)
                        for half in range(2):
                            steps.did(dve.bn_stats(st6[:, n, half], v[:, n, half * HALF:(half + 1) * HALF]))
                        steps.sync()
                        if n < CH - 1:
                            steps.did(dve.bn_aggr(mv[:, n], st6[:, n]))
                        else:
                            dve.bn_aggr(mv[:, n], st6[:, n]).then_inc(var_ready, 1)
                    dve.wait_ge(var_std, s["half"] + 1)
                    steps.did(dve.reciprocal(rln[:], rln[:]))
                    steps.sync()
                    for n in range(CH):
                        steps.did(dve.tensor_scalar(v[:, n], v[:, n], mv[:, n, 0:1], rln[:, n:n + 1],
                                                    ALU.subtract, ALU.mult))
                        steps.sync()
                        steps.did(dve.tensor_tensor(v[:, n], v[:, n], rows[:, 1], ALU.mult))
                        steps.sync()
                        dve.tensor_tensor(v[:, n], v[:, n], rows[:, 2], ALU.add).then_inc(ln_ready, 1)
                    for g in range(KT):
                        k = g % 4
                        dve.wait_ge(mix_ready, KT * s["half"] + g + 1)
                        wait(dve, hid_ready, s["H"] + g)
                        full = t[:, g % 2].rearrange("p (n q) -> p n q", n=CH)
                        dve.tensor_tensor(full, bank[k][:].rearrange("p (n q) -> p n q", n=CH),
                                          bsp[:, g:g + 1].to_broadcast([P, CH, P]),
                                          ALU.add).then_inc(bank_free[k], 1)
                        dve.wait_ge(bank_free[k], (s["G"] + 2 * KT) // 4 + g // 4 + 1)
                        steps.did(dve.tensor_tensor(t[:, g % 2], t[:, g % 2], u[:, g], ALU.mult))
                        steps.sync()
                        steps.did(dve.tensor_copy(hid[:, g, 0], t[:, g % 2]))
                        steps.sync()
                        dve.tensor_tensor(hid[:, g, 1], t[:, g % 2], hid[:, g, 0].bitcast(F32),
                                          ALU.subtract).then_inc(hid_ready, 1)
                    dve.wait_ge(hid_ready, s["H_end"])
                    make_h(p, s["U_out"])

                n = n_norm["post", s["j"]]
                if p:
                    dve.wait_ge(x_out, 16 * s["j"])
                    wait(dve, h_ready, KT * min(s["j"], len(stages) - 2))
                clear_acc(n)
                for ft in range(KT):
                    dve.wait_ge(unit_done, y_done(s, ft // 4, ft % 4))
                    dve.tensor_copy(y[:, ft], bank[ft % 4][:]).then_inc(bank_free[ft % 4], 1)
                    if ft:
                        add_square(n, ft - 1)
                add_square(n, KT - 1)
            post(stages[-1])


def launch_tables():
    axis = DH // 2
    inv = np.float32(10000.0) ** (-np.arange(0, axis, 2, dtype=np.float32) / np.float32(axis))
    row = np.repeat(np.arange(T // 64, dtype=np.float32), 64)
    col = np.tile(np.arange(64, dtype=np.float32), T // 64)
    cos, sin = np.zeros((P, T), np.float32), np.zeros((P, T), np.float32)
    for p in range(P):
        pos = row if p % DH < axis else col
        f = p % axis
        ang = (pos * inv[f % (axis // 2)]).astype(np.float32)
        cos[p] = np.cos(ang)
        sin[p] = np.sin(ang) if f >= axis // 2 else -np.sin(ang)
    return np.ascontiguousarray(np.stack([cos, sin], 1))


def kernel(x, c, ctx, c_ctx, w_ada, b_ada, g_mix_pre, g_mix_post, g_ffn_pre, g_ffn_post, w_qkv, w_attn_out,
           lam_q1, lam_k1, lam_q2, lam_k2, g_subln, w_uv, b_uv, g_sgu, b_sgu, w_spatial, b_spatial,
           w_cmlp_out, w_ffn_in, w_ffn_out):
    import concourse.bacc as bacc
    from concourse.bass_utils import run_bass_kernel_spmd

    def arr(v):
        return np.asarray(v)

    def tiles(w):
        w = arr(w)
        K, N = w.shape
        return np.ascontiguousarray(w.reshape(K // P, P, N // P, P).transpose(2, 1, 0, 3)).reshape(N // P, P, K)

    def cols(v):
        return arr(v).reshape(-1, P).T

    def row(v):
        return np.broadcast_to(arr(v).reshape(1, -1), (P, arr(v).size))

    ada = arr(w_ada).reshape(2, KT, P, 6, D).transpose(0, 3, 1, 2, 4).reshape(12, KT, P, D)
    vecs = np.concatenate([cols(b_ada), cols(g_mix_pre), cols(g_mix_post), cols(g_ffn_pre), cols(g_ffn_post),
                           cols(c), cols(c_ctx), cols(arr(b_uv)[0, :D]), cols(g_subln)], axis=1)
    uv = tiles(arr(w_uv)[0])
    arrays = {
        "xT": arr(x)[0].T.reshape(KT, P, T),
        "ctxT": arr(ctx)[0].T.reshape(KT, P, C),
        "vecs": vecs,
        "lamv": np.stack([row(lam_q1), row(lam_k1), row(lam_q2), row(lam_k2)], 1),
        "trig": launch_tables(),
        "ident": np.eye(P, dtype=np.float32),
        "w_ada": ada,
        "w_qkv": tiles(arr(w_qkv)[0]),
        "w_attn_out": tiles(arr(w_attn_out)[0]),
        "w_uv": np.concatenate([uv[KT:], uv[:KT]]),
        "w_cmlp_out": tiles(arr(w_cmlp_out)[0]),
        "rows": np.stack([row(arr(b_uv)[0, D:]), row(g_sgu), row(b_sgu)], 1),
        "b_spatial": np.broadcast_to(arr(b_spatial)[0][None], (P, KT, P)),
        "w_spatialT": arr(w_spatial)[0].transpose(2, 0, 1),
    }
    for i in range(2):
        w = tiles(arr(w_ffn_in)[i])
        arrays[f"w_ffn_in{i}"] = np.stack([w[:HT], w[HT:]], 1).reshape(2 * HT, P, D)
        arrays[f"w_ffn_out{i}"] = tiles(arr(w_ffn_out)[i])
    nc = bacc.Bacc("TRN2", target_bir_lowering=False, num_devices=1)
    feed, aps = {}, {}
    for name, v in arrays.items():
        feed[f"in_{name}"] = v = np.ascontiguousarray(v)
        aps[name] = nc.dram_tensor(f"in_{name}", list(v.shape), F32, kind="ExternalInput").ap()
    out = nc.dram_tensor("out_xT", [KT, P, T], F32, kind="ExternalOutput").ap()
    build(nc, aps, out)
    got = run_bass_kernel_spmd(nc, [feed], core_ids=[0]).results[0]["out_xT"]
    return np.ascontiguousarray(got.reshape(D, T).T).reshape(1, T, D)
```

```python
import math
from contextlib import ExitStack

import numpy as np
import concourse.bass as bass
from concourse import mybir
from concourse.alu_op_type import AluOpType as ALU

ACT = mybir.ActivationFunctionType
AX = mybir.AxisListType
F32 = mybir.dt.float32
F32R = mybir.dt.float32r

P = 128
D = 1024
KT = D // P
T = 1024
C = 256
TA = T + C
HALF = T // 2
FH = 2816
HT = FH // P
DH = 64
NPAIR = 8
NADA = 2 * 6 * KT
EPS = 1e-6
LAM_INIT = 0.8 - 0.6 * math.exp(-0.3 * 0)
NRING = 4
GROUPS_KT = [(0, 8), (8, 16), (16, HT)]

V_BADA = 0
V_MIXPRE = V_BADA + NADA
V_MIXPOST = V_MIXPRE + 2 * KT
V_FFNPRE = V_MIXPOST + 2 * KT
V_FFNPOST = V_FFNPRE + 2 * KT
V_C = V_FFNPOST + 2 * KT
V_CCTX = V_C + KT
V_BU = V_CCTX + KT
V_SUBLN = V_BU + KT
NV = V_SUBLN + 1
SH_M, SC_M, G_M, SH_F, SC_F, G_F = range(6)
REGION_KB = 136


def wait(eng, sem, value):
    if isinstance(value, int) and value <= 0:
        return
    eng.wait_ge(sem, value)


def opens(i):
    return isinstance(i, int) and i == 0


def loop(eng, n, body):
    body(0)
    if n > 1:
        with eng.Fori(1, n) as i:
            body(i)


class Steps:

    def __init__(self, eng, sem):
        self.eng, self.sem, self.n, self.base = eng, sem, 0, 0

    def did(self, ins):
        ins.then_inc(self.sem, 1)
        self.n += 1

    def sync(self):
        self.eng.wait_ge(self.sem, self.base + self.n)

    def loop(self, n, per, body):
        start = self.n
        body(0)
        assert self.n - start == per, (self.n - start, per)
        if n > 1:
            with self.eng.Fori(1, n) as i:
                self.n, self.base = start, i * per
                body(i)
            self.base = 0
        self.n = start + n * per


def product(pe, out, n_kt, weight, x):
    for kt in range(n_kt):
        for a, b in ((0, 0), (0, 1), (1, 0)):
            last = pe.matmul(out, weight(a, kt), x(b, kt), start=weight.first and kt == 0 and a == b == 0,
                             stop=weight.last and kt == n_kt - 1 and a == 1)
    return last


class W:

    def __init__(self, at, first=True, last=True):
        self.at, self.first, self.last = at, first, last

    def __call__(self, a, kt):
        return self.at(a, kt)


def split_weights(pool, turn, steps, raw, ws, slot, n_kt, split_ready):
    pool.sem_inc(turn, 1)
    steps.did(pool.tensor_scalar(ws[:, slot, 0, 0:n_kt, :], raw[:, slot, 0:n_kt, :], 1.0, 1.0, ALU.mult, ALU.mult))
    steps.sync()
    pool.tensor_tensor(ws[:, slot, 1, 0:n_kt, :], raw[:, slot, 0:n_kt, :],
                       ws[:, slot, 0, 0:n_kt, :].bitcast(F32), ALU.subtract).then_inc(split_ready, 1)


def build(nc, a, out):
    with ExitStack() as keep:
        def sb(name, shape, dt=F32):
            return keep.enter_context(nc.sbuf_tensor(name, shape, dt))

        qT = nc.dram_tensor("q_scratch", [KT, P, 2, T], F32, kind="Internal").ap()
        kT = nc.dram_tensor("k_scratch", [KT, P, 2, TA], F32, kind="Internal").ap()
        vS = nc.dram_tensor("v_scratch", [TA // P, P, D], F32, kind="Internal").ap()
        oT = nc.dram_tensor("o_scratch", [NPAIR, P, 2, HALF], F32, kind="Internal").ap()
        xS = nc.dram_tensor("x_scratch", [KT, P, T], F32, kind="Internal").ap()
        c = {
            "vecs": sb("vecs", [P, NV]),
            "mod": sb("mod", [P, NADA]),
            "modc": sb("modc", [P, 2 * KT]),
            "A": sb("A", [P, 5, KT]),
            "G": sb("G", [P, 4, KT]),
            "neglam": sb("neglam", [P, 1]),
            "gsub": sb("gsub", [P, 1]),
            "ones": sb("ones", [P, P]),
            "eps": sb("eps", [P, 1]),
        }
        base = -(-nc.sbuf_base // 32) * 32

        def at(name, shape, kb, dt=F32):
            return nc.alloc_sbuf_tensor_at(name, shape, dt, offset=base + kb * 1024)

        def sem(name):
            return keep.enter_context(nc.semaphore(name))

        c["kd0"] = at("k_double0", [P, 2, 2, TA], 0, F32R)
        c["q0"] = at("q_stack0", [P, 2, T], 20, F32R)
        c["o_a"] = at("o_half_a", [P, NPAIR, 2, HALF], 32, F32R)
        c["ws"] = at("wsplit3", [P, NRING, 2, KT, P], 88, F32R)
        c["raw"] = at("wraw3", [P, NRING, KT, P], 120)
        c["pair_in"] = [sem(f"pair_in{s}") for s in range(2)]
        c["raw_full"] = [sem(f"b3_raw_full{s}") for s in range(NRING)]
        c["split_ready"], c["split_step"], c["split_turn"] = sem("b3_split_ready"), sem("b3_pool_step"), sem("b3_turn")
        block1(nc, a, c, at, qT, kT, vS)
        block2(nc, a, c, at, qT, kT, vS, oT)
        block3(nc, a, c, at, oT, xS, out)


def load_qk(sp, q, kd, qT_pair, kT_pair, full):
    for e in range(2):
        rows = slice(e * DH, (e + 1) * DH)
        for part in range(2):
            sp.dma_start(q[part * DH:(part + 1) * DH, e].bitcast(F32), qT_pair[rows, part]).then_inc(full, 16)
            for copy in range(2):
                sp.dma_start(kd[copy * DH:(copy + 1) * DH, e, part].bitcast(F32), kT_pair[rows, part]).then_inc(full, 16)


def block1(nc, a, c, at, qT, kT, vS):
    with ExitStack() as ctx:
        def sb(name, shape, dt=F32):
            return ctx.enter_context(nc.sbuf_tensor(name, shape, dt))

        def sem(name):
            return ctx.enter_context(nc.semaphore(name))

        W_ADA = T
        ctx.enter_context(nc.sbuf_tensor("shared_region1", [P, 72 * 256 + 8], F32))
        h = sb("h_all", [P, 2, KT, TA], F32R)
        ws = at("wsplit1", [P, NRING, 2, KT, P], 0, F32R)
        first_sum = at("first_sum", [P, 2, W_ADA], 16)
        y = at("x_in", [P, 2, KT, HALF], 32)
        xc = at("ctx_in", [P, KT, C], 32)
        late = at("ctx_tmp", [P, 5, C], 40)
        late_sum = at("late_sum", [P, 2, 2, W_ADA], 48)
        ws_v = at("wsplit_v", [P, NRING, 2, KT, P], 32, F32R)
        st = at("qk_out", [P, 2, 2, HALF], 64, F32R)
        raw = sb("wraw1", [P, NRING, KT, P])
        ada = sb("ada_raw", [P, 4, W_ADA])
        trig = sb("trig", [P, 2, T])
        sq = sb("sq1", [P, 2, HALF])
        t = sb("t1", [P, 2, HALF])
        cosp = sb("cos_part", [P, HALF])
        rstd = sb("rstd1", [P, HALF])
        lamv = sb("lamv", [P, 4, DH])
        lams = sb("lams", [P, 4])
        sx = sb("silu_c", [P, 2, KT])
        bank = [ctx.enter_context(nc.psum_tensor(f"acc1_{b}", [P, HALF], F32)) for b in range(4)]
        pstat = ctx.enter_context(nc.psum_tensor("stat1", [P, HALF], F32))
        pada = ctx.enter_context(nc.psum_tensor("ada_ps", [P, HALF], F32))

        last_sum = trig
        vecs_in, lam_in, trig_in = sem("vecs_in"), sem("lam_in"), sem("trig_in")
        x_in = [sem(f"x_in{s}") for s in range(3)]
        raw_full = [sem(f"b1_raw_full{s}") for s in range(NRING)]
        ada_full = [sem(f"ada_full{s}") for s in range(4)]
        split_ready = sem("b1_split_ready")
        ada_dve, ada_pool = sem("ada_dve"), sem("ada_pool")
        ada_scaled = sem("ada_scaled")
        sum_ready, mod_out = sem("sum_ready"), sem("mod_out")
        silu_ready, const_ready, mods_ready = sem("silu_ready"), sem("const_ready"), sem("mods_ready")
        sq_ready, sq_used = sem("b1_sq_ready"), sem("b1_sq_used")
        std_ready, y_ready, t_ready = sem("b1_std_ready"), sem("b1_y_ready"), sem("b1_t_ready")
        hi_ready, h_ready = sem("b1_hi_ready"), sem("b1_h_ready")
        group_ready = sem("b1_group_ready")
        bank_free = [sem(f"b1_bank_free{b}") for b in range(4)]
        rope_done, qk_hi, qk_lo = sem("rope_done"), sem("qk_hi"), sem("qk_lo")
        st_out = [sem(f"st_out{s}") for s in range(2)]
        v_out = [sem(f"v_out{s}") for s in range(2)]
        dve_step, pool_step, turn = sem("b1_dve_step"), sem("b1_pool_step"), sem("b1_turn")
        lam_exp = sem("lam_exp")

        SEG = [(y[:, 0], HALF, C, sq, t, rstd), (y[:, 1], HALF, C + HALF, sq, t, rstd),
               (xc, C, 0, late[:, 0:2], late[:, 2:4], late[:, 4])]
        FIRST = 2
        QKG = [[1, 2], [1, 2, 0]]
        G_K, G_V = 2 * KT, 2 * KT + 3 * KT
        VT = TA // P
        CTX_TILES = {(2, 0): (0, 3), (2, 1): (3, 6), (3, 0): (6, KT)}

        def cols(g):
            return (0, C) if g == 0 else (C + (g - 1) * HALF, C + g * HALF)

        def before(kind, i, k, n):
            if n > 0:
                return kind, i, k, n - 1
            if k > 0:
                return kind, i, k - 1, len(QKG[kind]) - 1
            if opens(i):
                return (0, 1, 3, 1) if kind else None
            return kind, i - 1, 3, len(QKG[kind]) - 1

        def number(kind, i, k, n):
            ng = len(QKG[kind])
            return (G_K if kind else 0) + 4 * ng * i + ng * k + n, ng * k + n

        def first_of_all(kind, i, k):
            return kind == 0 and opens(i) and k == 0

        block = ctx.enter_context(nc.Block())

        def sums_of(j):
            return last_sum if j >= 4 else late_sum[:, j % 2]

        def wait_sums_free(eng, j):
            wait(eng, sum_ready, FIRST + 5 if j == 5 else FIRST + j - 1)

        @block.sync
        def _(sp):
            def load_first_ada(n):
                wait(sp, ada_dve, n - 3)
                sp.dma_start(ada[:, n % 4], a["w_ada"][n // KT, n % KT]).then_inc(ada_full[n % 4], 16)

            def load_ada(j, kt):
                for e, (used, before) in enumerate(((ada_dve, FIRST * KT), (ada_pool, 0))):
                    wait(sp, used, before + KT * j + kt - 1)
                    s = 2 * e + kt % 2
                    sp.dma_start(ada[:, s], a["w_ada"][2 * j + e, kt]).then_inc(ada_full[s], 16)

            def load_w(u, s):
                wait(sp, split_ready, u - NRING + 1)
                sp.dma_start(raw[:, s], a["w_qkv"][u].rearrange("p (k c) -> p k c", k=KT)).then_inc(raw_full[s], 16)

            sp.dma_start(c["vecs"][:], a["vecs"]).then_inc(vecs_in, 16)
            sp.dma_start(lamv[:], a["lamv"]).then_inc(lam_in, 16)
            for half in range(2):
                sp.dma_start(y[:, half], a["xT"][:, :, half * HALF:(half + 1) * HALF].rearrange(
                    "k p t -> p k t")).then_inc(x_in[half], 16)
                for kt in range(KT):
                    load_first_ada(half * KT + kt)
            for u in range(NRING):
                load_w(u, u)
            sp.dma_start(trig[:], a["trig"]).then_inc(trig_in, 16)
            sp.wait_ge(t_ready, KT)
            sp.dma_start(xc[:], a["ctxT"].rearrange("k p t -> p k t")).then_inc(x_in[2], 16)
            sp.wait_ge(ada_dve, FIRST * KT)

            def body(j):
                for k in range(4):
                    load_ada(j, 2 * k)
                    load_ada(j, 2 * k + 1)
                    load_w(4 * j + k + NRING, k)
            loop(sp, 4, body)
            for k in range(NRING):
                load_w(5 * NRING + k, k)
            for j in (4, 5):
                for kt in range(KT):
                    load_ada(j, kt)
            sp.wait_ge(group_ready, G_V + VT)
            for s in range(2):
                sp.wait_ge(st_out[s], 16 * (2 * KT + 3 * KT) // 2)
            load_qk(sp, c["q0"], c["kd0"], qT[0], kT[0], c["pair_in"][0])

        @block.gpsimd
        def _(pool):
            steps = Steps(pool, pool_step)
            def modulation(j, kt):
                m = KT * j + kt
                total, term = sums_of(j)[:, 1], ada[:, 2 + kt % 2]
                wait(pool, ada_scaled, m + 1)
                wait(pool, ada_pool, m)
                if kt == 0:
                    wait_sums_free(pool, j)
                pool.sem_inc(turn, 1)
                if kt == 0:
                    pool.tensor_scalar(total, term, 1.0, 1.0, ALU.mult, ALU.mult).then_inc(ada_pool, 1)
                else:
                    pool.tensor_tensor(total, total, term, ALU.add).then_inc(ada_pool, 1)

            def split(turn_, k, into):
                pool.wait_ge(raw_full[k], 16 * turn_)
                split_weights(pool, turn, steps, raw, into, k, KT, split_ready)

            for k in range(NRING):
                if k == 2:
                    pool.wait_ge(sum_ready, FIRST)
                split(1, k, ws)
            pool.wait_ge(t_ready, 2 * KT)

            for kind in range(2):
                def unit(i, k):
                    last, _ = number(kind, i, k, len(QKG[kind]) - 1)
                    pool.wait_ge(group_ready, last + 1)
                    split(2 * kind + i + 2, k, ws)
                    modulation(2 * kind + i, 2 * k)
                    modulation(2 * kind + i, 2 * k + 1)
                steps.loop(2, 4, lambda i: [unit(i, k) for k in range(4)])
            pool.wait_ge(sum_ready, FIRST + 4)
            for k in range(NRING):
                split(6, k, ws_v)
            pool.wait_ge(qk_lo, G_V)
            for j in (4, 5):
                for kt in range(KT):
                    modulation(j, kt)

        @block.tensor
        def _(pe):
            def statistics(s):
                w = SEG[s][1]
                wait(pe, std_ready, s)
                for kt in range(KT):
                    pe.wait_ge(sq_ready, KT * s + kt + 1)
                    pe.matmul(pstat[:, 0:w], c["ones"][:], SEG[s][3][:, kt % 2, 0:w], start=kt == 0,
                              stop=kt == KT - 1).then_inc(sq_used, 1)

            def partition_sums(sums, col0):
                for n in range(KT):
                    last = pe.matmul(pada[:, col0 + n:col0 + n + 1], sums[:, n * P:(n + 1) * P], c["ones"][:, 0:1],
                                     start=True, stop=True)
                return last

            def late_sums(j):
                pe.wait_ge(ada_dve, FIRST * KT + KT * (j + 1))
                pe.wait_ge(ada_pool, KT * (j + 1))
                pe.wait_ge(mod_out, 1 + j)
                partition_sums(sums_of(j)[:, 0], 0)
                partition_sums(sums_of(j)[:, 1], KT).then_inc(sum_ready, 1)

            pe.wait_ge(const_ready, 1)
            for s in range(2):
                statistics(s)
            for s in range(FIRST):
                pe.wait_ge(ada_dve, KT * (s + 1))
                partition_sums(first_sum[:, s], KT * s).then_inc(sum_ready, 1)

            def unit(i, k, kind):
                u = kind * KT + 4 * i + k
                wait(pe, split_ready, u + 1)
                first = first_of_all(kind, i, k)
                for n, g in enumerate(QKG[kind]):
                    G, at = number(kind, i, k, n)
                    b = at % 4
                    wait(pe, bank_free[b], (G_K if kind else 0) // 4 + len(QKG[kind]) * i + at // 4)
                    lo, hi = cols(g)
                    if kind == 1 and opens(i) and k == 0 and g == 0:
                        pe.wait_ge(h_ready, 3 * KT)
                    if first:
                        for kt in range(KT):
                            pe.wait_ge(h_ready, KT * (g - 1) + kt + 1)
                            last = product(pe, bank[b][:, 0:hi - lo], 1,
                                           W(lambda p, _: ws[:, k, p, kt], kt == 0, kt == KT - 1),
                                           lambda p, _: h[:, p, kt, lo:hi])
                    else:
                        last = product(pe, bank[b][:, 0:hi - lo], KT, W(lambda p, kt: ws[:, k, p, kt]),
                                       lambda p, kt: h[:, p, kt, lo:hi])
                    last.then_inc(group_ready, 1)
                    if k == 1 and n == 0 and not (kind == 0 and opens(i)):
                        late_sums(2 * kind + i - 1)
                if kind == 0 and opens(i) and k == 3:
                    statistics(2)

            for kind in range(2):
                loop(pe, 2, lambda i: [unit(i, k, kind) for k in range(4)])
            for half in range(2):
                pe.wait_ge(split_ready, 2 * KT + 4 * half + 4)
                wv = ws_v if half else ws
                for n in range(VT):
                    g = G_V + VT * half + n
                    pe.wait_ge(bank_free[g % 4], g // 4)
                    last = product(pe, bank[g % 4][:], KT, W(lambda p, kt: h[:, p, kt, n * P:(n + 1) * P]),
                                   lambda p, kt: wv[:, 0:4, p, kt])
                    last.then_inc(group_ready, 1)
                    if n == 2:
                        late_sums(3 + half)
                    if half == 1 and n == KT:
                        late_sums(5)

        @block.scalar
        def _(act):
            act.wait_ge(vecs_in, 16)
            act.activation(sx[:, 0], c["vecs"][:, V_C:V_C + KT], ACT.Silu).then_inc(silu_ready, 1)
            act.activation(sx[:, 1], c["vecs"][:, V_CCTX:V_CCTX + KT], ACT.Silu).then_inc(silu_ready, 1)
            act.wait_ge(dve_step, 4)
            act.activation(lams[:, 2:4], lams[:, 0:2], ACT.Exp).then_inc(lam_exp, 1)
            act.wait_ge(const_ready, 2)

            def squares(s):
                x, w, _, sq_, _, _ = SEG[s]
                act.wait_ge(x_in[s], 16)
                for kt in range(KT):
                    wait(act, sq_used, KT * s + kt - 1)
                    act.activation(sq_[:, kt % 2, 0:w], x[:, kt], ACT.Square).then_inc(sq_ready, 1)

            def std(s):
                act.wait_ge(sq_used, KT * (s + 1))
                wait(act, y_ready, KT * s)
                act.activation(SEG[s][5][:, 0:SEG[s][1]], pstat[:, 0:SEG[s][1]], ACT.Sqrt,
                               bias=c["eps"][:]).then_inc(std_ready, 1)

            def modulate(s, k0, k1):
                x, w, col0, _, t_, _ = SEG[s]
                scale = c["A"][:, 4 if s == 2 else 0]
                shift = c["modc"] if s == 2 else c["mod"]

                def full(kt):
                    act.wait_ge(y_ready, KT * s + kt + 1)
                    wait(act, h_ready, KT * s + kt - 1)
                    act.activation(t_[:, kt % 2, 0:w], x[:, kt], ACT.Identity, bias=shift[:, kt:kt + 1],
                                   scale=scale[:, kt:kt + 1]).then_inc(t_ready, 1)
                full(k0)
                for kt in range(k0, k1):
                    act.wait_ge(t_ready, KT * s + kt + 1)
                    act.activation(h[:, 0, kt, col0:col0 + w], t_[:, kt % 2, 0:w], ACT.Copy).then_inc(hi_ready, 1)
                    if kt + 1 < k1:
                        full(kt + 1)

            def modulation_product(j, kt):
                act.wait_ge(ada_full[2 + kt % 2], 16 * (FIRST * 2 + 4 * j + kt // 2 + 1))
                act.activation(ada[:, 2 + kt % 2], ada[:, 2 + kt % 2], ACT.Copy,
                               scale=sx[:, 1 if j == 0 else 0, kt:kt + 1]).then_inc(ada_scaled, 1)

            for s in range(2):
                squares(s)
                std(s)
            act.wait_ge(sum_ready, FIRST)
            act.activation(c["mod"][:, 0:FIRST * KT], pada[:, 0:FIRST * KT], ACT.Copy, scale=float(D)).then_inc(mod_out, 1)
            act.wait_ge(mods_ready, 1)
            for s in range(2):
                modulate(s, 0, KT)
            act.wait_ge(h_ready, 2 * KT)

            def write(kind, i, k, n):
                G, at = number(kind, i, k, n)
                lo, hi = cols(QKG[kind][n])
                wait(act, qk_lo, G + 1)
                dst = kT[4 * i + k][:, :, lo:hi] if kind else qT[4 * i + k][:, :, lo - C:hi - C]
                act.dma_start(dst, st[:, at % 2, :, 0:hi - lo].bitcast(F32)).then_inc(st_out[at % 2], 16)

            def modulation_out(j):
                act.wait_ge(sum_ready, FIRST + j + 1)
                dst = c["modc"][:] if j == 0 else c["mod"][:, 2 * KT * j:2 * KT * (j + 1)]
                act.activation(dst, pada[:, 0:2 * KT], ACT.Copy, scale=float(D)).then_inc(mod_out, 1)

            def unit(i, k, kind):
                ng = len(QKG[kind])
                for n, g in enumerate(QKG[kind]):
                    G, at = number(kind, i, k, n)
                    lo, hi = cols(g)
                    w = hi - lo
                    wait(act, group_ready, G + 1)
                    wait(act, rope_done, G - 1)
                    act.activation(sq[:, at % 2, 0:w], bank[at % 4][:, 0:w], ACT.Copy,
                                   scale=1.0 if kind else DH ** -0.5).then_inc(bank_free[at % 4], 1)
                    prev = before(kind, i, k, n)
                    if prev:
                        write(*prev)
                    wait(act, rope_done, G + 1)
                    wait(act, st_out[at % 2], 16 * ((G_K if kind else 0) // 2 + 2 * ng * i + at // 2))
                    act.activation(st[:, at % 2, 0, 0:w], t[:, at % 2, 0:w], ACT.Copy).then_inc(qk_hi, 1)
                    if g > 0:
                        modulation_product(2 * kind + i, 2 * k + g - 1)
                    if kind == 0 and not opens(i) and (k, n) in CTX_TILES:
                        act.wait_ge(mods_ready, 2)
                        modulate(2, *CTX_TILES[k, n])
                if k == 1 and not (kind == 0 and opens(i)):
                    modulation_out(2 * kind + i - 1)
                if kind == 0:
                    if opens(i) and k == 2:
                        squares(2)
                    if opens(i) and k == 3:
                        std(2)

            for kind in range(2):
                loop(act, 2, lambda i: [unit(i, k, kind) for k in range(4)])
            write(1, 1, 3, 2)
            for half in range(2):
                for n in range(VT):
                    m = VT * half + n
                    g = G_V + m
                    act.wait_ge(group_ready, g + 1)
                    wait(act, v_out[m % 2], 16 * (m // 2))
                    act.activation(t[:, m % 2], bank[g % 4][:], ACT.Copy).then_inc(bank_free[g % 4], 1)
                    act.wait_ge(bank_free[g % 4], g // 4 + 1)
                    act.dma_start(vS[n][:, half * HALF:(half + 1) * HALF], t[:, m % 2]).then_inc(v_out[m % 2], 16)
                    if n < KT:
                        modulation_product(4 + half, n)
                    if n == 3:
                        modulation_out(3 + half)
                    if half == 1 and n == KT:
                        modulation_out(5)
            for s in range(2):
                act.wait_ge(st_out[s], 16 * (2 * KT + 3 * KT) // 2)
                act.wait_ge(v_out[s], 16 * VT)

        @block.vector
        def _(dve):
            steps = Steps(dve, dve_step)
            vec = c["vecs"]
            swap = [(p + 16) % 32 for p in range(32)]
            dve.memset(c["ones"][:], 1.0 / D).then_inc(const_ready, 1)
            dve.memset(c["eps"][:], EPS).then_inc(const_ready, 1)
            dve.wait_ge(lam_in, 16)
            for j in range(2):
                steps.did(dve.tensor_tensor(lamv[:, 2 * j], lamv[:, 2 * j], lamv[:, 2 * j + 1], ALU.mult))
                steps.sync()
                steps.did(dve.tensor_reduce(lams[:, j:j + 1], lamv[:, 2 * j], AX.X, ALU.add))

            def first_modulation(n):
                dve.wait_ge(ada_full[n % 4], 16 * (n // 4 + 1))
                out_, w = first_sum[:, n // KT], ada[:, n % 4]
                if n % KT == 0:
                    dve.tensor_scalar(out_, w, sx[:, 0, 0:1], None, ALU.mult).then_inc(ada_dve, 1)
                else:
                    dve.wait_ge(ada_dve, n)
                    dve.scalar_tensor_tensor(out=out_, in0=w, scalar=sx[:, 0, n % KT:n % KT + 1], in1=out_,
                                             op0=ALU.mult, op1=ALU.add).then_inc(ada_dve, 1)

            def modulation(j, kt):
                dve.wait_ge(ada_full[kt % 2], 16 * (FIRST * 2 + 4 * j + kt // 2 + 1))
                dve.wait_ge(ada_dve, FIRST * KT + KT * j + kt)
                out_, w = sums_of(j)[:, 0], ada[:, kt % 2]
                stream = 1 if j == 0 else 0
                if kt == 0:
                    wait_sums_free(dve, j)
                    dve.tensor_scalar(out_, w, sx[:, stream, 0:1], None, ALU.mult).then_inc(ada_dve, 1)
                else:
                    dve.scalar_tensor_tensor(out=out_, in0=w, scalar=sx[:, stream, kt:kt + 1], in1=out_,
                                             op0=ALU.mult, op1=ALU.add).then_inc(ada_dve, 1)

            def inverse_rms(s):
                r = SEG[s][5][:, 0:SEG[s][1]]
                dve.wait_ge(std_ready, s + 1)
                steps.did(dve.reciprocal(r, r))
                steps.sync()

            def normalize(s, kt):
                x, w, _, _, _, r = SEG[s]
                dve.tensor_tensor(x[:, kt], x[:, kt], r[:, 0:w], ALU.mult).then_inc(y_ready, 1)

            def low_part(s, kt):
                _, w, col0, _, t_, _ = SEG[s]
                dve.wait_ge(hi_ready, KT * s + kt + 1)
                dve.tensor_tensor(h[:, 1, kt, col0:col0 + w], t_[:, kt % 2, 0:w],
                                  h[:, 0, kt, col0:col0 + w].bitcast(F32), ALU.subtract).then_inc(h_ready, 1)

            def modulation_vectors(shift_scale, A):
                steps.did(dve.tensor_tensor(shift_scale, shift_scale, vec[:, V_BADA:V_BADA + FIRST * KT], ALU.add))
                steps.sync()
                dve.scalar_tensor_tensor(out=A, in0=shift_scale[:, KT:2 * KT], scalar=1.0,
                                         in1=vec[:, V_MIXPRE:V_MIXPRE + KT], op0=ALU.add,
                                         op1=ALU.mult).then_inc(mods_ready, 1)

            dve.wait_ge(silu_ready, 2)
            for n in range(FIRST * KT):
                first_modulation(n)
                if n == 3:
                    inverse_rms(0)
                    for kt in range(KT):
                        normalize(0, kt)
            inverse_rms(1)
            dve.wait_ge(mod_out, 1)
            modulation_vectors(c["mod"][:, 0:FIRST * KT], c["A"][:, 0])
            for kt in range(KT):
                normalize(1, kt)
                low_part(0, kt)
            for kt in range(KT):
                low_part(1, kt)
            dve.wait_ge(lam_exp, 1)
            steps.did(dve.tensor_tensor(lams[:, 0:1], lams[:, 3:4], lams[:, 2:3], ALU.subtract))
            steps.sync()
            steps.did(dve.tensor_scalar(c["neglam"][:], lams[:, 0:1], -LAM_INIT, None, ALU.add))
            steps.did(dve.tensor_scalar(c["gsub"][:], vec[:, V_SUBLN:V_SUBLN + 1], 1.0 - LAM_INIT, None, ALU.mult))
            dve.wait_ge(trig_in, 16)
            dve.wait_ge(t_ready, 2 * KT)

            def unit(i, k, kind):
                for n, g in enumerate(QKG[kind]):
                    G, at = number(kind, i, k, n)
                    lo, hi = cols(g)
                    w = hi - lo
                    wait(dve, qk_lo, G - 1)
                    src, dst = sq[:, at % 2, 0:w], t[:, at % 2, 0:w]
                    wait(dve, bank_free[at % 4], (G_K if kind else 0) // 4 + len(QKG[kind]) * i + at // 4 + 1)
                    if g > 0:
                        cos, sin = (trig[:, m, lo - C:hi - C] for m in range(2))
                        partner, cp = rstd[:, 0:w], cosp[:, 0:w]
                        wait(dve, rope_done, G)
                        steps.did(dve.stream_shuffle(partner, src, swap))
                        steps.did(dve.tensor_tensor(cp, src, cos, ALU.mult))
                        steps.sync()
                        steps.did(dve.tensor_tensor(partner, partner, sin, ALU.mult))
                        steps.sync()
                        dve.tensor_tensor(dst, cp, partner, ALU.add).then_inc(rope_done, 1)
                        modulation(2 * kind + i, 2 * k + g - 1)
                    else:
                        dve.tensor_copy(dst, src).then_inc(rope_done, 1)
                    wait(dve, qk_hi, G + 1)
                    dve.tensor_tensor(st[:, at % 2, 1, 0:w], dst, st[:, at % 2, 0, 0:w].bitcast(F32),
                                      ALU.subtract).then_inc(qk_lo, 1)
                    if kind == 0 and not opens(i) and (k, n) in CTX_TILES:
                        for kt in range(*CTX_TILES[k, n]):
                            low_part(2, kt)
                if kind == 0:
                    if not opens(i) and k == 0:
                        inverse_rms(2)
                    if not opens(i) and k in (0, 1):
                        for kt in range(4 * k, 4 * k + 4):
                            normalize(2, kt)
                    if not opens(i) and k == 1:
                        dve.wait_ge(mod_out, 2)
                        modulation_vectors(c["modc"][:], c["A"][:, 4])

            for kind in range(2):
                for i in range(2):
                    for k in range(4):
                        unit(i, k, kind)
            dve.wait_ge(rope_done, G_V)
            for j in (4, 5):
                for kt in range(KT):
                    modulation(j, kt)

            dve.wait_ge(mod_out, 7)
            late_mod = c["mod"][:, FIRST * KT:NADA]
            steps.did(dve.tensor_tensor(late_mod, late_mod, vec[:, V_BADA + FIRST * KT:V_BADA + NADA], ALU.add))
            steps.sync()
            for n in range(4):
                layer, ffn = divmod(n, 2)
                m0 = layer * 6 * KT
                sc, gate = (SC_F, G_F) if ffn else (SC_M, G_M)
                pre = (V_FFNPRE if ffn else V_MIXPRE) + layer * KT
                post = (V_FFNPOST if ffn else V_MIXPOST) + layer * KT
                if n:
                    steps.did(dve.scalar_tensor_tensor(
                        out=c["A"][:, n], in0=c["mod"][:, m0 + sc * KT:m0 + (sc + 1) * KT], scalar=1.0,
                        in1=vec[:, pre:pre + KT], op0=ALU.add, op1=ALU.mult))
                steps.did(dve.tensor_tensor(c["G"][:, n], c["mod"][:, m0 + gate * KT:m0 + (gate + 1) * KT],
                                            vec[:, post:post + KT], ALU.mult))


def block2(nc, a, c, at, qT, kT, vS, oT):
    with ExitStack() as ctx:
        def sb(name, shape, dt=F32):
            return ctx.enter_context(nc.sbuf_tensor(name, shape, dt))

        def sem(name):
            return ctx.enter_context(nc.semaphore(name))

        QT = T // P
        NT = NPAIR * QT
        BODY = 2 * QT
        KEYS = TA // P
        LAST = NT // BODY - 1

        ctx.enter_context(nc.sbuf_tensor("shared_region2", [P, REGION_KB * 256 + 8], F32))
        q = [c["q0"], sb("q_stack1", [P, 2, T], F32R)]
        kd = [c["kd0"], at("k_double1", [P, 2, 2, TA], 64, F32R)]
        v = sb("v_pair", [P, 2, KEYS, P])
        prob = sb("prob", [P, 2, 2, TA])
        w = sb("w_diff", [P, 2, TA])
        wT = sb("w_diffT", [P, 2, KEYS, P])
        negmax = sb("negmax", [P, 2, 2])
        sums = sb("sums", [P, 2, 2])
        rsum = sb("rsum", [P, 4, 2])
        coef = sb("coef", [P, 2])
        junk = sb("junk", [P, P])
        ss = sb("ss", [P, 2])
        ms = sb("ms", [P, 2])
        half = sb("minus_half", [P, 1])
        rstd = sb("rstd2", [P, 2])
        on = sb("o_norm", [P, 2, P])
        osb = sb("o_copy", [P, 4, P])
        of = sb("o_full", [P, 2, 2 * P])
        ost = sb("o_out", [P, 2, 2, 2 * P], F32R)
        ident = sb("ident", [P, P])

        s_ps = [ctx.enter_context(nc.psum_tensor(f"scores{e}", [P, 3 * 512], F32)) for e in range(2)]
        t_ps = ctx.enter_context(nc.psum_tensor("transposed", [P, 512], F32))
        o_ps = ctx.enter_context(nc.psum_tensor("o_ps", [P, 512], F32))

        ident_in, half_set = sem("ident_in"), sem("half_set")
        pair_in = c["pair_in"]
        s_ready, max_ready, exp_done = sem("s_ready"), sem("max_ready"), sem("exp_done")
        rsum_ready, coef_ready, w_ready = sem("rsum_ready"), sem("coef_ready"), sem("w_ready")
        t_ready, wT_ready, o_ready = sem("t_ready"), sem("wT_ready"), sem("o_ready")
        o_copied = sem("o_copied")
        ss_ready, rstd_ready, on_ready = sem("ss_ready"), sem("rstd_ready"), sem("on_ready")
        oT_ready, of_ready, ost_ready = sem("oT_ready"), sem("of_ready"), sem("ost_ready")
        o_out = [sem(f"o_out{s}") for s in range(2)]
        pool_step, hi_step, turn = sem("b2_pool_step"), sem("b2_hi_step"), sem("b2_turn")

        BANK = 512
        CUTS = [0, BANK, 2 * BANK, TA]
        CHUNKS = [(0, 4), (4, 8), (8, KEYS)]

        class Tile:

            def __init__(self, i, at, first=False, last=False):
                self.exists = not (first and at < 0) and not (last and at >= BODY)
                self.n = BODY * i + at
                self.s = at % 2
                self.q = at % QT
                self.pair = BODY // QT * i + at // QT
                self.buf = at // QT % 2
                self.fill = i + at // BODY
                self.duo = BODY // 2 * i + at // 2
                self.duo_slot = at // 2 % 2
                self.half = self.q // (QT // 2)
                self.s4 = at % 4

        def steps_of(eng, step):
            for at in range(-2, BODY):
                step(lambda k: Tile(0, at + k, first=True))
            with eng.Fori(1, LAST) as i:
                for at in range(BODY):
                    step(lambda k: Tile(i, at + k))
            for at in range(BODY + 5):
                step(lambda k: Tile(LAST, at + k, last=True))

        block = ctx.enter_context(nc.Block())

        @block.sync
        def _(sp):
            def load_v(p, s):
                sp.dma_start(v[:, s], vS.rearrange("n p (h e) -> h p n e", h=NPAIR)[p]).then_inc(pair_in[s], 16)

            def load_pair(p, s):
                load_qk(sp, q[s], kd[s], qT[p], kT[p], pair_in[s])
                load_v(p, s)

            load_v(0, 0)
            sp.dma_start(ident[:], a["ident"]).then_inc(ident_in, 16)
            load_pair(1, 1)
            for k in range(NRING):
                sp.dma_start(c["raw"][:, k], a["w_attn_out"][k].rearrange("p (k c) -> p k c", k=KT)
                             ).then_inc(c["raw_full"][k], 16)

            def tile_done(o):
                if o.q == QT - 1 and not (isinstance(o.pair, int) and o.pair + 2 >= NPAIR) and not o.last:
                    sp.wait_ge(o_ready, o.n + 1)
                    load_pair(o.pair + 2, o.buf)
                if o.s == 1 and o.half == 1:
                    sp.wait_ge(ost_ready, o.duo + 1)
                    sp.dma_start(oT[o.pair][:, :, (o.q - 1) * P - HALF:(o.q + 1) * P - HALF],
                                 ost[:, o.duo_slot].bitcast(F32)).then_inc(o_out[o.duo_slot], 16)

            def body(i, last=False):
                for at in range(BODY):
                    o = Tile(i, at)
                    o.last = last
                    tile_done(o)
            body(0)
            with sp.Fori(1, LAST) as i:
                body(i)
            body(LAST, True)
            for s in range(2):
                sp.wait_ge(o_out[s], 16 * NPAIR)

        @block.tensor
        def _(pe):
            pe.wait_ge(ident_in, 16)

            def scores(new, e):
                if new.q == 0 and e == 0:
                    wait(pe, pair_in[new.buf], 16 * 13 * (new.fill + 1))
                wait(pe, exp_done, 2 * (new.n - 1) + e + 1)
                for lo, hi in zip(CUTS, CUTS[1:]):
                    for part in range(2):
                        last = pe.matmul(s_ps[e][:, lo:hi], q[new.buf][:, e, new.q * P:(new.q + 1) * P],
                                         kd[new.buf][:, e, part, lo:hi], start=part == 0, stop=part == 1)
                last.then_inc(s_ready, 1)

            def transposes(tr, ch):
                k0, k1 = CHUNKS[ch]
                wait(pe, wT_ready, 3 * tr.n + ch)
                for kt in range(k0, k1):
                    last = pe.transpose(t_ps[:, (kt - k0) * P:(kt - k0 + 1) * P],
                                        w[:, tr.s, kt * P:(kt + 1) * P], ident[:])
                last.then_inc(t_ready, 1)

            def step(tile):
                new, tr, pv, ot = tile(2), tile(0), tile(-1), tile(-4)
                if tr.exists:
                    wait(pe, w_ready, tr.n + 1)
                    wait(pe, of_ready, tr.n - 4)
                    transposes(tr, 0)
                if new.exists:
                    scores(new, 0)
                if tr.exists:
                    transposes(tr, 1)
                if pv.exists:
                    wait(pe, wT_ready, 3 * pv.n + 3)
                    wait(pe, o_copied, pv.n)
                    for kt in range(KEYS):
                        last = pe.matmul(o_ps[:, 0:P], wT[:, pv.s, kt], v[:, pv.buf, kt],
                                         start=kt == 0, stop=kt == KEYS - 1)
                    last.then_inc(o_ready, 1)
                if ot.exists:
                    wait(pe, on_ready, ot.n + 1)
                    wait(pe, wT_ready, 3 * tr.n + 2 if tr.exists else 3 * NT)
                    wait(pe, of_ready, ot.n)
                    pe.transpose(t_ps[:, 3 * P:4 * P], on[:, ot.s], ident[:]).then_inc(oT_ready, 1)
                if tr.exists:
                    transposes(tr, 2)
                if new.exists:
                    scores(new, 1)

            steps_of(pe, step)

        @block.scalar
        def _(act):
            def copy_wT(tr, ch):
                k0, k1 = CHUNKS[ch]
                wait(act, t_ready, 3 * tr.n + ch + 1)
                act.activation(wT[:, tr.s, k0:k1], t_ps[:, 0:(k1 - k0) * P], ACT.Copy).then_inc(wT_ready, 1)

            def exponentials(new, e):
                wait(act, max_ready, 2 * new.n + e + 1)
                wait(act, w_ready, new.n - 1)
                act.activation(prob[:, new.s, e], s_ps[e][:, 0:TA], ACT.Exp, bias=negmax[:, new.s, e:e + 1],
                               accum_out=sums[:, new.s, e:e + 1]).then_inc(exp_done, 1)

            def step(tile):
                new, nx, tr, done, ot = tile(2), tile(1), tile(0), tile(-2), tile(-4)
                if tr.exists:
                    wait(act, o_ready, tr.n - 1)
                    copy_wT(tr, 0)
                if done.exists:
                    wait(act, o_ready, done.n + 1)
                    wait(act, on_ready, done.n - 3)
                    wait(act, rsum_ready, done.n + 1)
                    act.activation(osb[:, done.s4], o_ps[:, 0:P], ACT.Copy,
                                   scale=rsum[:, done.s4, 0:1]).then_inc(o_copied, 1)
                if nx.exists:
                    exponentials(nx, 1)
                if tr.exists:
                    copy_wT(tr, 1)
                if new.exists:
                    exponentials(new, 0)
                if tr.exists:
                    copy_wT(tr, 2)
                if ot.exists:
                    wait(act, oT_ready, ot.n + 1)
                    wait(act, ost_ready, ot.duo - 1)
                    act.activation(of[:, ot.duo_slot, ot.s * P:(ot.s + 1) * P], t_ps[:, 3 * P:4 * P], ACT.Copy,
                                   scale=c["gsub"][:]).then_inc(of_ready, 1)

            steps_of(act, step)

        @block.vector
        def _(dve):
            dve.memset(half[:], -0.5).then_inc(half_set, 1)

            def maximum(new, e):
                wait(dve, s_ready, 2 * new.n + e + 1)
                dve.tensor_reduce(negmax[:, new.s, e:e + 1], s_ps[e][:, 0:TA], AX.X,
                                  ALU.max, negate=True).then_inc(max_ready, 1)

            def step(tile):
                new, nx, sq_t, ot = tile(2), tile(1), tile(-2), tile(-5)
                if nx.exists:
                    maximum(nx, 1)
                if new.exists:
                    maximum(new, 0)
                if nx.exists:
                    wait(dve, exp_done, 2 * nx.n + 2)
                    wait(dve, o_copied, nx.n - 3)
                    dve.reciprocal(rsum[:, nx.s4], sums[:, nx.s]).then_inc(rsum_ready, 1)
                    wait(dve, rsum_ready, nx.n + 1)
                    wait(dve, w_ready, nx.n - 1)
                    dve.tensor_scalar(coef[:, nx.s:nx.s + 1], sums[:, nx.s, 0:1], rsum[:, nx.s4, 1:2], c["neglam"][:],
                                      ALU.mult, ALU.mult).then_inc(coef_ready, 1)
                if nx.exists:
                    wait(dve, coef_ready, nx.n + 1)
                    wait(dve, t_ready, 3 * (nx.n - 2) + 3)
                    dve.scalar_tensor_tensor(out=w[:, nx.s], in0=prob[:, nx.s, 1], scalar=coef[:, nx.s:nx.s + 1],
                                             in1=prob[:, nx.s, 0], op0=ALU.mult, op1=ALU.add).then_inc(w_ready, 1)
                if sq_t.exists:
                    wait(dve, o_copied, sq_t.n + 1)
                    wait(dve, rstd_ready, sq_t.n - 1)
                    wait(dve, ss_ready, sq_t.n)
                    o = osb[:, sq_t.s4]
                    dve.tensor_tensor_reduce(junk[:], o, o, 1.0, 0.0, ALU.mult, ALU.add,
                                             ss[:, sq_t.s:sq_t.s + 1]).then_inc(ss_ready, 1)
                if ot.exists and ot.s == 1:
                    full = of[:, ot.duo_slot]
                    wait(dve, of_ready, ot.n + 1)
                    if ot.half:
                        hi, lo = ost[:, ot.duo_slot, 0], ost[:, ot.duo_slot, 1]
                        wait(dve, o_out[ot.duo_slot], 16 * ot.pair)
                    else:
                        hi, lo = (c["o_a"][:, bass.ds(ot.pair, 1), p, (ot.q - 1) * P:(ot.q + 1) * P] for p in range(2))
                    dve.tensor_copy(hi, full).then_inc(hi_step, 1)
                    wait(dve, hi_step, ot.duo + 1)
                    dve.tensor_tensor(lo, full, hi.bitcast(F32), ALU.subtract).then_inc(ost_ready, 1)

            steps_of(dve, step)

        @block.gpsimd
        def _(pool):
            split_steps = Steps(pool, c["split_step"])
            pool.wait_ge(half_set, 1)

            def step(tile):
                nx, pv = tile(1), tile(-2)
                for k in range(NRING):
                    if isinstance(nx.n, int) and nx.n == 4 + 2 * k:
                        pool.wait_ge(c["raw_full"][k], 16)
                        split_weights(pool, c["split_turn"], split_steps, c["raw"], c["ws"], k, KT, c["split_ready"])
                if pv.exists:
                    wait(pool, ss_ready, pv.n + 1)
                    wait(pool, on_ready, pv.n - 1)
                    pool.sem_inc(turn, 1)
                    pool.tensor_scalar(ms[:, pv.s:pv.s + 1], ss[:, pv.s:pv.s + 1], 1.0 / P, EPS,
                                       ALU.mult, ALU.add).then_inc(pool_step, 1)
                    wait(pool, pool_step, pv.n + 1)
                    pool.tensor_tensor(rstd[:, pv.s:pv.s + 1], ms[:, pv.s:pv.s + 1], half[:],
                                       ALU.pow).then_inc(rstd_ready, 1)
                    wait(pool, rstd_ready, pv.n + 1)
                    wait(pool, oT_ready, pv.n - 1)
                    pool.sem_inc(turn, 1)
                    pool.tensor_scalar(on[:, pv.s], osb[:, pv.s4], rstd[:, pv.s:pv.s + 1], 1.0,
                                       ALU.mult, ALU.mult).then_inc(on_ready, 1)

            steps_of(pool, step)


def block3(nc, a, c, at, oT, xS, out):
    with ExitStack() as ctx:
        def sb(name, shape, dt=F32):
            return ctx.enter_context(nc.sbuf_tensor(name, shape, dt))

        def sem(name):
            return ctx.enter_context(nc.semaphore(name))

        CH = HALF // P
        MIX_AT = 4

        ctx.enter_context(nc.sbuf_tensor("shared_region3", [P, REGION_KB * 256 + 8], F32))
        o = [c["o_a"], at("o_half_b", [P, KT, 2, HALF], 0, F32R)]
        hid = at("hid", [P, HT, 2, HALF], 0, F32R)
        y_o = at("y_second_o", [P, KT, HALF], 64)
        ws_v = at("wsplit_v3", [P, NRING, 2, KT, P], 0, F32R)
        u = at("u", [P, KT, HALF], 32)
        v = at("v", [P, CH, D], 48)
        rows = at("rows", [P, 3, D], 64)
        bsp = at("bsp", [P, KT, P], 76)
        wsp = at("wsp", [P, KT, P], 80)

        h = sb("h", [P, 2, KT, HALF], F32R)
        ws, raw = c["ws"], c["raw"]
        y = sb("y", [P, KT, HALF])
        sq = sb("sq3", [P, 2, HALF])
        sil = sb("silu3", [P, 2, HALF])
        t = sb("t3", [P, 2, HALF])
        acc = sb("acc3", [P, HALF])
        rstd = sb("rstd3", [P, HALF])
        xr = sb("x_ring", [P, 2, HALF])
        st6 = sb("bn6", [P, CH, 2, 6])
        mv = sb("mv", [P, CH, 2])
        rln = sb("rln", [P, CH])
        bank = [ctx.enter_context(nc.psum_tensor(f"acc3_{b}", [P, HALF], F32)) for b in range(4)]
        mix_bank = [ctx.enter_context(nc.psum_tensor(f"mixed{b}", [P, HALF], F32)) for b in range(2)]
        pstat = ctx.enter_context(nc.psum_tensor("stat3", [P, HALF], F32))

        o_in, rows_in = sem("o_in"), sem("rows_in")
        raw_full, split_ready = c["raw_full"], c["split_ready"]
        unit_done = sem("unit_done")
        mix_ready, mix_free = sem("mix_ready"), sem("mix_free")
        bank_free = [sem(f"b3_bank_free{b}") for b in range(4)]
        silu_ready, hid_ready = sem("silu_ready3"), sem("hid_ready")
        sq_ready, sq_used = sem("b3_sq_ready"), sem("b3_sq_used")
        stat_ready, std_ready = sem("b3_stat_ready"), sem("b3_std_ready")
        x_in = [sem(f"b3_x_in{s}") for s in range(2)]
        x_new, x_out = sem("x_new"), sem("x_out")
        t_ready, hf_ready, h_ready = sem("b3_t_ready"), sem("b3_hf_ready"), sem("b3_h_ready")
        v_ready, var_std, ln_ready = sem("v_ready"), sem("var_std"), sem("ln_ready")
        var_ready = sem("var_ready")
        dve_step, pool_step, turn = sem("b3_dve_step"), c["split_step"], c["split_turn"]

        stages = []
        U = G = H = S = 0
        for kind, layer in (("O", 0), ("F", 0), ("C", 1), ("F", 1)):
            for half in range(2):
                units = {"O": (0, KT), "F": (2 * HT, 3 * KT), "C": (2 * KT, KT)}[kind]
                groups = {"O": (0, KT), "F": (2 * HT, KT), "C": (2 * KT, KT)}[kind]
                s = dict(kind=kind, layer=layer, half=half, j=len(stages), U=U, G=G, H=H, S=S,
                         vec=2 * layer + (kind == "F"),
                         U_out=U + units[0], G_out=G + groups[0],
                         last_layer=kind == "F" and layer == 1)
                U, G = U + sum(units), G + sum(groups)
                H += {"O": 0, "F": HT, "C": KT}[kind]
                S += HT if kind == "F" else 0
                s.update(U_end=U, H_end=H)
                s["final"] = s["last_layer"] and half == 1
                stages.append(s)
        n_norm = {}
        for s in stages:
            n_norm["post", s["j"]] = len(n_norm)
            if not s["last_layer"]:
                n_norm["pre", s["j"]] = len(n_norm)

        def prev(s):
            return stages[s["j"] - 1] if s["j"] else None

        def y_of(s):
            return y_o if s["kind"] == "O" and s["half"] else y

        def y_done(s, i4, f):
            per = 3 if s["kind"] == "F" else 1
            return s["U_out"] + per * (4 * i4 + f + 1)

        block = ctx.enter_context(nc.Block())

        @block.sync
        def _(sp):
            for k in range(KT):
                sp.dma_start(o[1][:, k].bitcast(F32), oT[k]).then_inc(o_in, 16)

            def load(u, slot, n_kt, src):
                wait(sp, split_ready, u - NRING + 1)
                sp.dma_start(raw[:, slot, 0:n_kt], src).then_inc(raw_full[slot], 16)

            def plain(name, u0, n):
                def body(i):
                    for k in range(4):
                        load(u0 + 4 * i + k, k, KT, a[name][4 * i + k].rearrange("p (k c) -> p k c", k=KT))
                loop(sp, n, body)

            for s in stages:
                if s["kind"] == "O":
                    for n in range(0 if s["half"] else NRING, KT):
                        load(s["U"] + n, n % NRING, KT, a["w_attn_out"][n].rearrange("p (k c) -> p k c", k=KT))
                elif s["kind"] == "C":
                    plain("w_uv", s["U"], 4)
                    plain("w_cmlp_out", s["U_out"], 2)
                else:
                    plain(f"w_ffn_in{s['layer']}", s["U"], HT // 2)

                    def body(i):
                        for f in range(4):
                            w = a[f"w_ffn_out{s['layer']}"][4 * i + f].rearrange("p (k c) -> p k c", k=HT)
                            for m, (k0, k1) in enumerate(GROUPS_KT):
                                n = 3 * f + m
                                load(s["U_out"] + 12 * i + n, n % NRING, k1 - k0, w[:, k0:k1])
                    loop(sp, 2, body)

        @block.gpsimd
        def _(pool):
            steps = Steps(pool, pool_step)
            steps.n = NRING

            def unit(u0, i4, k, n_kt, done=None, into=ws):
                pool.wait_ge(raw_full[k % NRING], 16 * (u0 // NRING + i4 + k // NRING + 1))
                wait(pool, unit_done, u0 + 4 * i4 + k - NRING + 1 if done is None else done)
                split_weights(pool, turn, steps, raw, into, k % NRING, n_kt, split_ready)

            for s in stages:
                if s["kind"] == "O":
                    for n in range(0 if s["half"] else NRING, KT):
                        unit(s["U"], n // NRING, n % NRING, KT)
                elif s["kind"] == "C":
                    for k in range(4):
                        unit(s["U"], 0, k, KT)
                    for k in range(4):
                        unit(s["U"], 1, k, KT, prev(s)["U_end"], ws_v)
                    for k in range(4):
                        unit(s["U"], 2, k, KT, s["U"] + 4)
                    steps.loop(3, 4, lambda i: [unit(s["U"] + 12, i, k, KT) for k in range(4)])
                else:
                    steps.loop(HT // 2, 4, lambda i: [unit(s["U"], i, k, KT) for k in range(4)])
                    steps.loop(2, 12, lambda i: [unit(s["U_out"], 3 * i, 3 * f + m, k1 - k0)
                                                 for f in range(4) for m, (k0, k1) in enumerate(GROUPS_KT)])

        @block.tensor
        def _(pe):
            def bank_wait(g0, i4, at):
                wait(pe, bank_free[at % 4], g0 // 4 + i4 + at // 4)

            def stat(which, s):
                if s is None or (which, s["j"]) not in n_norm:
                    return
                n = n_norm[which, s["j"]]
                pe.wait_ge(sq_used, KT * (n + 1))
                wait(pe, std_ready, n)
                pe.matmul(pstat[:], c["ones"][:], acc[:], start=True, stop=True).then_inc(stat_ready, 1)

            def one(u0, g0, i, k, x):
                wait(pe, split_ready, u0 + 4 * i + k + 1)
                bank_wait(g0, i, k)
                product(pe, bank[k][:], KT, W(lambda p, kt: ws[:, k, p, kt]), x).then_inc(unit_done, 1)

            def mix(s, g):
                pe.wait_ge(ln_ready, CH * (s["half"] + 1))
                M = KT * s["half"] + g
                wait(pe, mix_free, M - 1)
                for n in range(CH):
                    last = pe.matmul(mix_bank[g % 2][:, n * P:(n + 1) * P], v[:, n, g * P:(g + 1) * P],
                                     wsp[:, g], start=True, stop=True)
                last.then_inc(mix_ready, 1)

            for s in stages:
                if s["kind"] == "O":
                    if s["half"]:
                        pe.wait_ge(o_in, 16 * KT)
                    for n in range(KT):
                        one(s["U"], s["G"], n // 4, n % 4, lambda p, kt: o[s["half"]][:, kt, p])
                        if n == 0:
                            stat("post", prev(s))
                        if n == 4:
                            stat("pre", prev(s))
                    continue

                pe.wait_ge(h_ready, KT * (s["j"] - 1))
                if s["kind"] == "F":
                    def hidden_tile(i, m):
                        for k in (2 * m, 2 * m + 1):
                            one(s["U"], s["G"], i, k, lambda p, kt: h[:, p, kt])
                    for i in range(4):
                        for m in range(2):
                            hidden_tile(i, m)
                            if (i, m) == (0, 0):
                                stat("post", prev(s))
                            if (i, m) == (3, 0):
                                stat("pre", prev(s))
                    with pe.Fori(4, HT // 2) as i:
                        for m in range(2):
                            hidden_tile(i, m)

                    def body(i):
                        for f in range(4):
                            bank_wait(s["G_out"], i, f)
                            for m, (k0, k1) in enumerate(GROUPS_KT):
                                n = 3 * f + m
                                wait(pe, split_ready, s["U_out"] + 12 * i + n + 1)
                                pe.wait_ge(hid_ready, s["H"] + k1)
                                product(pe, bank[f][:], k1 - k0,
                                        W(lambda p, kt: ws[:, n % NRING, p, kt], m == 0, m == 2),
                                        lambda p, kt: hid[:, k0 + kt, p]).then_inc(unit_done, 1)
                    loop(pe, 2, body)
                else:
                    for half in range(2):
                        pe.wait_ge(split_ready, s["U"] + 4 * half + 4)
                        wv = ws_v if half else ws
                        for n in range(CH):
                            bank_wait(s["G"], half, n)
                            product(pe, bank[n][:], KT, W(lambda p, kt: h[:, p, kt, n * P:(n + 1) * P]),
                                    lambda p, kt: wv[:, 0:4, p, kt]).then_inc(unit_done, 1)
                            if (half, n) == (0, 1):
                                stat("post", prev(s))
                    for g in range(KT):
                        one(s["U"] + KT, s["G"] + KT, g // 4, g % 4, lambda p, kt: h[:, p, kt])
                        if g == 0:
                            stat("pre", prev(s))
                        for m in range(2 * (g - MIX_AT), 2 * (g - MIX_AT) + 2):
                            if m >= 0:
                                mix(s, m)
                    wait(pe, split_ready, s["U_out"] + 1)
                    bank_wait(s["G_out"], 0, 0)
                    for kt in range(KT):
                        pe.wait_ge(hid_ready, s["H"] + kt + 1)
                        last = product(pe, bank[0][:], 1, W(lambda p, _: ws[:, 0, p, kt], kt == 0, kt == KT - 1),
                                       lambda p, _: hid[:, kt, p])
                    last.then_inc(unit_done, 1)
                    for n in range(1, KT):
                        one(s["U_out"], s["G_out"], n // 4, n % 4, lambda p, kt: hid[:, kt, p])
            stat("post", stages[-1])

        @block.scalar
        def _(act):
            def square(n, ft):
                wait(act, sq_used, KT * n + ft - 1)
                act.activation(sq[:, ft % 2], y[:, ft], ACT.Square).then_inc(sq_ready, 1)

            def load_x(s, ft):
                j = s["j"]
                if j >= 2 and ft == 0:
                    act.wait_ge(x_out, 16 * (j - 1))
                wait(act, x_new, KT * j + ft - 1)
                src = a["xT"] if s["kind"] == "O" else xS
                act.dma_start(xr[:, ft % 2], src[ft][:, s["half"] * HALF:(s["half"] + 1) * HALF]
                              ).then_inc(x_in[ft % 2], 16)

            def std(which, s):
                n = n_norm[which, s["j"]]
                act.wait_ge(stat_ready, n + 1)
                if which == "post":
                    wait(act, t_ready, KT * min(s["j"], len(stages) - 2))
                else:
                    act.wait_ge(x_new, KT * (s["j"] + 1))
                act.activation(rstd[:], pstat[:], ACT.Sqrt, bias=c["eps"][:]).then_inc(std_ready, 1)

            def post(s, between=()):
                std("post", s)
                for ft in range(KT):
                    act.wait_ge(x_new, KT * s["j"] + ft + 1)
                    if ft + 2 < KT:
                        load_x(s, ft + 2)
                    if not s["last_layer"]:
                        square(n_norm["pre", s["j"]], ft)
                    if s["final"]:
                        act.dma_start(out[ft][:, HALF:T], y[:, ft]).then_inc(x_out, 16)
                    if ft in between:
                        between[ft]()
                if s["final"]:
                    return
                cols = slice(s["half"] * HALF, (s["half"] + 1) * HALF)
                dst = out if s["last_layer"] else xS
                act.dma_start(dst[:, :, cols].rearrange("k p t -> p k t"), y[:]).then_inc(x_out, 16)

            def make_h(s):
                m = s["vec"] + 1
                shift0 = (m // 2) * 6 * KT + (SH_F if m % 2 else SH_M) * KT
                for ft in range(KT):
                    act.wait_ge(t_ready, KT * s["j"] + ft + 1)
                    act.activation(t[:, ft % 2], t[:, ft % 2], ACT.Identity,
                                   bias=c["mod"][:, shift0 + ft:shift0 + ft + 1],
                                   scale=c["A"][:, m, ft:ft + 1]).then_inc(hf_ready, 1)

            for s in stages:
                p = prev(s)
                if p:
                    load_x(p, 0)
                    load_x(p, 1)
                if s["kind"] == "O":
                    if p:
                        post(p)
                        std("pre", p)
                        make_h(p)
                elif s["kind"] == "F":
                    def silu(i, m):
                        wait(act, unit_done, s["U"] + 4 * i + 2 * m + 1)
                        wait(act, bank_free[2 * m + 1], s["G"] // 4 + i)
                        act.activation(sil[:, m], bank[2 * m][:], ACT.Silu).then_inc(silu_ready, 1)
                    silu(0, 0)
                    post(p, {3: lambda: silu(0, 1)})
                    for i, m in ((1, 0), (1, 1), (2, 0), (2, 1)):
                        silu(i, m)
                    if not p["last_layer"]:
                        std("pre", p)
                    with act.Fori(3, HT // 2) as i:
                        for m in range(2):
                            silu(i, m)
                    if not p["last_layer"]:
                        make_h(p)
                else:
                    if s["half"] == 0:
                        act.wait_ge(unit_done, p["U_end"])
                        act.dma_start(rows[:], a["rows"]).then_inc(rows_in, 16)
                        act.dma_start(bsp[:], a["b_spatial"]).then_inc(rows_in, 16)
                        act.dma_start(wsp[:], a["w_spatialT"]).then_inc(rows_in, 16)

                    def gelu_v(half, n):
                        act.wait_ge(bank_free[n], s["G"] // 4 + half + 1)
                        x = v[:, n, half * HALF:(half + 1) * HALF]
                        act.activation(x, x, ACT.Gelu).then_inc(v_ready, 1)
                    gelu_v(0, 0)
                    gelu_v(0, 1)
                    post(p, {3: lambda: gelu_v(0, 2), 6: lambda: gelu_v(0, 3)})
                    for n in range(CH):
                        gelu_v(1, n)
                    std("pre", p)
                    for ft in range(KT):
                        if ft == 2:
                            act.wait_ge(var_ready, s["half"] + 1)
                            act.activation(rln[:], mv[:, :, 1], ACT.Sqrt, bias=c["eps"][:]).then_inc(var_std, 1)
                        act.wait_ge(unit_done, s["U"] + KT + ft + 1)
                        act.activation(u[:, ft], bank[ft % 4][:], ACT.Gelu,
                                       bias=c["vecs"][:, V_BU + ft:V_BU + ft + 1]).then_inc(bank_free[ft % 4], 1)
                    make_h(p)

                def squares(i):
                    for f in range(4):
                        wait(act, bank_free[f], s["G_out"] // 4 + i + 1)
                        n = n_norm["post", s["j"]]
                        wait(act, sq_used, KT * n + 4 * i + f - 1)
                        act.activation(sq[:, f % 2], y_of(s)[:, 4 * i + f], ACT.Square).then_inc(sq_ready, 1)
                for i in range(2):
                    squares(i)
            s = stages[-1]
            load_x(s, 0)
            load_x(s, 1)
            post(s)
            act.wait_ge(x_out, 16 * (len(stages) - 1 + KT))

        @block.vector
        def _(dve):
            steps = Steps(dve, dve_step)

            def add_square(n, ft):
                dve.wait_ge(sq_ready, KT * n + ft + 1)
                wait(dve, sq_used, KT * n + ft)
                dve.tensor_tensor(acc[:], acc[:], sq[:, ft % 2], ALU.add).then_inc(sq_used, 1)

            def clear_acc(n):
                wait(dve, stat_ready, n)
                steps.did(dve.memset(acc[:], 0.0))
                steps.sync()

            def inverse(which, s):
                dve.wait_ge(std_ready, n_norm[which, s["j"]] + 1)
                steps.did(dve.reciprocal(rstd[:], rstd[:]))
                steps.sync()

            def post(s, between=()):
                inverse("post", s)
                n = n_norm.get(("pre", s["j"]))
                if n is not None:
                    clear_acc(n)
                if y_of(s) is not y:
                    dve.wait_ge(x_out, 16 * s["j"])
                    dve.wait_ge(h_ready, KT * s["j"])
                for ft in range(KT):
                    steps.did(dve.tensor_tensor(y_of(s)[:, ft], y_of(s)[:, ft], rstd[:], ALU.mult))
                    steps.sync()
                    dve.wait_ge(x_in[ft % 2], 16 * (KT // 2 * s["j"] + ft // 2 + 1))
                    dve.scalar_tensor_tensor(out=y[:, ft], in0=y_of(s)[:, ft], scalar=c["G"][:, s["vec"], ft:ft + 1],
                                             in1=xr[:, ft % 2], op0=ALU.mult, op1=ALU.add).then_inc(x_new, 1)
                    if n is not None and ft:
                        add_square(n, ft - 1)
                    if ft in between:
                        between[ft]()
                if n is not None:
                    add_square(n, KT - 1)

            def make_h(s, h_free, between=()):
                wait(dve, unit_done, h_free)
                wait(dve, hid_ready, s["H_end"])

                def scaled(ft):
                    wait(dve, h_ready, KT * s["j"] + ft - 1)
                    dve.tensor_tensor(t[:, ft % 2], y[:, ft], rstd[:], ALU.mult).then_inc(t_ready, 1)
                scaled(0)
                for ft in range(KT):
                    if ft + 1 < KT:
                        scaled(ft + 1)
                    dve.wait_ge(hf_ready, KT * s["j"] + ft + 1)
                    steps.did(dve.tensor_copy(h[:, 0, ft], t[:, ft % 2]))
                    steps.sync()
                    dve.tensor_tensor(h[:, 1, ft], t[:, ft % 2], h[:, 0, ft].bitcast(F32),
                                      ALU.subtract).then_inc(h_ready, 1)
                    if ft in between:
                        between[ft]()

            for s in stages:
                p = prev(s)
                def take(ft):
                    dve.wait_ge(unit_done, y_done(s, ft // 4, ft % 4))
                    dve.tensor_copy(y_of(s)[:, ft], bank[ft % 4][:]).then_inc(bank_free[ft % 4], 1)

                if s["kind"] == "O":
                    if p:
                        post(p, {3: lambda: take(0), 5: lambda: take(1), 7: lambda: take(2)})
                        inverse("pre", p)
                        make_h(p, 0, {n - 3: lambda n=n: take(n) for n in range(3, KT)})
                elif s["kind"] == "F":
                    dve.wait_ge(unit_done, p["U_end"])

                    def hidden_tile(i, m):
                        full, up = t[:, m], 2 * m + 1
                        dve.wait_ge(silu_ready, s["S"] + 2 * i + m + 1)
                        dve.wait_ge(unit_done, s["U"] + 4 * i + 2 * m + 2)
                        wait(dve, hid_ready, s["H"] + 2 * i + m - 1)
                        dve.tensor_tensor(full, sil[:, m], bank[up][:], ALU.mult).then_inc(bank_free[up], 1)
                        dve.wait_ge(bank_free[up], s["G"] // 4 + i + 1)
                        hi = hid[:, bass.ds(2 * i + m, 1), 0]
                        lo = hid[:, bass.ds(2 * i + m, 1), 1]
                        dve.tensor_copy(hi, full).then_inc(bank_free[2 * m], 1)
                        dve.wait_ge(bank_free[2 * m], s["G"] // 4 + i + 1)
                        dve.tensor_tensor(lo, full, hi.bitcast(F32), ALU.subtract).then_inc(hid_ready, 1)
                    hidden_tile(0, 0)
                    post(p, {3: lambda: hidden_tile(0, 1)})
                    for i, m in ((1, 0), (1, 1), (2, 0), (2, 1)):
                        hidden_tile(i, m)
                    if not p["last_layer"]:
                        inverse("pre", p)
                    with dve.Fori(3, HT // 2) as i:
                        for m in range(2):
                            hidden_tile(i, m)
                    if not p["last_layer"]:
                        dve.wait_ge(hid_ready, s["H_end"])
                        make_h(p, s["U_out"])
                else:
                    dve.wait_ge(unit_done, p["U_end"])
                    dve.wait_ge(rows_in, 48)

                    def add_bias(half, n):
                        dve.wait_ge(unit_done, s["U"] + 4 * half + n + 1)
                        cols = slice(half * HALF, (half + 1) * HALF)
                        dve.tensor_tensor(v[:, n, cols], bank[n][:], rows[:, 0, cols],
                                          ALU.add).then_inc(bank_free[n], 1)
                    add_bias(0, 0)
                    add_bias(0, 1)
                    post(p, {3: lambda: add_bias(0, 2), 6: lambda: add_bias(0, 3)})
                    for n in range(CH):
                        add_bias(1, n)
                    inverse("pre", p)
                    for n in range(CH):
                        dve.wait_ge(v_ready, 2 * CH * s["half"] + CH + n + 1)
                        for half in range(2):
                            steps.did(dve.bn_stats(st6[:, n, half], v[:, n, half * HALF:(half + 1) * HALF]))
                        steps.sync()
                        if n < CH - 1:
                            steps.did(dve.bn_aggr(mv[:, n], st6[:, n]))
                        else:
                            dve.bn_aggr(mv[:, n], st6[:, n]).then_inc(var_ready, 1)
                    dve.wait_ge(var_std, s["half"] + 1)
                    steps.did(dve.reciprocal(rln[:], rln[:]))
                    steps.sync()
                    for n in range(CH):
                        steps.did(dve.tensor_scalar(v[:, n], v[:, n], mv[:, n, 0:1], rln[:, n:n + 1],
                                                    ALU.subtract, ALU.mult))
                        steps.sync()
                        steps.did(dve.tensor_tensor(v[:, n], v[:, n], rows[:, 1], ALU.mult))
                        steps.sync()
                        dve.tensor_tensor(v[:, n], v[:, n], rows[:, 2], ALU.add).then_inc(ln_ready, 1)
                    for g in range(KT):
                        dve.wait_ge(mix_ready, KT * s["half"] + g + 1)
                        wait(dve, hid_ready, s["H"] + g)
                        full = t[:, g % 2].rearrange("p (n q) -> p n q", n=CH)
                        dve.tensor_tensor(full, mix_bank[g % 2][:].rearrange("p (n q) -> p n q", n=CH),
                                          bsp[:, g:g + 1].to_broadcast([P, CH, P]),
                                          ALU.add).then_inc(mix_free, 1)
                        dve.wait_ge(mix_free, KT * s["half"] + g + 1)
                        dve.wait_ge(bank_free[g % 4], (s["G"] + KT + g) // 4 + 1)
                        steps.did(dve.tensor_tensor(t[:, g % 2], t[:, g % 2], u[:, g], ALU.mult))
                        steps.sync()
                        steps.did(dve.tensor_copy(hid[:, g, 0], t[:, g % 2]))
                        steps.sync()
                        dve.tensor_tensor(hid[:, g, 1], t[:, g % 2], hid[:, g, 0].bitcast(F32),
                                          ALU.subtract).then_inc(hid_ready, 1)
                    dve.wait_ge(hid_ready, s["H_end"])
                    make_h(p, s["U_out"])

                n = n_norm["post", s["j"]]
                taken = y_of(s) is not y
                if p and not taken:
                    dve.wait_ge(x_out, 16 * s["j"])
                    wait(dve, h_ready, KT * min(s["j"], len(stages) - 2))
                clear_acc(n)
                for ft in range(KT):
                    if not taken:
                        take(ft)
                    if ft:
                        add_square(n, ft - 1)
                add_square(n, KT - 1)
            post(stages[-1])


def launch_tables():
    axis = DH // 2
    inv = np.float32(10000.0) ** (-np.arange(0, axis, 2, dtype=np.float32) / np.float32(axis))
    row = np.repeat(np.arange(T // 64, dtype=np.float32), 64)
    col = np.tile(np.arange(64, dtype=np.float32), T // 64)
    cos, sin = np.zeros((P, T), np.float32), np.zeros((P, T), np.float32)
    for p in range(P):
        pos = row if p % DH < axis else col
        f = p % axis
        ang = (pos * inv[f % (axis // 2)]).astype(np.float32)
        cos[p] = np.cos(ang)
        sin[p] = np.sin(ang) if f >= axis // 2 else -np.sin(ang)
    return np.ascontiguousarray(np.stack([cos, sin], 1))


def kernel(x, c, ctx, c_ctx, w_ada, b_ada, g_mix_pre, g_mix_post, g_ffn_pre, g_ffn_post, w_qkv, w_attn_out,
           lam_q1, lam_k1, lam_q2, lam_k2, g_subln, w_uv, b_uv, g_sgu, b_sgu, w_spatial, b_spatial,
           w_cmlp_out, w_ffn_in, w_ffn_out):
    import concourse.bacc as bacc
    from concourse.bass_utils import run_bass_kernel_spmd

    def arr(v):
        return np.asarray(v)

    def tiles(w):
        w = arr(w)
        K, N = w.shape
        return np.ascontiguousarray(w.reshape(K // P, P, N // P, P).transpose(2, 1, 0, 3)).reshape(N // P, P, K)

    def cols(v):
        return arr(v).reshape(-1, P).T

    def row(v):
        return np.broadcast_to(arr(v).reshape(1, -1), (P, arr(v).size))

    ada = arr(w_ada).reshape(2, KT, P, 6, D).transpose(0, 3, 1, 2, 4).reshape(12, KT, P, D)
    vecs = np.concatenate([cols(b_ada), cols(g_mix_pre), cols(g_mix_post), cols(g_ffn_pre), cols(g_ffn_post),
                           cols(c), cols(c_ctx), cols(arr(b_uv)[0, :D]), cols(g_subln)], axis=1)
    uv = tiles(arr(w_uv)[0])
    arrays = {
        "xT": arr(x)[0].T.reshape(KT, P, T),
        "ctxT": arr(ctx)[0].T.reshape(KT, P, C),
        "vecs": vecs,
        "lamv": np.stack([row(lam_q1), row(lam_k1), row(lam_q2), row(lam_k2)], 1),
        "trig": launch_tables(),
        "ident": np.eye(P, dtype=np.float32),
        "w_ada": ada,
        "w_qkv": tiles(arr(w_qkv)[0]),
        "w_attn_out": tiles(arr(w_attn_out)[0]),
        "w_uv": np.concatenate([uv[KT:], uv[:KT]]),
        "w_cmlp_out": tiles(arr(w_cmlp_out)[0]),
        "rows": np.stack([row(arr(b_uv)[0, D:]), row(g_sgu), row(b_sgu)], 1),
        "b_spatial": np.broadcast_to(arr(b_spatial)[0][None], (P, KT, P)),
        "w_spatialT": arr(w_spatial)[0].transpose(2, 0, 1),
    }
    for i in range(2):
        w = tiles(arr(w_ffn_in)[i])
        arrays[f"w_ffn_in{i}"] = np.stack([w[:HT], w[HT:]], 1).reshape(2 * HT, P, D)
        arrays[f"w_ffn_out{i}"] = tiles(arr(w_ffn_out)[i])
    nc = bacc.Bacc("TRN2", target_bir_lowering=False, num_devices=1)
    feed, aps = {}, {}
    for name, v in arrays.items():
        feed[f"in_{name}"] = v = np.ascontiguousarray(v)
        aps[name] = nc.dram_tensor(f"in_{name}", list(v.shape), F32, kind="ExternalInput").ap()
    out = nc.dram_tensor("out_xT", [KT, P, T], F32, kind="ExternalOutput").ap()
    build(nc, aps, out)
    got = run_bass_kernel_spmd(nc, [feed], core_ids=[0]).results[0]["out_xT"]
    return np.ascontiguousarray(got.reshape(D, T).T).reshape(1, T, D)
```
